# Optimizing a Trainium2 kernel written in Bass

```python
import jax, jax.numpy as jnp
from jax import lax
import numpy as np

D_MODEL = 1024
BATCH = 1
SEQ = 256
DEPTH = 2

GRID_W = 64
CTX_LEN = 256
N_MIXERS = 4
ALPHA = (2 * DEPTH) ** 0.25
BETA = (8 * DEPTH) ** -0.25
LN_EPS = 1e-5
RMS_EPS = 1e-6
NEG_INF = -1e30
ROPE_THETA = 10000.0
Q_BLOCK = 128
F32 = jnp.float32

HGRN_HEADS = 8
HGRN_DK = D_MODEL // HGRN_HEADS
HGRN_DV = D_MODEL // HGRN_HEADS
GLA_CHUNK = 64

SWA_Q_HEADS = 16
SWA_KV_HEADS = 4
SWA_HEAD_DIM = D_MODEL // SWA_Q_HEADS
SWA_WINDOW = 128

NA_HEADS = 16
NA_HEAD_DIM = D_MODEL // NA_HEADS
NA_WIN_ROWS = 8
NA_WIN_COLS = 16

GQA_Q_HEADS = 8
GQA_KV_HEADS = 2
GQA_HEAD_DIM = D_MODEL // GQA_Q_HEADS

PEER_HEADS = 8
PEER_NKEYS = 128
PEER_N = PEER_NKEYS * PEER_NKEYS
PEER_DQ = 256
PEER_TOPK = 16
PEER_CHUNK = 128

kernel_name = 'hybrid_diffusion_hgrn2_swa_natten_gqa_peer'

def layer_norm(x, g, b):
    xf = x.astype(F32)
    mu = jnp.mean(xf, axis=-1, keepdims=True)
    var = jnp.mean(jnp.square(xf - mu), axis=-1, keepdims=True)
    return ((xf - mu) * lax.rsqrt(var + LN_EPS) * g + b).astype(x.dtype)

def rms_norm(x, g):
    xf = x.astype(F32)
    return (xf * lax.rsqrt(jnp.mean(jnp.square(xf), axis=-1, keepdims=True) + RMS_EPS) * g).astype(x.dtype)

def axial_rope(x):
    n_tok, dh = x.shape[1], x.shape[-1]
    t = jnp.arange(n_tok)
    pos = jnp.stack([t // GRID_W, t % GRID_W]).astype(F32)
    d_axis = dh // 2
    inv = ROPE_THETA ** (-jnp.arange(0, d_axis, 2, dtype=F32) / d_axis)
    ang = pos[:, :, None] * inv
    cos = jnp.cos(ang)[:, :, None, :].astype(x.dtype)
    sin = jnp.sin(ang)[:, :, None, :].astype(x.dtype)
    parts = []
    for a, xa in enumerate(jnp.split(x, 2, axis=-1)):
        x1, x2 = jnp.split(xa, 2, axis=-1)
        parts.append(jnp.concatenate([x1 * cos[a] - x2 * sin[a], x2 * cos[a] + x1 * sin[a]], axis=-1))
    return jnp.concatenate(parts, axis=-1)

def qkv_heads(h, w_in, hq, hkv, dh):
    z = h @ w_in
    bsz, n_tok, _ = z.shape
    q = z[..., :hq * dh].reshape(bsz, n_tok, hq, dh)
    k = z[..., hq * dh:(hq + hkv) * dh].reshape(bsz, n_tok, hkv, dh)
    v = z[..., (hq + hkv) * dh:].reshape(bsz, n_tok, hkv, dh)
    return q, k, v

def attend(q, k, v, bias=None, sink=None):
    bsz, lq, hq, dh = q.shape
    hkv = k.shape[2]
    grp = hq // hkv
    s = jnp.einsum('bqhgd,bkhd->bhgqk', q.reshape(bsz, lq, hkv, grp, dh), k).astype(F32) * (dh ** -0.5)
    if bias is not None:
        s = s + bias
    if sink is None:
        p = jax.nn.softmax(s, axis=-1)
    else:
        sk = jnp.broadcast_to(sink.astype(F32).reshape(1, hkv, grp, 1, 1), s.shape[:-1] + (1,))
        p = jax.nn.softmax(jnp.concatenate([s, sk], axis=-1), axis=-1)[..., :-1]
    o = jnp.einsum('bhgqk,bkhd->bqhgd', p.astype(v.dtype), v)
    return o.reshape(bsz, lq, hq, dh)

def unblock(o):
    nb, bsz, blk, h, dh = o.shape
    return o.transpose(1, 0, 2, 3, 4).reshape(bsz, nb * blk, h * dh)

def gla_chunkwise(q, k, v, logf, s0):
    bsz, h, n_tok, _ = q.shape
    n_chunks = n_tok // GLA_CHUNK
    tri = jnp.tril(jnp.ones((GLA_CHUNK, GLA_CHUNK), bool))

    def chunks(a):
        return a.reshape(bsz, h, n_chunks, GLA_CHUNK, a.shape[-1]).transpose(2, 0, 1, 3, 4)

    def step(state, inp):
        qb, kb, vb, gb = inp
        b = jnp.cumsum(gb, axis=2)
        rel = jnp.where(tri[:, :, None], b[:, :, :, None, :] - b[:, :, None, :, :], -jnp.inf)
        att = jnp.einsum('bhtk,bhsk,bhtsk->bhts', qb, kb, jnp.exp(rel))
        o = jnp.einsum('bhts,bhsv->bhtv', att, vb) + jnp.einsum('bhtk,bhkv->bhtv', qb * jnp.exp(b), state)
        b_end = b[:, :, -1:, :]
        state = jnp.exp(b_end[:, :, 0, :, None]) * state + jnp.einsum('bhsk,bhsv->bhkv', kb * jnp.exp(b_end - b), vb)
        return state, o

    state, o = lax.scan(step, s0, (chunks(q), chunks(k), chunks(v), chunks(logf)))
    return o.transpose(1, 2, 0, 3, 4).reshape(bsz, h, n_tok, -1), state

def hgrn2_mixer(hx, hc, w_in, lb, norm_g, w_out, with_ctx):
    def gates(h):
        bsz, n_tok, _ = h.shape
        q, i, f_fw, f_bw, g = jnp.split(h @ w_in, 5, axis=-1)
        heads = lambda a: a.reshape(bsz, n_tok, HGRN_HEADS, -1).transpose(0, 2, 1, 3).astype(F32)

        def decay(fz):
            f = lb + (1.0 - lb) * jax.nn.sigmoid(fz.astype(F32))
            return heads(1.0 - f), heads(jnp.log(f))
        return heads(jax.nn.silu(q)), heads(i), decay(f_fw), decay(f_bw), g

    def readout(o, g):
        bsz, _, n_tok, _ = o.shape
        o = rms_norm(o.transpose(0, 2, 1, 3), norm_g).reshape(bsz, n_tok, D_MODEL)
        return (o.astype(g.dtype) * jax.nn.silu(g)) @ w_out

    flip = lambda a: jnp.flip(a, axis=2)
    qc, vc, (kcf, lcf), (kcb, lcb), gc = gates(hc)
    s0 = jnp.zeros((hc.shape[0], HGRN_HEADS, HGRN_DK, HGRN_DV), F32)
    oc_f, sc_f = gla_chunkwise(qc, kcf, vc, lcf, s0)
    oc_b, sc_b = gla_chunkwise(flip(qc), flip(kcb), flip(vc), flip(lcb), s0)
    qx, vx, (kxf, lxf), (kxb, lxb), gx = gates(hx)
    ox_f, _ = gla_chunkwise(qx, kxf, vx, lxf, sc_f)
    ox_b, _ = gla_chunkwise(flip(qx), flip(kxb), flip(vx), flip(lxb), sc_b)
    yx = readout(ox_f + flip(ox_b), gx)
    yc = readout(oc_f + flip(oc_b), gc) if with_ctx else None
    return yx, yc

def swa_mixer(hx, hc, w_in, sink, w_out, with_ctx):
    bsz, s_len, _ = hx.shape
    qx, kx, vx = qkv_heads(hx, w_in, SWA_Q_HEADS, SWA_KV_HEADS, SWA_HEAD_DIM)
    qc, kc, vc = qkv_heads(hc, w_in, SWA_Q_HEADS, SWA_KV_HEADS, SWA_HEAD_DIM)
    qx, kx = axial_rope(qx), axial_rope(kx)
    pad = ((0, 0), (SWA_WINDOW, SWA_WINDOW), (0, 0), (0, 0))
    kp, vp = jnp.pad(kx, pad), jnp.pad(vx, pad)
    span = Q_BLOCK + 2 * SWA_WINDOW
    ctx_bias = jnp.zeros((Q_BLOCK, kc.shape[1]), F32)

    def block(n):
        start = n * Q_BLOCK
        q = lax.dynamic_slice_in_dim(qx, start, Q_BLOCK, axis=1)
        k = lax.dynamic_slice_in_dim(kp, start, span, axis=1)
        v = lax.dynamic_slice_in_dim(vp, start, span, axis=1)
        qpos = start + jnp.arange(Q_BLOCK)
        kpos = start - SWA_WINDOW + jnp.arange(span)
        ok = (jnp.abs(qpos[:, None] - kpos[None, :]) <= SWA_WINDOW) & (kpos[None, :] >= 0) & (kpos[None, :] < s_len)
        bias = jnp.concatenate([jnp.where(ok, 0.0, NEG_INF), ctx_bias], axis=-1)
        return attend(q, jnp.concatenate([k, kc], axis=1), jnp.concatenate([v, vc], axis=1), bias, sink)

    yx = unblock(lax.map(block, jnp.arange(s_len // Q_BLOCK))) @ w_out
    yc = attend(qc, kc, vc, sink=sink).reshape(bsz, hc.shape[1], D_MODEL) @ w_out if with_ctx else None
    return yx, yc

def na_mixer(hx, hc, w_in, rpb, w_out, with_ctx):
    bsz, s_len, _ = hx.shape
    rows = s_len // GRID_W
    wr = min(NA_WIN_ROWS, rows)
    qx, kx, vx = qkv_heads(hx, w_in, NA_HEADS, NA_HEADS, NA_HEAD_DIM)
    qc, kc, vc = qkv_heads(hc, w_in, NA_HEADS, NA_HEADS, NA_HEAD_DIM)
    col = jnp.arange(GRID_W)
    cstart = jnp.clip(col - NA_WIN_COLS // 2, 0, GRID_W - NA_WIN_COLS)
    col_ok = (col[None, :] >= cstart[:, None]) & (col[None, :] < cstart[:, None] + NA_WIN_COLS)
    dcol = jnp.clip(col[None, :] - col[:, None] + NA_WIN_COLS - 1, 0, 2 * NA_WIN_COLS - 2)
    ctx_bias = jnp.zeros((NA_HEADS, GRID_W, kc.shape[1]), F32)

    def row_block(r):
        rstart = jnp.clip(r - wr // 2, 0, rows - wr)
        q = lax.dynamic_slice_in_dim(qx, r * GRID_W, GRID_W, axis=1)
        k = lax.dynamic_slice_in_dim(kx, rstart * GRID_W, wr * GRID_W, axis=1)
        v = lax.dynamic_slice_in_dim(vx, rstart * GRID_W, wr * GRID_W, axis=1)
        drow = rstart + jnp.arange(wr) - r + NA_WIN_ROWS - 1
        rel = rpb[:, drow[None, :, None], dcol[:, None, :]].astype(F32)
        bias = jnp.where(col_ok[:, None, :], rel, NEG_INF).reshape(NA_HEADS, GRID_W, wr * GRID_W)
        bias = jnp.concatenate([bias, ctx_bias], axis=-1)[None, :, None]
        return attend(q, jnp.concatenate([k, kc], axis=1), jnp.concatenate([v, vc], axis=1), bias)

    yx = unblock(lax.map(row_block, jnp.arange(rows))) @ w_out
    yc = attend(qc, kc, vc).reshape(bsz, hc.shape[1], D_MODEL) @ w_out if with_ctx else None
    return yx, yc

def gqa_mixer(hx, hc, w_in, q_norm, k_norm, w_out, with_ctx):
    bsz, s_len, _ = hx.shape
    qx, kx, vx = qkv_heads(hx, w_in, GQA_Q_HEADS, GQA_KV_HEADS, GQA_HEAD_DIM)
    qc, kc, vc = qkv_heads(hc, w_in, GQA_Q_HEADS, GQA_KV_HEADS, GQA_HEAD_DIM)
    qx, kx = axial_rope(rms_norm(qx, q_norm)), axial_rope(rms_norm(kx, k_norm))
    qc, kc = rms_norm(qc, q_norm), rms_norm(kc, k_norm)
    k_all = jnp.concatenate([kx, kc], axis=1)
    v_all = jnp.concatenate([vx, vc], axis=1)

    def block(n):
        return attend(lax.dynamic_slice_in_dim(qx, n * Q_BLOCK, Q_BLOCK, axis=1), k_all, v_all)

    yx = unblock(lax.map(block, jnp.arange(s_len // Q_BLOCK))) @ w_out
    yc = attend(qc, kc, vc).reshape(bsz, hc.shape[1], D_MODEL) @ w_out if with_ctx else None
    return yx, yc

def peer_ffn(tokens, wq, sub_keys, u, v):
    n_tok, d = tokens.shape

    def chunk(h):
        t = h.shape[0]
        q = (h @ wq).reshape(t, PEER_HEADS, 2, PEER_DQ // 2)
        s = jnp.einsum('thpd,hpnd->thpn', q, sub_keys).astype(F32)
        sv, si = lax.top_k(s, PEER_TOPK)
        cand_s = (sv[:, :, 0, :, None] + sv[:, :, 1, None, :]).reshape(t, PEER_HEADS, -1)
        cand_i = (si[:, :, 0, :, None] * PEER_NKEYS + si[:, :, 1, None, :]).reshape(t, PEER_HEADS, -1)
        best_s, best = lax.top_k(cand_s, PEER_TOPK)
        idx = jnp.take_along_axis(cand_i, best, axis=-1)
        gate = jax.nn.softmax(best_s, axis=-1)
        act = jax.nn.gelu(jnp.einsum('td,thkd->thk', h, u[idx]).astype(F32))
        return jnp.einsum('thk,thkd->td', (gate * act).astype(v.dtype), v[idx])

    out = lax.map(chunk, tokens.reshape(n_tok // PEER_CHUNK, PEER_CHUNK, d))
    return out.reshape(n_tok, d)

def setup_inputs(seed: int = 0) -> dict:
    key = jax.random.key(seed)
    ks = iter(jax.random.split(key, 32))
    nrm = lambda shape, scale: jax.random.normal(next(ks), shape, F32) * scale
    occ = [len(range(m, DEPTH, N_MIXERS)) for m in range(N_MIXERS)]
    d = D_MODEL
    out_scale = d ** -0.5 * BETA
    return {
        'x': nrm((BATCH, SEQ, d), 1.0),
        'c': nrm((BATCH, d), 1.0),
        'ctx': nrm((BATCH, CTX_LEN, d), 1.0),
        'c_ctx': nrm((d,), 1.0),
        'mod_w': nrm((DEPTH, d, 6 * d), d ** -0.5),
        'mod_b': nrm((DEPTH, 6 * d), 0.02),
        'ln_g': 1.0 + nrm((DEPTH, 2, d), 0.02),
        'ln_b': nrm((DEPTH, 2, d), 0.02),
        'peer_wq': nrm((DEPTH, d, PEER_HEADS * PEER_DQ), d ** -0.5),
        'peer_keys': nrm((DEPTH, PEER_HEADS, 2, PEER_NKEYS, PEER_DQ // 2), (PEER_DQ // 2) ** -0.5),
        'peer_u': nrm((DEPTH, PEER_N, d), d ** -0.5),
        'peer_v': nrm((DEPTH, PEER_N, d), BETA),
        'hgrn_w_in': nrm((occ[0], d, 5 * d), d ** -0.5),
        'hgrn_lb_logits': nrm((DEPTH + 1, HGRN_HEADS * HGRN_DK), 0.1),
        'hgrn_norm_g': 1.0 + nrm((occ[0], HGRN_DV), 0.02),
        'hgrn_w_out': nrm((occ[0], d, d), out_scale),
        'swa_w_in': nrm((occ[1], d, (SWA_Q_HEADS + 2 * SWA_KV_HEADS) * SWA_HEAD_DIM), d ** -0.5),
        'swa_sink': nrm((occ[1], SWA_Q_HEADS), 0.1),
        'swa_w_out': nrm((occ[1], SWA_Q_HEADS * SWA_HEAD_DIM, d), out_scale),
        'na_w_in': nrm((occ[2], d, 3 * NA_HEADS * NA_HEAD_DIM), d ** -0.5),
        'na_rpb': nrm((occ[2], NA_HEADS, 2 * NA_WIN_ROWS - 1, 2 * NA_WIN_COLS - 1), 0.02),
        'na_w_out': nrm((occ[2], NA_HEADS * NA_HEAD_DIM, d), out_scale),
        'gqa_w_in': nrm((occ[3], d, (GQA_Q_HEADS + 2 * GQA_KV_HEADS) * GQA_HEAD_DIM), d ** -0.5),
        'gqa_q_norm': 1.0 + nrm((occ[3], GQA_HEAD_DIM), 0.02),
        'gqa_k_norm': 1.0 + nrm((occ[3], GQA_HEAD_DIM), 0.02),
        'gqa_w_out': nrm((occ[3], GQA_Q_HEADS * GQA_HEAD_DIM, d), out_scale),
    }

def reference(x, c, ctx, c_ctx, mod_w, mod_b, ln_g, ln_b, peer_wq, peer_keys, peer_u, peer_v,
              hgrn_w_in, hgrn_lb_logits, hgrn_norm_g, hgrn_w_out,
              swa_w_in, swa_sink, swa_w_out,
              na_w_in, na_rpb, na_w_out,
              gqa_w_in, gqa_q_norm, gqa_k_norm, gqa_w_out):
    lower_bounds = jnp.cumsum(jax.nn.softmax(hgrn_lb_logits.astype(F32), axis=0), axis=0)
    cond_x = jax.nn.silu(c)
    cond_c = jax.nn.silu(c_ctx)
    for i in range(DEPTH):
        kind, occ = i % N_MIXERS, i // N_MIXERS
        last = i == DEPTH - 1
        mx = jnp.split((cond_x @ mod_w[i] + mod_b[i])[:, None, :], 6, axis=-1)
        mc = jnp.split(cond_c @ mod_w[i] + mod_b[i], 6, axis=-1)
        hx = x * (1.0 + mx[1]) + mx[0]
        hc = ctx * (1.0 + mc[1]) + mc[0]
        if kind == 0:
            yx, yc = hgrn2_mixer(hx, hc, hgrn_w_in[occ], lower_bounds[i], hgrn_norm_g[occ], hgrn_w_out[occ], not last)
        elif kind == 1:
            yx, yc = swa_mixer(hx, hc, swa_w_in[occ], swa_sink[occ], swa_w_out[occ], not last)
        elif kind == 2:
            yx, yc = na_mixer(hx, hc, na_w_in[occ], na_rpb[occ], na_w_out[occ], not last)
        else:
            yx, yc = gqa_mixer(hx, hc, gqa_w_in[occ], gqa_q_norm[occ], gqa_k_norm[occ], gqa_w_out[occ], not last)
        x = layer_norm(ALPHA * x + mx[2] * yx, ln_g[i, 0], ln_b[i, 0])
        tokens = (x * (1.0 + mx[4]) + mx[3]).reshape(-1, D_MODEL)
        if not last:
            ctx = layer_norm(ALPHA * ctx + mc[2] * yc, ln_g[i, 0], ln_b[i, 0])
            tokens = jnp.concatenate([tokens, (ctx * (1.0 + mc[4]) + mc[3]).reshape(-1, D_MODEL)], axis=0)
        y = peer_ffn(tokens, peer_wq[i], peer_keys[i], peer_u[i], peer_v[i])
        n_lat = x.shape[0] * x.shape[1]
        x = layer_norm(ALPHA * x + mx[5] * y[:n_lat].reshape(x.shape), ln_g[i, 1], ln_b[i, 1])
        if not last:
            ctx = layer_norm(ALPHA * ctx + mc[5] * y[n_lat:].reshape(ctx.shape), ln_g[i, 1], ln_b[i, 1])
    return x


_drawn_inputs = setup_inputs


def setup_inputs(seed=0):
    import zlib

    import numpy as np

    out = dict(_drawn_inputs(seed))
    spreads = {}
    factors = {'hgrn_lb_logits': 7.898, 'hgrn_norm_g': 3.844, 'swa_sink': 64.0}
    for name, (base, spread) in spreads.items():
        noise = np.random.default_rng([zlib.crc32(name.encode()), seed]).standard_normal(out[name].shape)
        drawn = base * np.exp(spread * noise) if base else spread * noise
        out[name] = __import__('jax').numpy.asarray(drawn.astype(out[name].dtype))
    for name, factor in factors.items():
        out[name] = (out[name] * factor).astype(out[name].dtype)
    return out
```

```python
from contextlib import ExitStack

import numpy as np
import concourse.bass as bass
from concourse import mybir

F32 = mybir.dt.float32
F32R = mybir.dt.float32r
U32 = mybir.dt.uint32
U8 = mybir.dt.uint8
ALU = mybir.AluOpType
ACT = mybir.ActivationFunctionType
AX = mybir.AxisListType

P = 128
D = 1024
KT = D // P
SEQ = 256
CTX = 256
TOK = SEQ + CTX
NB = TOK // P
DEPTH = 2
ALPHA = (2 * DEPTH) ** 0.25
LN_EPS = 1e-5
RMS_EPS = 1e-6
HEADS = 8
LEVELS = 8
CHUNKS = 6
WCOLS = 512
MOD_TILES = DEPTH * CHUNKS * D // WCOLS
HCOLS = 5 * P
WSLOT = KT * HCOLS
SWA_Q, SWA_KV, SWA_D = 16, 4, 64
SWA_SCALE = SWA_D ** -0.5
PH = 8
TOPK = 16
NK = 128
PT_ = 256
PASSES = 3
LOWEST = -3.4e38
SCORE_MASK = -1e30

C_ID, C_IOTA, C_ONE, C_ROT, C_COS, C_SIN, C_MASK = 0, 128, 256, 384, 512, 768, 1024
C_KEEP, C_ALL = 384, 1024 + 256


class Steps:

    def __init__(self, eng, sem):
        self.eng, self.sem, self.base, self.k = eng, sem, 0, 0

    def did(self, ins):
        ins.then_inc(self.sem, 1)
        self.k += 1

    def wait(self):
        self.eng.wait_ge(self.sem, self.base + self.k)

    def link(self, ins):
        self.did(ins)
        self.wait()

    def enter(self, i, per):
        self.start = self.base + self.k
        self.base, self.k, self.per = self.start + i * per, 0, per

    def leave(self, n):
        assert self.k == self.per, (self.k, self.per)
        self.base, self.k = self.start + n * self.per, 0


def build(nc, a):
    ctx = ExitStack()
    with ctx:
        def sem(name):
            return ctx.enter_context(nc.semaphore(name))

        def sb(name, shape, dt=F32):
            return ctx.enter_context(nc.sbuf_tensor(name, shape, dt))

        modd = nc.dram_tensor("mod_scratch", [2, DEPTH * CHUNKS * D], F32, kind="Internal").ap()
        xs = nc.dram_tensor("x_scratch", [NB, P, D], F32, kind="Internal").ap()

        arena = sb("arena", [P, 128 * PT_])
        const = sb("const", [P, 384])
        modcol = sb("modcol", [P, DEPTH, 96])
        small = sb("small", [P, 160])
        u_raw = sb("u_raw", [P, 2, D])
        v_raw = sb("v_raw", [P, 2, D])
        u_hi = sb("u_hi", [P, 2, D], F32R)
        u_lo = sb("u_lo", [P, 2, D], F32R)
        v_hi = sb("v_hi", [P, 2, D], F32R)
        v_lo = sb("v_lo", [P, 2, D], F32R)
        h_hi = sb("h_hi", [P, KT, PT_], F32R)
        h_lo = sb("h_lo", [P, KT, PT_], F32R)
        act_s = sb("act_s", [P, 2, PT_])
        prod = sb("prod", [P, 2, PT_])
        p_hi = sb("p_hi", [P, 2, PT_], F32R)
        p_lo = sb("p_lo", [P, 2, PT_], F32R)
        ijw = sb("ijw", [P, 4, PT_])
        banks = [ctx.enter_context(nc.psum_tensor(f"bank{i}", [P, 512], F32)) for i in range(8)]

        def ar(off, size, **dims):
            v = arena[:, off:off + size]
            if dims:
                names = " ".join(dims)
                v = v.rearrange(f"p ({names}) -> p {names}", **dims)
            return v

        ident = const[:, C_ID:C_ID + P]
        iota = const[:, C_IOTA:C_IOTA + P]
        mean_w = const[:, C_ONE:C_ONE + P]
        lvlmask = prod[:, 0, :].bitcast(U8).rearrange("p (l t) -> p l t", l=LEVELS)
        sqbuf = act_s[:, :, :].rearrange("p a t -> p (a t)")

        W = [0, WSLOT]
        A_HT = 2 * WSLOT
        A_OT = A_HT + 4096
        A_HD = A_OT + 4096
        HD = 6144
        A_KT = A_HD + 2 * HD
        A_ST = A_KT + 768
        assert A_ST + 768 <= 128 * PT_
        hT = ar(A_HT, 4096, k=KT, t=TOK)
        oT = ar(A_OT, 4096, k=KT, t=TOK)
        xtok = ar(A_HD, 4096, b=NB, d=D)
        A_LN = A_HD
        ln_x = ar(A_LN, 4096, b=NB, d=D)
        ln_t = ar(A_LN + 4096, 2048, s=2, d=D)
        ln_m = ar(A_LN + 6144, 2048, s=2, d=D)
        ln_g = ar(A_LN + 8192, 1024)
        ln_b = ar(A_LN + 9216, 1024)

        cond = small[:, 0:16].rearrange("p (s k) -> p s k", s=2)
        lb = small[:, 16:24]
        omlb = small[:, 24:32]
        ng = small[:, 32:33]
        lgt = small[:, 33:57].rearrange("p (r h) -> p r h", r=3)
        sink = small[:, 57:73]
        stat = small[:, 73:153]
        neg_half = small[:, 153:154]

        const_in = sem("const_in")
        cond_in = sem("cond_in")
        lvlmask_in = sem("lvlmask_in")
        bias_in = sem("bias_in")
        w_loaded = [sem(f"w_loaded{i}") for i in range(2)]
        setup_t = sem("setup_transposed")
        setup_a = sem("setup_act")
        setup_v = sem("setup_vector")
        cond_done = sem("cond_done")
        mod_pe = [sem(f"mod_product{i}") for i in range(2)]
        mod_v = [sem(f"mod_biased{i}") for i in range(2)]
        mod_out = sem("mod_stored")
        mod_back = sem("mod_reloaded")
        mod_t = sem("mod_transposed")
        mod_c = sem("mod_columns")
        x_in = sem("x_loaded")
        xT_pe = sem("x_transposed")
        hT_done = sem("hT_ready")
        proj = sem("head_projected")
        vproj = sem("head_values_projected")
        sig = sem("head_sigmoids")
        vsb = sem("head_values_copied")
        init = sem("head_scaled")
        lvl = sem("level_products")
        lvlcp = sem("level_copied_out")
        upd = sem("level_decays_applied")
        kc_sb = sem("level_keys_ready")
        kt_pe = sem("keys_transposed")
        kt_sb = sem("keys_copied")
        ds = sem("state_products")
        st_done = sem("states_ready")
        o_pe = sem("head_output")
        sq_done = sem("head_squares")
        ss_pe = sem("head_square_sums")
        ms_a = sem("head_mean_squares")
        rms_p = sem("head_scales")
        y_done = sem("head_finished")
        rdiag = sem("head_scale_diagonals")
        rbc = sem("head_scales_spread")
        onorm = sem("head_normalised")
        ln_in = sem("ln_rows_loaded")
        ln_res = sem("ln_residual_loaded")
        y_pe = sem("mixer_output")
        y_used = sem("mixer_output_used")
        ln_v = sem("ln_variances")
        ln_p = sem("ln_scales")
        ln_r = sem("ln_statistics")
        ln_n = sem("ln_normalised")
        ln_o = sem("ln_finished")
        x_out = sem("x_stored")
        x1T = sem("tokens_transposed")
        h1 = sem("tokens_modulated")
        hh = sem("tokens_high_part")
        hl = sem("tokens_low_part")
        keys_in = sem("keys_loaded")
        pq_pe = sem("query_products")
        pq_sb = sem("queries_copied")
        ps_pe = sem("score_products")
        ps_sb = sem("scores_copied")
        jch = sem("choices_made")
        jon = sem("column_numbers_ready")
        ex_v = sem("gate_shifted")
        ex_a = sem("gate_exponentials")
        ch_t = sem("choices_transposed")
        ch_sb = sem("choices_copied")
        onehot = [sem(f"onehots{i}") for i in range(2)]
        g_pe = [sem(f"gate_products{i}") for i in range(2)]
        g_sb = [sem(f"gates_stored{i}") for i in range(2)]
        u_in = [sem(f"u_loaded{i}") for i in range(2)]
        v_in = [sem(f"v_loaded{i}") for i in range(2)]
        u_h = [sem(f"u_high{i}") for i in range(2)]
        u_l = [sem(f"u_low{i}") for i in range(2)]
        v_h = [sem(f"v_high{i}") for i in range(2)]
        v_l = [sem(f"v_low{i}") for i in range(2)]
        s_pe = [sem(f"expert_scores{i}") for i in range(2)]
        s_act = [sem(f"expert_gelus{i}") for i in range(2)]
        p_do = [sem(f"expert_weights{i}") for i in range(2)]
        p_h = [sem(f"weights_high{i}") for i in range(2)]
        p_l = [sem(f"weights_low{i}") for i in range(2)]
        y_ac = [sem(f"expert_outputs{i}") for i in range(2)]
        qk_pe = sem("swa_projected")
        qk_sb = sem("swa_copied")
        rot_pe = sem("swa_rotated")
        rope = sem("swa_roped")
        sv_pe = sem("swa_values_projected")
        sv_sb = sem("swa_values_copied")
        at_s = sem("swa_scores")
        at_m = sem("swa_maxima")
        at_e = sem("swa_exponentials")
        at_d = sem("swa_diagonals")
        at_t = sem("swa_probs_transposed")
        at_tc = sem("swa_probs_copied")
        at_o = sem("swa_outputs")
        at_oc = sem("swa_outputs_copied")
        swa_c = sem("swa_constants_loaded")
        lnv = sem("ln_scaled")
        jon2 = sem("column_numbers_masked")
        dstep = sem("vector_steps")

        B_HF = 2 * WSLOT
        B_Q = B_HF + 2048
        B_S = B_Q + 1024
        B_K = B_S + 4096
        B_C = B_K + 2048
        B_E = B_C + 2048
        B_F = B_E + 2048
        B_R = B_F + 2048
        assert B_R + 2048 <= 128 * PT_
        hf = ar(B_HF, 2048, k=KT, t=PT_)
        qp = ar(B_Q, 1024, c=4, t=PT_)
        sc = ar(B_S, 4096, b=2, m=16, n=NK)
        kp = ar(B_K, 2048, m=16, n=NK)
        cand = ar(B_C, 2048, h=PH, a=TOPK, b=TOPK)
        eqa = ar(B_E, 2048, h=PH, k=TOPK, a=TOPK)
        eqb = ar(B_F, 2048, h=PH, k=TOPK, a=TOPK)
        sv = ar(B_R, 256, m=16, k=TOPK)
        si = ar(B_R + 256, 256, m=16, k=TOPK)
        sif = ar(B_R + 512, 256, m=16, k=TOPK)
        bs = ar(B_R + 768, 128, h=PH, k=TOPK)
        bi = ar(B_R + 896, 128, h=PH, k=TOPK)
        ba = ar(B_R + 1024, 128, h=PH, k=TOPK)
        bb = ar(B_R + 1152, 128, h=PH, k=TOPK)
        af = ar(B_R + 1280, 128, h=PH, k=TOPK)
        bf = ar(B_R + 1408, 128, h=PH, k=TOPK)
        ijt = ar(B_R + 1536, 384, c=3, m=128)
        gsum = ar(B_R + 1920, 8)
        gate = arena[:, :].rearrange("p (t j) -> p t j", j=NK)

        T_WOUT0, T_WQ0, T_QKV, T_WOUT1, T_WQ1 = MOD_TILES, MOD_TILES + 2, MOD_TILES + 6, MOD_TILES + 9, MOD_TILES + 11

        def wt(slot):
            return ar(W[slot], KT * WCOLS, k=KT, n=WCOLS)

        def wh(slot):
            return ar(W[slot], WSLOT, k=KT, n=HCOLS)

        ORDER = ([("loop", i) for i in range(MOD_TILES)] + [("head", i) for i in range(HEADS)]
                 + [("wout0", i) for i in range(2)] + [("wqa", i) for i in range(4)] + [("wqb", i) for i in range(4)]
                 + [("qkv", i) for i in range(3)] + [("wout1", i) for i in range(2)] + [("wqc", i) for i in range(4)])
        RING = {n: k for k, n in enumerate(ORDER)}
        SRC = {"wout0": T_WOUT0, "wqa": T_WQ0, "wqb": T_WQ0, "qkv": T_QKV, "wout1": T_WOUT1, "wqc": T_WQ1}


        def onehots(buf, slot):
            return buf[:, slot, :].rearrange("p (t j) -> p t j", t=8)

        A_MOD = 2 * WSLOT
        MODN = DEPTH * CHUNKS * D
        modsb = arena[0:2, A_MOD:A_MOD + MODN]
        A_RAW = A_MOD + MODN
        modraw = arena[0:96, A_RAW:A_RAW + 256].rearrange("p (l d) -> p l d", l=DEPTH)
        condraw = arena[0:16, A_RAW + 256:A_RAW + 384]
        lbraw = arena[0:24, A_RAW + 384:A_RAW + 512]

        lvlraw = ar(A_RAW + 512, LEVELS * P)

        def mcol(layer, s, chunk, k):
            n = s * 48 + chunk * KT + k
            return modcol[:, layer, n:n + 1]

        def hd(slot, off, n):
            return arena[:, A_HD + slot * HD + off:A_HD + slot * HD + off + n]

        O_Q, O_QD, O_KD, O_C, O_G, O_V, O_AT = 0, 512, 1536, 2560, 4608, 5120, 5632

        def coff(k):
            return O_C + 2048 - (2048 >> k)

        def hap(slot, off, *dims):
            return bass.AP(tensor=arena[:, 0:1].tensor, offset=A_HD + slot * HD + off,
                           ap=[[128 * PT_, P]] + [list(d) for d in dims])

        def level_operand(slot, off, m, blk):
            return hap(slot, off + blk * P, (2 * m, P // (2 * m)), (TOK + m, 2), (1, m))

        def rmsdiag(h):
            return u_raw[:, h % 2, 0:TOK]

        kc = ijw[:, :, :].rearrange("p (s a) t -> p s (a t)", s=2)
        KTr = ar(A_KT, 768, c=6, k=P)
        STr = ar(A_ST, 768, c=6, k=P)
        FW, BW = [0, 1, 2], [1, 0, 3]
        CHAIN = FW + BW

        A_Q1 = A_OT + 2048
        A_K1 = A_HD + 4096
        q1 = ar(A_Q1, 2048, j=8, t=SEQ)
        k1 = ar(A_K1, 1024, j=2, t=TOK)
        v1 = ar(A_K1 + 1024, 1024, b=NB, c=256)
        c1 = ar(A_K1 + 2048, C_ALL - C_KEEP)
        o1 = ar(A_OT, 2048, j=8, t=SEQ)
        rawq = ar(A_K1 + 2048 + 1024, 1024, s=2, t=512)
        rtmp = ar(A_K1 + 2048 + 2048, 1024, s=2, t=512)
        prb = ar(A_K1 + 2048 + 1024, 1024, s=2, t=512)
        prT = ar(A_K1 + 2048 + 2048, 1024, s=2, t=512)
        diag = ar(A_K1 + 2048 + 3072, 256, s=2, t=P)
        assert A_K1 + 2048 + 3072 + 256 <= 128 * PT_
        rot = c1[:, C_ROT - C_KEEP:C_ROT - C_KEEP + P]
        cos = c1[:, C_COS - C_KEEP:C_COS - C_KEEP + SEQ]
        sin = c1[:, C_SIN - C_KEEP:C_SIN - C_KEEP + SEQ]
        wmask = c1[:, C_MASK - C_KEEP:C_MASK - C_KEEP + 256].rearrange("p (b k) -> p b k", b=2)

        xblk = ar(B_C, 2048, b=2, d=D)
        PASS_LAYER = [0, 0, 1]
        PASS_S = [0, 1, 1]
        LN_BASE = [4, 6, 10]
        LN1_BASE = [0, 8]
        PAIRS = NK // 2

        ON_PE = [*mod_pe, lvl, ds, ss_pe, o_pe, *g_pe, *y_ac]
        ON_ACT = [*g_sb, ms_a]
        ON_DVE = [*mod_v, *u_l, *v_l, *p_l, *p_do]

        def in_hand(eng, sems):
            for x in sems:
                eng.sem_inc(x, 1)

        block = ctx.enter_context(nc.Block())

        @block.sync
        def _(sp):
            def tile(name, i):
                k = RING[(name, i)]
                s = k % 2
                was, at = ORDER[k - 2]
                if was == "head":
                    sp.wait_ge(vproj, at + 1)
                elif was in ("wout0", "wout1"):
                    sp.wait_ge(y_pe, 4 * (at + 1) if was == "wout0" else 8 + 2 * (at + 1))
                elif was == "qkv":
                    sp.wait_ge(qk_pe if at < 2 else sv_pe, 4 * (at + 1) if at < 2 else 4)
                else:
                    sp.wait_ge(pq_pe, 4 * ["wqa", "wqb", "wqc"].index(was) + at + 1)
                sp.dma_start(ar(W[s], KT * WCOLS), a["wst"][SRC[name] + i]).then_inc(w_loaded[s], 16)

            sp.dma_start(const[:, :], a["const"][:, 0:C_KEEP]).then_inc(const_in, 16)
            sp.dma_start(condraw[0:8, :], a["c_ctx"].rearrange("(k d) -> k d", d=P)).then_inc(cond_in, 16)
            sp.dma_start(condraw[8:16, :], a["c"].rearrange("o (k d) -> (o k) d", d=P)).then_inc(cond_in, 16)
            sp.dma_start(lbraw[:, :], a["lb"].rearrange("r (h d) -> (r h) d", d=P)).then_inc(cond_in, 16)
            sp.dma_start(ng, a["ng"].rearrange("o d -> d o")).then_inc(cond_in, 16)
            sp.dma_start(sink, a["sink"].partition_broadcast(P)).then_inc(cond_in, 16)
            sp.dma_start(lvlraw, a["lvlmask"]).then_inc(lvlmask_in, 16)
            for s in range(2):
                sp.dma_start(modsb[s:s + 1, :], a["mod_b"].rearrange("(o l) n -> o (l n)", o=1)).then_inc(bias_in, 16)
            with sp.Fori(0, MOD_TILES // 2) as n:
                for s in range(2):
                    sp.wait_ge(mod_pe[s], 1 + n)
                    sp.dma_start(ar(W[s], KT * WCOLS), a["wst"][2 * n + s]).then_inc(w_loaded[s], 16)
            MT = MOD_TILES // 2
            for s in range(2):
                sp.wait_ge(mod_pe[s], 1 + MT)
                sp.dma_start(ar(W[s], WSLOT), a["whd"][s]).then_inc(w_loaded[s], 16)
            for s in range(2):
                sp.wait_ge(mod_v[s], 1 + MT)
            sp.dma_start(modd[:, :], modsb[:, :]).then_inc(mod_out, 16)
            sp.wait_ge(mod_out, 16)
            rows = modd.rearrange("s (l r d) -> s l r d", l=DEPTH, d=P)
            for l in range(DEPTH):
                for s in range(2):
                    sp.dma_start(modraw[s * 48:s * 48 + 48, l, :], rows[s, l]).then_inc(mod_back, 16)
            for b in range(2):
                sp.dma_start(xtok[:, b, :], a["ctx"][0, b * P:b * P + P, :]).then_inc(x_in, 16)
                sp.dma_start(xtok[:, 2 + b, :], a["x"][0, b * P:b * P + P, :]).then_inc(x_in, 16)
            with sp.Fori(1, HEADS // 2) as n:
                for s in range(2):
                    sp.wait_ge(vproj, 2 * n + (s - 1))
                    sp.dma_start(ar(W[s], WSLOT), a["whd"][2 * n + s]).then_inc(w_loaded[s], 16)

            def ln_rows(layer, which, streams, base, blocks, src):
                sp.dma_start(ln_g, a["ln_g"][layer, which].partition_broadcast(P)).then_inc(ln_in, 16)
                sp.dma_start(ln_b, a["ln_b"][layer, which].partition_broadcast(P)).then_inc(ln_in, 16)
                chunk = 2 if which == 0 else 5
                at = (layer * CHUNKS + chunk) * D
                for s in streams:
                    sp.dma_start(ln_m[:, s, :], modd[s, at:at + D].partition_broadcast(P)).then_inc(ln_in, 16)
                for b in blocks:
                    sp.dma_start(ln_x[:, b, :], src(b)).then_inc(ln_res, 16)

            def ln_store(base, blocks, dst):
                for k, b in enumerate(blocks):
                    sp.wait_ge(ln_o, base + k + 1)
                    sp.dma_start(dst(b), ln_x[:, b, :]).then_inc(x_out, 16)

            def x_of(b):
                return a["ctx"][0, b * P:b * P + P, :] if b < 2 else a["x"][0, (b - 2) * P:(b - 1) * P, :]

            def peer(p):
                layer, s = PASS_LAYER[p], PASS_S[p]
                blocks = [2 * s, 2 * s + 1]
                names = ["wqa", "wqb", "wqc"][p]
                sp.wait_ge(x_out, 16 * LN_BASE[p])
                for k, b in enumerate(blocks):
                    sp.dma_start(xblk[:, k, :], xs[b]).then_inc(x_in, 16)
                sp.dma_start(kp.rearrange("p m n -> p (m n)"), a["keys"][layer]).then_inc(keys_in, 16)
                for i in range(4):
                    tile(names, i)
                for q in range(2):
                    sp.wait_ge(g_pe[q], 1 + 2 * (PT_ // 16) * (p + 1))
                with sp.Fori(0, PAIRS) as n:
                    for q in range(2):
                        j = 2 * n + q
                        sp.wait_ge(u_l[q], 1 + n + p * PAIRS)
                        sp.dma_start(u_raw[:, q, :], a["u"][layer, j]).then_inc(u_in[q], 16)
                        sp.wait_ge(v_l[q], 1 + n + p * PAIRS)
                        sp.dma_start(v_raw[:, q, :], a["v"][layer, j]).then_inc(v_in[q], 16)
                sp.wait_ge(y_ac[1], 1 + PAIRS * (p + 1))
                ln_rows(layer, 1, [s], LN_BASE[p], blocks, lambda b: xs[b])
                if p < 2:
                    ln_store(LN_BASE[p], blocks, lambda b: xs[b])
                else:
                    ln_store(LN_BASE[p], blocks, lambda b: a["out"][0, (b - 2) * P:(b - 1) * P, :])

            for i in range(2):
                tile("wout0", i)
            sp.wait_ge(y_done, 1 + HEADS)
            ln_rows(0, 0, [0, 1], 0, range(4), x_of)
            ln_store(0, range(4), lambda b: xs[b])
            peer(0)
            peer(1)
            for b in range(NB):
                if b == 0:
                    sp.wait_ge(x_out, 16 * 8)
                sp.dma_start(xtok[:, b, :], xs[b]).then_inc(x_in, 16)
            sp.dma_start(c1, a["const"][:, C_KEEP:C_ALL]).then_inc(swa_c, 16)
            for i in range(3):
                tile("qkv", i)
            for i in range(2):
                tile("wout1", i)
            sp.wait_ge(at_oc, 32)
            ln_rows(1, 0, [1], 8, [2, 3], lambda b: xs[b])
            ln_store(8, [2, 3], lambda b: xs[b])
            peer(2)
            sp.wait_ge(x_out, 16 * 12)

        @block.tensor
        def _(pe):
            mm = nc.tensor.matmul
            in_hand(pe, ON_PE)

            def arrived(name, i):
                k = RING[(name, i)]
                pe.wait_ge(w_loaded[k % 2], 16 * (k // 2 + 1))
                return k % 2

            pe.wait_ge(const_in, 16)
            pe.wait_ge(cond_in, 80)
            nc.tensor.transpose(banks[2][:, 0:16], condraw, ident[0:16, 0:16])
            nc.tensor.transpose(banks[3][:, 0:24], lbraw, ident[0:24, 0:24]).then_inc(setup_t, 1)
            pe.wait_ge(cond_done, 1)
            with pe.Fori(0, MOD_TILES // 2) as n:
                for s in range(2):
                    pe.wait_ge(w_loaded[s], 16 * n + 16)
                    pe.wait_ge(mod_v[s], 1 + n)
                    for k in range(KT):
                        last = mm(banks[s][0:2, :], cond[:, :, k], wt(s)[:, k, :], start=(k == 0), stop=(k == KT - 1))
                    last.then_inc(mod_pe[s], 1)
            pe.wait_ge(mod_back, 64)
            for l in range(DEPTH):
                last = nc.tensor.transpose(banks[2 + l][:, 0:96], modraw[:, l, :], ident[0:96, 0:96])
            last.then_inc(mod_t, 1)

            def transpose_x(layer, need):
                pe.wait_ge(x_in, need)
                for k in range(KT):
                    if k >= 2:
                        pe.wait_ge(hT_done, 2 * (8 * layer + k - 1))
                    for b in range(NB):
                        last = nc.tensor.transpose(banks[k % 2][:, b * P:(b + 1) * P], xtok[:, b, k * P:(k + 1) * P], ident)
                    last.then_inc(xT_pe, 1)
                pe.wait_ge(hT_done, 16 * (layer + 1))

            transpose_x(0, 64)

            MT = MOD_TILES // 2

            def proj_piece(slot, c, half):
                for k in range(4 * half, 4 * half + 4):
                    last = mm(banks[c][:, :], wh(slot)[:, k, c * P:(c + 1) * P], hT[:, k, :], start=(k == 0), stop=(k == KT - 1))
                if half:
                    last.then_inc(proj, 1)

            def value_piece(slot, b, final):
                for k in range(KT):
                    last = mm(banks[7][:, b * P:(b + 1) * P], hT[:, k, b * P:(b + 1) * P], wh(slot)[:, k, 4 * P:5 * P],
                              start=(k == 0), stop=(k == KT - 1))
                if final:
                    last.then_inc(vproj, 1)

            pe.wait_ge(w_loaded[0], 16 * (MT + 1))
            for c in range(4):
                for half in range(2):
                    proj_piece(0, c, half)
            for b in range(NB):
                value_piece(0, b, b == NB - 1)

            def head(h, slot, more, wfill):
                nxt = 1 - slot
                if more:
                    pe.wait_ge(w_loaded[nxt], wfill)
                for l in range(LEVELS):
                    if l == 0:
                        pe.wait_ge(init, h + 1)
                    if more:
                        proj_piece(nxt, l // 2, l % 2)
                    if l == 0:
                        pe.wait_ge(y_done, h + 1)
                    if l == 1:
                        pe.wait_ge(ms_a, 1 + h)
                    if l >= 2:
                        pe.wait_ge(lvlcp, 8 * h + l - 1)
                    bank = banks[4 + l % 2]
                    for b in range(NB):
                        out = bank[:, b * P:(b + 1) * P]
                        if l == 0:
                            qb = hd(slot, O_Q + b * P, P)
                            mm(out, hd(slot, O_KD + b * P, P), qb, start=True, stop=False)
                            last = mm(out, hd(slot, O_KD + TOK + b * P, P), qb, start=False, stop=True)
                        else:
                            m = 1 << (l - 1)
                            if b == 0:
                                pe.wait_ge(kc_sb, 7 * h + l)
                            last = mm(out, kc[:, l % 2, b * P:(b + 1) * P], level_operand(slot, O_QD, m, b), start=True, stop=True)
                    last.then_inc(lvl, 1)
                pe.wait_ge(upd, 7 * h + 7)
                for d in range(2):
                    if d:
                        pe.wait_ge(lvlcp, 8 * h + 7)
                    for i in range(3):
                        b = CHAIN[3 * d + i]
                        last = nc.tensor.transpose(banks[6 - 2 * d][:, i * P:(i + 1) * P], hd(slot, O_KD + d * TOK + b * P, P), ident)
                    last.then_inc(kt_pe, 1)
                if more:
                    value_piece(nxt, 0, False)
                for d in range(2):
                    pe.wait_ge(kt_sb, 2 * h + d + 1)
                    if d == 0:
                        pe.wait_ge(lvlcp, 8 * h + 8)
                        pe.wait_ge(vsb, h + 1)
                    for i in range(3):
                        b = CHAIN[3 * d + i]
                        last = mm(banks[5 + d][:, i * P:(i + 1) * P], KTr[:, 3 * d + i, :], hd(slot, O_V + b * P, P), start=True, stop=True)
                    last.then_inc(ds, 1)
                    if more:
                        value_piece(nxt, 1 + d, False)
                for b in range(NB):
                    out = banks[4][:, b * P:(b + 1) * P]
                    terms = [(hd(slot, O_V + b * P, P), hd(slot, O_AT + b * P, P))]
                    if b:
                        terms.append((STr[:, b - 1, :], hd(slot, O_QD + TOK + b * P, P)))
                    if b != 1:
                        terms.append((STr[:, {0: 3, 3: 4, 2: 5}[b], :], hd(slot, O_QD + b * P, P)))
                    if b == 0:
                        pe.wait_ge(st_done, h + 1)
                    for i, (x, y) in enumerate(terms):
                        last = mm(out, x, y, start=(i == 0), stop=(i == len(terms) - 1))
                last.then_inc(o_pe, 1)
                if more:
                    value_piece(nxt, 3, True)
                pe.wait_ge(sq_done, h + 1)
                for b in range(NB):
                    last = mm(banks[5][:, b:b + 1], sqbuf[:, b * P:(b + 1) * P], mean_w[:, 0:1], start=True, stop=True)
                last.then_inc(ss_pe, 1)

            with pe.Fori(0, HEADS // 2 - 1) as n:
                head(2 * n, 0, True, 16 * n + 16 * (MT + 1))
                head(2 * n + 1, 1, True, 16 * n + 16 * (MT + 2))
            head(HEADS - 2, 0, True, 16 * (MT + HEADS // 2))
            head(HEADS - 1, 1, False, 0)

            def mixer_out(name, oview, blocks, bank0):
                for half in range(2):
                    s = arrived(name, half)
                    for i, b in enumerate(blocks):
                        for k in range(KT):
                            last = mm(banks[bank0 + 2 * i + half][:, :], oview[:, k, b * P:(b + 1) * P], wt(s)[:, k, :],
                                      start=(k == 0), stop=(k == KT - 1))
                        last.then_inc(y_pe, 1)

            for h in range(HEADS):
                pe.wait_ge(rdiag, h + 1)
                mm(banks[h % 4][:, :], mean_w, rmsdiag(h), start=True, stop=True).then_inc(rbc, 1)
            pe.wait_ge(onorm, HEADS)
            mixer_out("wout0", oT, range(4), 0)

            def peer(p):
                layer, s = PASS_LAYER[p], PASS_S[p]
                pe.wait_ge(x_in, [64 + 32, 64 + 64, 64 + 64 + 64 + 32][p])
                pe.wait_ge(ln_o, LN_BASE[p])
                for k in range(KT):
                    if k >= 2:
                        pe.wait_ge(h1, 8 * p + k - 1)
                    for b in range(2):
                        last = nc.tensor.transpose(banks[k % 2][:, b * P:(b + 1) * P], xblk[:, b, k * P:(k + 1) * P], ident)
                    last.then_inc(x1T, 1)
                pe.wait_ge(h1, 8 * p + 8)
                for i in range(4):
                    w = arrived(["wqa", "wqb", "wqc"][p], i)
                    if i:
                        pe.wait_ge(pq_sb, 4 * p + i)
                    for m in range(4):
                        for k in range(KT):
                            last = mm(banks[2 + m // 2][:, (m % 2) * PT_:(m % 2 + 1) * PT_], wt(w)[:, k, m * P:(m + 1) * P],
                                      hf[:, k, :], start=(k == 0), stop=(k == KT - 1))
                    last.then_inc(pq_pe, 1)
                    if i == 0:
                        pe.wait_ge(keys_in, 16 * (p + 1))
                    pe.wait_ge(pq_sb, 4 * p + i + 1)
                    for b in range(2):
                        if i:
                            pe.wait_ge(ps_sb, 2 * (4 * p + i - 1) + b + 1)
                        for m in range(4):
                            last = mm(banks[4 + b][:, m * NK:(m + 1) * NK], qp[:, m, b * P:(b + 1) * P], kp[:, 4 * i + m, :],
                                      start=True, stop=True)
                        last.then_inc(ps_pe, 1)
                for b in range(2):
                    pe.wait_ge(jch, 2 * p + b + 1)
                    for c in range(3):
                        last = nc.tensor.transpose(banks[6 + b][:, c * P:(c + 1) * P], ijt[:, c, :], ident)
                    last.then_inc(ch_t, 1)
                with pe.Fori(0, PT_ // 16) as n:
                    for q in range(2):
                        N = n + p * (PT_ // 16)
                        pe.wait_ge(onehot[q], N + 1)
                        pe.wait_ge(g_sb[q], 1 + 2 * N)
                        for half in range(2):
                            for t in range(4 * half, 4 * half + 4):
                                out = banks[2 * q + half][:, (t % 4) * NK:(t % 4 + 1) * NK]
                                last = mm(out, onehots(u_raw, q)[:, t, :], onehots(v_raw, q)[:, t, :], start=True, stop=True)
                            last.then_inc(g_pe[q], 1)
                pe.wait_ge(hl, 8 * (p + 1))

                def scores(q, N):
                    pe.wait_ge(u_l[q], 1 + N + 1)
                    pe.wait_ge(s_act[q], N)
                    n3 = 0
                    for k in range(KT):
                        col = slice(k * P, (k + 1) * P)
                        for w, h in ((u_hi, h_hi), (u_hi, h_lo), (u_lo, h_hi)):
                            last = mm(banks[q][:, 0:PT_], w[:, q, col], h[:, k, :], start=(n3 == 0), stop=(n3 == 3 * KT - 1))
                            n3 += 1
                    last.then_inc(s_pe[q], 1)

                def outputs(q, N, first, final):
                    pe.wait_ge(p_l[q], 1 + N + 1)
                    pe.wait_ge(v_l[q], 1 + N + 1)
                    for b in range(2):
                        for half in range(2):
                            col = slice(half * 512, half * 512 + 512)
                            for i, (x, y) in enumerate(((p_hi, v_hi), (p_hi, v_lo), (p_lo, v_hi))):
                                last = mm(banks[2 + 2 * b + half][:, :], x[:, q, b * P:(b + 1) * P], y[:, q, col],
                                          start=(first and i == 0), stop=(final and i == 2))
                    last.then_inc(y_ac[q], 1)

                N0 = p * PAIRS
                scores(0, N0)
                pe.wait_ge(g_sb[1], 1 + 2 * (PT_ // 16) * (p + 1))
                scores(1, N0)
                outputs(0, N0, True, False)
                with pe.Fori(0, PAIRS - 1) as n:
                    scores(0, n + N0 + 1)
                    outputs(1, n + N0, False, False)
                    scores(1, n + N0 + 1)
                    outputs(0, n + N0 + 1, False, False)
                outputs(1, N0 + PAIRS - 1, False, True)

            peer(0)
            peer(1)
            transpose_x(1, 64 + 64 + 64)

            n_qk = 0
            for i in range(2):
                w = arrived("qkv", i)
                for m in range(4):
                    if n_qk >= 2:
                        pe.wait_ge(rope, n_qk - 1)
                    for k in range(KT):
                        last = mm(banks[n_qk % 2][:, 0:SEQ], wt(w)[:, k, m * P:(m + 1) * P], hT[:, k, CTX:TOK],
                                  start=(k == 0), stop=(k == KT - 1))
                    last.then_inc(qk_pe, 1)
                    pe.wait_ge(qk_sb, n_qk + 1)
                    if n_qk == 0:
                        pe.wait_ge(swa_c, 16)
                    mm(banks[2 + n_qk % 2][:, 0:SEQ], rot, rawq[:, n_qk % 2, 0:SEQ], start=True, stop=True).then_inc(rot_pe, 1)
                    n_qk += 1
            w = arrived("qkv", 2)
            for m in range(2):
                pe.wait_ge(rope, n_qk - 1)
                for k in range(KT):
                    last = mm(banks[n_qk % 2][:, :], wt(w)[:, k, m * P:(m + 1) * P], hT[:, k, :], start=(k == 0), stop=(k == KT - 1))
                last.then_inc(qk_pe, 1)
                pe.wait_ge(qk_sb, n_qk + 1)
                mm(banks[2 + n_qk % 2][:, 0:SEQ], rot, rawq[:, n_qk % 2, CTX:TOK], start=True, stop=True).then_inc(rot_pe, 1)
                n_qk += 1
            for b in range(NB):
                for k in range(KT):
                    last = mm(banks[4 + b // 2][:, (b % 2) * 256:(b % 2 + 1) * 256], hT[:, k, b * P:(b + 1) * P], wt(w)[:, k, 256:512],
                              start=(k == 0), stop=(k == KT - 1))
                last.then_inc(sv_pe, 1)
            pe.wait_ge(rope, 10)
            pe.wait_ge(sv_sb, 1)

            def att_scores(i):
                j, half, b = i // 4, i % 2, (i // 2) % 2
                bank = banks[i % 2]
                rows = slice(half * SWA_D, (half + 1) * SWA_D)
                if i >= 2:
                    pe.wait_ge(at_e, i - 1)
                mm(bank[:, :], q1[rows, j, b * P:(b + 1) * P], k1[rows, j // 4, :], start=True, stop=False)
                far = slice(CTX + P, TOK) if b == 0 else slice(CTX, CTX + P)
                mm(bank[:, far], ident, wmask[:, b, :], start=False, stop=True).then_inc(at_s, 1)

            att_scores(0)
            for i in range(32):
                j, half, b = i // 4, i % 2, (i // 2) % 2
                if i < 31:
                    att_scores(i + 1)
                pe.wait_ge(at_d, i + 1)
                pe.wait_ge(at_e, i + 1)
                if i >= 2:
                    pe.wait_ge(at_tc, i - 1)
                for c in range(4):
                    last = mm(banks[2 + i % 2][:, c * P:(c + 1) * P], prb[:, i % 2, c * P:(c + 1) * P], diag[:, i % 2, :],
                              start=True, stop=True)
                last.then_inc(at_t, 1)
                pe.wait_ge(at_tc, i + 1)
                if i >= 2:
                    pe.wait_ge(at_oc, i - 1)
                kv = 2 * (j // 4) + half
                for c in range(4):
                    last = mm(banks[4 + i % 2][half * SWA_D:(half + 1) * SWA_D, 0:P], v1[:, c, kv * SWA_D:(kv + 1) * SWA_D],
                              prT[:, i % 2, c * P:(c + 1) * P], start=(c == 0), stop=(c == 3))
                last.then_inc(at_o, 1)
            pe.wait_ge(at_oc, 32)
            mixer_out("wout1", o1, range(2), 0)
            peer(2)

        @block.scalar
        def _(act):
            af_ = nc.scalar.activation
            in_hand(act, ON_ACT)
            act.wait_ge(setup_t, 1)
            af_(cond.rearrange("p s k -> p (s k)"), banks[2][:, 0:16], ACT.Sigmoid).then_inc(setup_a, 1)
            act.wait_ge(setup_v, 1)
            af_(lgt, lgt, ACT.Exp).then_inc(setup_a, 1)

            def modulate_x(layer):
                for k in range(KT):
                    act.wait_ge(xT_pe, 8 * layer + k + 1)
                    for s in range(2):
                        cols = slice(s * CTX, (s + 1) * CTX)
                        af_(hT[:, k, cols], banks[k % 2][:, cols], ACT.Identity,
                            scale=mcol(layer, s, 1, k), bias=mcol(layer, s, 0, k)).then_inc(hT_done, 1)

            act.wait_ge(mod_c, 2)
            modulate_x(0)

            def sigmoid(g, slot, c):
                off = (O_Q, coff(0) + TOK, coff(0), O_G)[c]
                act.wait_ge(proj, 4 * g + c + 1)
                af_(hd(slot, off, TOK), banks[c][:, :], ACT.Sigmoid).then_inc(sig, 1)

            def values(g, slot):
                act.wait_ge(vproj, g + 1)
                af_(hd(slot, O_V, TOK), banks[7][:, :], ACT.Copy).then_inc(vsb, 1)

            def head(h, slot, more):
                for l in range(1, LEVELS):
                    if l == 1:
                        act.wait_ge(init, h + 1)
                    else:
                        act.wait_ge(upd, 7 * h + l - 1)
                    act.wait_ge(lvl, 1 + 8 * h + (l - 1 if l > 2 else 0))
                    m = 1 << (l - 1)
                    af_(kc[:, l % 2, :].rearrange("p (n w r) -> p n w r", w=2, r=m),
                        hap(slot, O_KD, (2 * m, TOK // (2 * m)), (TOK + m, 2), (1, m)), ACT.Copy).then_inc(kc_sb, 1)
                    if more and l % 2:
                        if l == 1:
                            act.wait_ge(y_done, h + 1)
                        sigmoid(h + 1, 1 - slot, l // 2)
                for d in range(2):
                    act.wait_ge(kt_pe, 2 * h + d + 1)
                    act.wait_ge(ds, 1 + 2 * h)
                    af_(KTr[:, 3 * d:3 * d + 3, :].rearrange("p c k -> p (c k)"), banks[6 - 2 * d][:, 0:3 * P], ACT.Copy).then_inc(kt_sb, 1)
                act.wait_ge(o_pe, 1 + h + 1)
                act.wait_ge(ss_pe, 1 + h)
                af_(sqbuf, banks[4][:, :], ACT.Square).then_inc(sq_done, 1)
                if more:
                    values(h + 1, 1 - slot)
                act.wait_ge(ss_pe, 1 + h + 1)
                dst = stat[:, h * NB:(h + 1) * NB] if isinstance(h, int) else stat[:, bass.ds(h * NB, NB)]
                af_(dst, banks[5][:, 0:NB], ACT.Copy, bias=RMS_EPS).then_inc(ms_a, 1)

            for c in range(4):
                sigmoid(0, 0, c)
            values(0, 0)
            with act.Fori(0, HEADS // 2 - 1) as n:
                head(2 * n, 0, True)
                head(2 * n + 1, 1, True)
            head(HEADS - 2, 0, True)
            head(HEADS - 1, 1, False)

            def norms(base, blocks):
                for i, b in enumerate(blocks):
                    act.wait_ge(ln_r, base + i + 1)
                    st = stat[:, (i % 4) * 20:(i % 4) * 20 + 20]
                    af_(ln_t[:, i % 2, :], ln_x[:, b, :], ACT.Identity, scale=st[:, 14:15], bias=st[:, 15:16]).then_inc(ln_n, 1)

            norms(0, range(4))

            def peer(p):
                layer, s = PASS_LAYER[p], PASS_S[p]
                for k in range(KT):
                    act.wait_ge(x1T, 8 * p + k + 1)
                    af_(hf[:, k, :], banks[k % 2][:, 0:PT_], ACT.Identity,
                        scale=mcol(layer, s, 4, k), bias=mcol(layer, s, 3, k)).then_inc(h1, 1)
                for k in range(KT):
                    if k == 0:
                        act.wait_ge(h1, 8 * p + 8)
                    af_(h_hi[:, k, :], hf[:, k, :], ACT.Copy).then_inc(hh, 1)
                for i in range(4):
                    act.wait_ge(pq_pe, 4 * p + i + 1)
                    act.wait_ge(ps_pe, 2 * (4 * p + i))
                    for half in range(2):
                        ins = af_(qp[:, 2 * half:2 * half + 2, :].rearrange("p c t -> p (c t)"), banks[2 + half][:, :], ACT.Copy)
                    ins.then_inc(pq_sb, 1)
                    for b in range(2):
                        act.wait_ge(ps_pe, 2 * (4 * p + i) + b + 1)
                        af_(sc[:, b, 4 * i:4 * i + 4, :].rearrange("p m n -> p (m n)"), banks[4 + b][:, :], ACT.Copy).then_inc(ps_sb, 1)
                for b in range(2):
                    act.wait_ge(ex_v, 2 * p + b + 1)
                    af_(bs[:, :, :], bs[:, :, :], ACT.Exp).then_inc(ex_a, 1)
                for b in range(2):
                    act.wait_ge(ch_t, 2 * p + b + 1)
                    ins = af_(ijw[:, 0:3, b * P:(b + 1) * P], banks[6 + b][:, 0:3 * P].rearrange("p (c t) -> p c t", c=3), ACT.Copy)
                    ins.then_inc(ch_sb, 1)
                with act.Fori(0, PT_ // 16) as n:
                    for q in range(2):
                        N = n + p * (PT_ // 16)
                        for half in range(2):
                            act.wait_ge(g_pe[q], 1 + 2 * N + half + 1)
                            t0 = 16 * n + 8 * q + 4 * half
                            af_(gate[:, bass.ds(t0, 4), :], banks[2 * q + half][:, :].rearrange("p (t j) -> p t j", t=4), ACT.Copy).then_inc(g_sb[q], 1)

                def high_u(q, N):
                    act.wait_ge(u_in[q], 16 * N + 16)
                    act.wait_ge(s_pe[q], N)
                    af_(u_hi[:, q, :], u_raw[:, q, :], ACT.Copy).then_inc(u_h[q], 1)

                def step(q, N, nq, nN, more=True):
                    if more:
                        high_u(nq, nN)
                    act.wait_ge(s_pe[q], N + 1)
                    act.wait_ge(p_do[q], 1 + N)
                    af_(act_s[:, q, :], banks[q][:, 0:PT_], ACT.Gelu_apprx_tanh).then_inc(s_act[q], 1)
                    act.wait_ge(v_in[q], 16 * N + 16)
                    act.wait_ge(y_ac[q], 1 + N)
                    af_(v_hi[:, q, :], v_raw[:, q, :], ACT.Copy).then_inc(v_h[q], 1)
                    act.wait_ge(p_do[q], 1 + N + 1)
                    af_(p_hi[:, q, :], prod[:, q, :], ACT.Copy).then_inc(p_h[q], 1)

                N0 = p * PAIRS
                G16 = PT_ // 16
                for q in range(2):
                    act.wait_ge(g_pe[q], 1 + 2 * G16 * (p + 1))
                high_u(0, N0)
                step(0, N0, 1, N0)
                with act.Fori(0, PAIRS - 1) as n:
                    step(1, n + N0, 0, n + N0 + 1)
                    step(0, n + N0 + 1, 1, n + N0 + 1)
                step(1, N0 + PAIRS - 1, 0, 0, more=False)
                norms(LN_BASE[p], [2 * s, 2 * s + 1])

            peer(0)
            peer(1)
            modulate_x(1)
            for i in range(10):
                act.wait_ge(qk_pe, i + 1)
                if i >= 2:
                    act.wait_ge(rope, i - 1)
                n = SEQ if i < 8 else TOK
                af_(rawq[:, i % 2, 0:n], banks[i % 2][:, 0:n], ACT.Copy).then_inc(qk_sb, 1)
            act.wait_ge(sv_pe, 4)
            for i in range(2):
                ins = af_(v1[:, 2 * i:2 * i + 2, :].rearrange("p b c -> p (b c)"), banks[4 + i][:, :], ACT.Copy)
            ins.then_inc(sv_sb, 1)
            for i in range(32):
                st = stat[:, (i % 4) * 20:(i % 4) * 20 + 20]
                act.wait_ge(at_m, i + 1)
                if i == 0:
                    act.wait_ge(rope, 10)
                if i >= 2:
                    act.wait_ge(at_t, i - 1)
                af_(prb[:, i % 2, :], banks[i % 2][:, :], ACT.Exp, scale=SWA_SCALE, bias=st[:, 2:3], accum_out=st[:, 3:4])
                af_(st[:, 4:5], st[:, 5:6], ACT.Exp, bias=st[:, 2:3]).then_inc(at_e, 1)
                act.wait_ge(at_t, i + 1)
                if i >= 2:
                    act.wait_ge(at_o, i - 1)
                af_(prT[:, i % 2, :], banks[2 + i % 2][:, :], ACT.Copy).then_inc(at_tc, 1)
            norms(8, [2, 3])
            peer(2)

        @block.vector
        def _(dve):
            V = nc.vector
            st_ = Steps(dve, dstep)
            link, did = st_.link, st_.did
            in_hand(dve, ON_DVE)
            V.memset(neg_half, -0.5)
            dve.wait_ge(setup_a, 1)
            V.tensor_tensor(cond.rearrange("p s k -> p (s k)"), banks[2][:, 0:16], cond.rearrange("p s k -> p (s k)"), ALU.mult).then_inc(cond_done, 1)
            lgf = banks[3][:, 0:24].rearrange("p (r h) -> p r h", r=3)
            link(V.tensor_copy(lgt, lgf))
            link(V.tensor_tensor(lb, lgt[:, 0, :], lgt[:, 1, :], ALU.max))
            link(V.tensor_tensor(lb, lb, lgt[:, 2, :], ALU.max))
            V.tensor_tensor(lgt, lgt, lb.unsqueeze(1).broadcast_to([P, 3, HEADS]), ALU.subtract).then_inc(setup_v, 1)
            dve.wait_ge(setup_a, 2)
            link(V.tensor_tensor(lb, lgt[:, 0, :], lgt[:, 1, :], ALU.add))
            link(V.tensor_tensor(lb, lb, lgt[:, 2, :], ALU.add))
            link(V.reciprocal(lb, lb))
            link(V.tensor_tensor(lb, lb, lgt[:, 0, :], ALU.mult))
            link(V.tensor_scalar(omlb, lb, -1.0, 1.0, ALU.mult, ALU.add))
            dve.wait_ge(lvlmask_in, 16)
            V.tensor_copy(lvlmask.rearrange("p l t -> p (l t)"), lvlraw)
            dve.wait_ge(bias_in, 32)
            with dve.Fori(0, MOD_TILES // 2) as n:
                for s in range(2):
                    dve.wait_ge(mod_pe[s], 1 + n + 1)
                    row = modsb[:, bass.ds((2 * n + s) * WCOLS, WCOLS)]
                    V.tensor_tensor(row, banks[s][0:2, :], row, ALU.add).then_inc(mod_v[s], 1)
            dve.wait_ge(mod_t, 1)
            for l in range(DEPTH):
                did(V.tensor_copy(modcol[:, l, :], banks[2 + l][:, 0:96]))
            st_.wait()
            for chunk in (1, 4):
                c = modcol[:, :, :].rearrange("p l (s c k) -> p l s c k", s=2, c=CHUNKS)[:, :, :, chunk, :]
                V.tensor_scalar(c, c, 1.0, None, ALU.add).then_inc(mod_c, 1)

            link(V.tensor_scalar(ng, ng, float(P), None, ALU.mult))
            V.memset(stat, 0.0).then_inc(y_done, 1)

            def scale_head(g, slot):
                dve.wait_ge(sig, 4 * g + 4)
                dve.wait_ge(proj, 4 * g + 4)
                q = hd(slot, O_Q, TOK)
                f2 = hd(slot, coff(0), 2 * TOK)
                did(V.tensor_tensor(q, banks[0][:, :], q, ALU.mult))
                gg = hd(slot, O_G, TOK)
                did(V.tensor_tensor(gg, banks[3][:, :], gg, ALU.mult))
                h1_, l1_ = (omlb[:, bass.ds(g, 1)], lb[:, bass.ds(g, 1)])
                did(V.tensor_scalar(f2, f2, h1_, l1_, ALU.mult, ALU.add))
                st_.wait()
                for d in range(2):
                    did(V.tensor_scalar(hd(slot, O_KD + d * TOK, TOK), hd(slot, coff(0) + (1 - d) * TOK, TOK), -1.0, 1.0, ALU.mult, ALU.add))
                V.tensor_tensor(hap(slot, O_QD, (TOK, 2), (1, TOK)), hap(slot, coff(0), (TOK, 2), (1, TOK)),
                                hap(slot, O_Q, (0, 2), (1, TOK)), ALU.mult).then_inc(init, 1)

            def levels(h, slot):
                at = hd(slot, O_AT, TOK).rearrange("p (b t) -> p b t", b=NB)
                for l in range(LEVELS):
                    dve.wait_ge(lvl, 1 + 8 * h + l + 1)
                    src = banks[4 + l % 2][:, :].rearrange("p (b t) -> p b t", b=NB)
                    if l == 0:
                        V.tensor_copy(at, src).then_inc(lvlcp, 1)
                        continue
                    dve.wait_ge(lvlcp, 8 * h + l)
                    k, m = l - 1, 1 << (l - 1)
                    ns, blocks = TOK // m, TOK // (2 * m)
                    qv = hap(slot, O_QD, (2 * m, blocks), (TOK + m, 2), (1, m))
                    kv = hap(slot, O_KD, (2 * m, blocks), (TOK + m, 2), (1, m))
                    cq = hap(slot, coff(k) + 1, (2, blocks), (ns - 1, 2), (0, m))
                    ck = hap(slot, coff(k) + ns + 1, (2, blocks), (-(ns + 1), 2), (0, m))
                    if l == 1:
                        dve.wait_ge(init, h + 1)
                    else:
                        dve.wait_ge(upd, 7 * h + l - 1)
                    V.tensor_tensor(hap(slot, coff(k + 1), (1, 2 * blocks)), hap(slot, coff(k), (2, 2 * blocks)), hap(slot, coff(k) + 1, (2, 2 * blocks)), ALU.mult)
                    V.copy_predicated(at, lvlmask[:, l, :].unsqueeze(1).broadcast_to([P, NB, P]), src).then_inc(lvlcp, 1)
                    V.tensor_tensor(qv, qv, cq, ALU.mult)
                    V.tensor_tensor(kv, kv, ck, ALU.mult).then_inc(upd, 1)

            def states(h, slot):
                decay = lambda d, b: hd(slot, coff(7) + 4 * (1 - d) + b, 1)
                dve.wait_ge(o_pe, 1 + h)
                dve.wait_ge(upd, 7 * h + 7)
                for d in range(2):
                    dve.wait_ge(ds, 1 + 2 * h + d + 1)
                    for i in range(3):
                        src = banks[5 + d][:, i * P:(i + 1) * P]
                        if i == 0:
                            ins = V.tensor_copy(STr[:, 3 * d, :], src)
                        else:
                            ins = V.scalar_tensor_tensor(STr[:, 3 * d + i, :], STr[:, 3 * d + i - 1, :], decay(d, CHAIN[3 * d + i]), src, ALU.mult, ALU.add)
                        if d == 1 and i == 2:
                            ins.then_inc(st_done, 1)
                        else:
                            link(ins)

            def finish(h, slot):
                dve.wait_ge(sq_done, h + 1)
                V.scalar_tensor_tensor(arena[:, bass.ds(A_OT + h * TOK, TOK)] if not isinstance(h, int) else oT[:, h, :],
                                       banks[4][:, :], ng, hd(slot, O_G, TOK), ALU.mult, ALU.mult).then_inc(y_done, 1)

            def head(h, slot, more):
                levels(h, slot)
                states(h, slot)
                if more:
                    scale_head(h + 1, 1 - slot)
                finish(h, slot)

            scale_head(0, 0)
            PER = 2 * (5 + 5)
            with dve.Fori(0, HEADS // 2 - 1) as n:
                st_.enter(n, PER)
                head(2 * n, 0, True)
                head(2 * n + 1, 1, True)
            st_.leave(HEADS // 2 - 1)
            head(HEADS - 2, 0, True)
            head(HEADS - 1, 1, False)
            dve.wait_ge(rms_p, 1)
            for h in range(HEADS):
                if h >= 2:
                    dve.wait_ge(rbc, h - 1)
                V.tensor_tensor(rmsdiag(h).rearrange("p (b t) -> p b t", b=NB), ident.unsqueeze(1).broadcast_to([P, NB, P]),
                                stat[:, h * NB:(h + 1) * NB].unsqueeze(2).broadcast_to([P, NB, P]), ALU.mult).then_inc(rdiag, 1)
                if h:
                    dve.wait_ge(rbc, h)
                    V.tensor_tensor(oT[:, h - 1, :], banks[(h - 1) % 4][:, :], oT[:, h - 1, :], ALU.mult).then_inc(onorm, 1)
            dve.wait_ge(rbc, HEADS)
            V.tensor_tensor(oT[:, HEADS - 1, :], banks[(HEADS - 1) % 4][:, :], oT[:, HEADS - 1, :], ALU.mult).then_inc(onorm, 1)

            def norms(base, blocks, bank0, rows_in, res_in, stream):
                dve.wait_ge(ln_in, rows_in)
                dve.wait_ge(ln_res, res_in)
                done = []

                def front(i, b):
                    st = stat[:, (i % 4) * 20:(i % 4) * 20 + 20]
                    if i >= 2:
                        dve.wait_ge(ln_o, base + i - 1)
                    for half in range(2):
                        cols = slice(512 * half, 512 * half + 512)
                        ins = V.tensor_tensor(ln_t[:, i % 2, cols], banks[bank0 + 2 * i + half][:, :], ln_m[:, stream(b), cols], ALU.mult)
                        did(ins)
                    st_.wait()
                    link(V.scalar_tensor_tensor(ln_x[:, b, :], ln_x[:, b, :], ALPHA, ln_t[:, i % 2, :], ALU.mult, ALU.add))
                    for half in range(2):
                        did(V.bn_stats(st[:, 6 * half:6 * half + 6], ln_x[:, b, 512 * half:512 * half + 512]))
                    st_.wait()
                    link(V.bn_aggr(st[:, 12:14], st[:, 0:12]))
                    V.tensor_scalar(st[:, 13:14], st[:, 13:14], LN_EPS, None, ALU.add).then_inc(ln_v, 1)
                    dve.wait_ge(ln_p, base + i + 1)
                    V.scalar_tensor_tensor(st[:, 15:16], st[:, 12:13], -1.0, st[:, 14:15], ALU.mult, ALU.mult).then_inc(ln_r, 1)

                def back(i, b):
                    dve.wait_ge(ln_n, base + i + 1)
                    V.tensor_tensor(ln_t[:, i % 2, :], ln_t[:, i % 2, :], ln_g, ALU.mult).then_inc(lnv, 1)

                for i, b in enumerate(blocks):
                    front(i, b)
                    if i:
                        back(i - 1, blocks[i - 1])
                back(len(blocks) - 1, blocks[len(blocks) - 1])

            dve.wait_ge(y_pe, 8)
            norms(0, list(range(4)), 0, 64, 64, lambda b: b // 2)

            def top16(vals, idx, src):
                link(V.max(vals[:, 0:8], src))
                link(V.max_index(idx[:, 0:8], vals[:, 0:8], src))
                link(V.match_replace(src, vals[:, 0:8], src, LOWEST))
                link(V.max(vals[:, 8:16], src))
                link(V.max_index(idx[:, 8:16], vals[:, 8:16], src))

            def peer(p):
                layer, s = PASS_LAYER[p], PASS_S[p]
                for k in range(KT):
                    dve.wait_ge(hh, 8 * p + k + 1)
                    V.tensor_tensor(h_lo[:, k, :], hf[:, k, :], h_hi[:, k, :], ALU.subtract).then_inc(hl, 1)
                siu = si.bitcast(U32)
                biu = bi.bitcast(U32)
                for b in range(2):
                    if b:
                        dve.wait_ge(ch_t, 2 * p + b)
                    for m in range(16):
                        if b == 0 and m % 4 == 0:
                            dve.wait_ge(ps_sb, 2 * (4 * p + m // 4) + 2)
                        src = sc[:, b, m, :]
                        vals, idx = sv[:, m, :], siu[:, m, :]
                        if b and m == 0:
                            dve.wait_ge(jch, 2 * p + 1)
                        top16(vals, idx, src)
                    link(V.tensor_copy(sif.rearrange("p m k -> p (m k)"), siu.rearrange("p m k -> p (m k)")))
                    svh = sv.rearrange("p (h c) k -> p h c k", c=2)
                    link(V.tensor_tensor(cand, svh[:, :, 0, :].unsqueeze(3).broadcast_to([P, PH, TOPK, TOPK]),
                                         svh[:, :, 1, :].unsqueeze(2).broadcast_to([P, PH, TOPK, TOPK]), ALU.add))
                    for h in range(PH):
                        top16(bs[:, h, :], biu[:, h, :], cand[:, h, :, :].rearrange("p a b -> p (a b)"))
                    link(V.tensor_copy(gsum, bs[:, :, 0]))
                    V.tensor_tensor(bs, bs, gsum.unsqueeze(2).broadcast_to([P, PH, TOPK]), ALU.subtract).then_inc(ex_v, 1)
                    did(V.tensor_scalar(ba.bitcast(U32), biu, 4, None, ALU.logical_shift_right))
                    link(V.tensor_scalar(bb.bitcast(U32), biu, TOPK - 1, None, ALU.bitwise_and))
                    did(V.tensor_copy(bf, bb.bitcast(U32)))
                    link(V.tensor_copy(af, ba.bitcast(U32)))
                    i16 = iota[:, 0:TOPK].unsqueeze(1).unsqueeze(1).broadcast_to([P, PH, TOPK, TOPK])
                    V.tensor_tensor(eqb, bf.unsqueeze(3).broadcast_to([P, PH, TOPK, TOPK]), i16, ALU.is_equal).then_inc(jon, 1)
                    link(V.tensor_tensor(eqa, af.unsqueeze(3).broadcast_to([P, PH, TOPK, TOPK]), i16, ALU.is_equal))
                    sih = sif.rearrange("p (h c) k -> p h c k", c=2)
                    link(V.tensor_tensor(eqa, eqa, sih[:, :, 0, :].unsqueeze(2).broadcast_to([P, PH, TOPK, TOPK]), ALU.mult))
                    did(V.tensor_reduce(ijt[:, 0, :].rearrange("p (h k) -> p h k", h=PH), eqa, AX.X, ALU.add))
                    dve.wait_ge(ex_a, 2 * p + b + 1)
                    link(V.tensor_reduce(gsum, bs, AX.X, ALU.add))
                    link(V.reciprocal(gsum, gsum))
                    did(V.tensor_tensor(ijt[:, 2, :].rearrange("p (h k) -> p h k", h=PH), bs, gsum.unsqueeze(2).broadcast_to([P, PH, TOPK]), ALU.mult))
                    dve.wait_ge(jon2, 2 * p + b + 1)
                    V.tensor_reduce(ijt[:, 1, :].rearrange("p (h k) -> p h k", h=PH), eqb, AX.X, ALU.add).then_inc(jch, 1)
                dve.wait_ge(ch_sb, 2 * p + 2)
                with dve.Fori(0, PT_ // 16) as n:
                    for q in range(2):
                        N = n + p * (PT_ // 16)
                        dve.wait_ge(g_pe[q], 1 + 2 * N)
                        for t in range(8):
                            i_t, j_t, w_t = (ijw[:, c, bass.ds(16 * n + (8 * q + t), 1)] for c in range(3))
                            V.tensor_scalar(onehots(u_raw, q)[:, t, :], iota, i_t, None, ALU.is_equal)
                            last = V.tensor_scalar(onehots(v_raw, q)[:, t, :], iota, j_t, w_t, ALU.is_equal, ALU.mult)
                        last.then_inc(onehot[q], 1)

                def low_u(q, N):
                    dve.wait_ge(u_h[q], N + 1)
                    V.tensor_tensor(u_lo[:, q, :], u_raw[:, q, :], u_hi[:, q, :], ALU.subtract).then_inc(u_l[q], 1)

                def step(j, q, N, nq, nN, more=True):
                    if more:
                        low_u(nq, nN)
                    dve.wait_ge(s_act[q], N + 1)
                    dve.wait_ge(p_l[q], 1 + N)
                    V.tensor_tensor(prod[:, q, :], act_s[:, q, :], gate[:, :, j] if isinstance(j, int) else gate[:, :, bass.ds(j, 1)].rearrange("p t o -> p (t o)"), ALU.mult).then_inc(p_do[q], 1)
                    dve.wait_ge(v_h[q], N + 1)
                    V.tensor_tensor(v_lo[:, q, :], v_raw[:, q, :], v_hi[:, q, :], ALU.subtract).then_inc(v_l[q], 1)
                    dve.wait_ge(p_h[q], N + 1)
                    V.tensor_tensor(p_lo[:, q, :], prod[:, q, :], p_hi[:, q, :], ALU.subtract).then_inc(p_l[q], 1)

                N0 = p * PAIRS
                for q in range(2):
                    dve.wait_ge(g_sb[q], 1 + 2 * (PT_ // 16) * (p + 1))
                low_u(0, N0)
                step(0, 0, N0, 1, N0)
                with dve.Fori(0, PAIRS - 1) as n:
                    step(2 * n + 1, 1, n + N0, 0, n + N0 + 1)
                    step(2 * n + 2, 0, n + N0 + 1, 1, n + N0 + 1)
                step(NK - 1, 1, N0 + PAIRS - 1, 0, 0, more=False)
                dve.wait_ge(y_ac[1], 1 + PAIRS * (p + 1))
                norms(LN_BASE[p], [2 * s, 2 * s + 1], 2, 16 * [7, 10, 16][p], 16 * [6, 8, 12][p], lambda b: s)

            peer(0)
            peer(1)
            dve.wait_ge(swa_c, 16)
            for i in range(10):
                if i < 8:
                    dst, lo = q1[:, i, :], 0
                else:
                    dst, lo = k1[:, i - 8, CTX:TOK], CTX
                raw = rawq[:, i % 2, lo:lo + SEQ]
                dve.wait_ge(qk_sb, i + 1)
                did(V.tensor_tensor(dst, raw, cos, ALU.mult))
                if i >= 8:
                    did(V.tensor_copy(k1[:, i - 8, 0:CTX], rawq[:, i % 2, 0:CTX]))
                dve.wait_ge(rot_pe, i + 1)
                link(V.tensor_tensor(rtmp[:, i % 2, 0:SEQ], banks[2 + i % 2][:, 0:SEQ], sin, ALU.mult))
                V.tensor_tensor(dst, dst, rtmp[:, i % 2, 0:SEQ], ALU.add).then_inc(rope, 1)

            def out_copy(i):
                j, half, b = i // 4, i % 2, (i // 2) % 2
                rows = slice(half * SWA_D, (half + 1) * SWA_D)
                dve.wait_ge(at_o, i + 1)
                V.tensor_copy(o1[rows, j, b * P:(b + 1) * P], banks[4 + i % 2][rows, 0:P]).then_inc(at_oc, 1)

            for i in range(32):
                j, half, b = i // 4, i % 2, (i // 2) % 2
                hq = (2 * (j // 4) + half) * 4 + j % 4
                st = stat[:, (i % 4) * 20:(i % 4) * 20 + 20]
                dve.wait_ge(at_s, i + 1)
                did(V.tensor_copy(st[:, 5:6], sink[:, hq:hq + 1]))
                link(V.reduce_max(st[:, 0:1], banks[i % 2][:, :], AX.X))
                link(V.tensor_scalar(st[:, 1:2], st[:, 0:1], SWA_SCALE, sink[:, hq:hq + 1], ALU.mult, ALU.max))
                V.tensor_scalar(st[:, 2:3], st[:, 1:2], -1.0, None, ALU.mult).then_inc(at_m, 1)
                if i >= 2:
                    out_copy(i - 2)
                dve.wait_ge(at_e, i + 1)
                link(V.tensor_tensor(st[:, 6:7], st[:, 3:4], st[:, 4:5], ALU.add))
                link(V.reciprocal(st[:, 7:8], st[:, 6:7]))
                if i >= 2:
                    dve.wait_ge(at_t, i - 1)
                V.tensor_scalar(diag[:, i % 2, :], ident, st[:, 7:8], None, ALU.mult).then_inc(at_d, 1)
            for i in (30, 31):
                out_copy(i)
            dve.wait_ge(y_pe, 12)
            norms(8, [2, 3], 0, 16 * 13, 16 * 10, lambda b: 1)
            peer(2)

        @block.gpsimd
        def _(pool):
            G = nc.gpsimd

            def norms(base, blocks):
                def shift(i):
                    pool.wait_ge(lnv, base + i + 1)
                    G.tensor_tensor(ln_x[:, blocks[i], :], ln_t[:, i % 2, :], ln_b, ALU.add).then_inc(ln_o, 1)

                for i in range(len(blocks)):
                    st = stat[:, (i % 4) * 20:(i % 4) * 20 + 20]
                    pool.wait_ge(ln_v, base + i + 1)
                    G.tensor_tensor(st[:, 14:15], st[:, 13:14], neg_half, ALU.pow).then_inc(ln_p, 1)
                    if i:
                        shift(i - 1)
                shift(len(blocks) - 1)

            pool.wait_ge(setup_v, 1)
            pool.wait_ge(ms_a, 1 + HEADS)
            ms = stat[:, 0:HEADS * NB]
            G.tensor_tensor(ms, ms, neg_half.broadcast_to([P, HEADS * NB]), ALU.pow).then_inc(rms_p, 1)
            norms(0, range(4))

            def peer(p):
                s = PASS_S[p]
                for b in range(2):
                    pool.wait_ge(jon, 2 * p + b + 1)
                    sih = sif.rearrange("p (h c) k -> p h c k", c=2)
                    G.tensor_tensor(eqb, eqb, sih[:, :, 1, :].unsqueeze(2).broadcast_to([P, PH, TOPK, TOPK]), ALU.mult).then_inc(jon2, 1)
                norms(LN_BASE[p], [2 * s, 2 * s + 1])

            peer(0)
            peer(1)
            norms(8, [2, 3])
            peer(2)


def constants():
    c = np.zeros((P, C_ALL), np.float32)
    c[:, C_ID:C_ID + P] = np.eye(P)
    c[:, C_IOTA:C_IOTA + P] = np.arange(P)
    c[:, C_ONE:C_ONE + P] = 1.0 / P
    rot = np.zeros((P, P), np.float32)
    for h in range(2):
        for ax in range(2):
            for f in range(16):
                x1 = h * 64 + ax * 32 + f
                rot[x1, x1 + 16] = -1.0
                rot[x1 + 16, x1] = 1.0
    c[:, C_ROT:C_ROT + P] = rot.T
    t = np.arange(SEQ)
    pos = np.stack([t // 64, t % 64]).astype(np.float32)
    inv = (np.float32(10000.0) ** (-np.arange(0, 32, 2, dtype=np.float32) / np.float32(32))).astype(np.float32)
    ang = pos[:, :, None] * inv
    for p in range(P):
        ax, f = (p % 64) // 32, p % 16
        c[p, C_COS:C_COS + SEQ] = np.cos(ang[ax, :, f])
        c[p, C_SIN:C_SIN + SEQ] = np.sin(ang[ax, :, f])
    q, k = np.arange(P)[:, None], np.arange(P)[None, :]
    c[:, C_MASK:C_MASK + P] = np.where(k <= q, 0.0, SCORE_MASK)
    c[:, C_MASK + P:C_MASK + 2 * P] = np.where(q <= k, 0.0, SCORE_MASK)
    m = np.zeros((P, LEVELS, P), np.float32)
    for l in range(1, LEVELS):
        h = 1 << (l - 1)
        m[:, l, :] = (q // (2 * h) == k // (2 * h)) & (q // h != k // h)
    return c, m.reshape(P, LEVELS * P)


def kernel(**inputs):
    import concourse.bacc as bacc
    from concourse.bass_utils import run_bass_kernel_spmd as run

    x = {k: np.ascontiguousarray(np.asarray(v)) for k, v in inputs.items()}

    def tiles(w, cols):
        n = w.shape[1] // cols
        return w.reshape(KT, P, n, cols).transpose(2, 1, 0, 3).reshape(n, P, KT * cols)

    qh = [(2 * (j // 4) + half) * 4 + j % 4 for j in range(8) for half in range(2)]
    qcols = np.concatenate([np.arange(64) + 64 * h for h in qh])
    swa = x["swa_w_in"][0]
    qkv = np.concatenate([swa[:, qcols], swa[:, 1024:]], axis=1)
    wst = np.concatenate(
        [tiles(x["mod_w"][l], WCOLS) for l in range(DEPTH)]
        + [tiles(x["hgrn_w_out"][0], WCOLS), tiles(x["peer_wq"][0], WCOLS), tiles(qkv, WCOLS),
           tiles(x["swa_w_out"][0][qcols], WCOLS), tiles(x["peer_wq"][1], WCOLS)])
    w5 = x["hgrn_w_in"][0].reshape(D, 5, HEADS, P)
    whd = tiles(w5[:, [0, 2, 3, 4, 1]].transpose(0, 2, 1, 3).reshape(D, HEADS * HCOLS), HCOLS)
    u = x["peer_u"].reshape(DEPTH, P, NK, KT, P).transpose(0, 2, 4, 3, 1).reshape(DEPTH, NK, P, D)
    v = x["peer_v"].reshape(DEPTH, P, NK, D).transpose(0, 2, 1, 3)
    keys = x["peer_keys"].transpose(0, 4, 1, 2, 3).reshape(DEPTH, P, 16 * NK)
    const, lvlmask = constants()
    arrays = {"x": x["x"], "ctx": x["ctx"], "c": x["c"], "c_ctx": x["c_ctx"], "mod_b": x["mod_b"], "ln_g": x["ln_g"],
              "ln_b": x["ln_b"], "lb": x["hgrn_lb_logits"], "ng": x["hgrn_norm_g"], "sink": x["swa_sink"][0],
              "wst": wst, "whd": whd, "u": u, "v": v, "keys": keys, "const": const, "lvlmask": lvlmask}
    arrays = {"in_" + k: np.ascontiguousarray(v) for k, v in arrays.items()}
    nc = bacc.Bacc("TRN2", target_bir_lowering=False, num_devices=1)
    args = {k[3:]: nc.dram_tensor(k, v.shape, mybir.dt.from_np(v.dtype), kind="ExternalInput").ap() for k, v in arrays.items()}
    args["out"] = nc.dram_tensor("out", (1, SEQ, D), F32, kind="ExternalOutput").ap()
    build(nc, args)
    r = run(nc, [arrays], core_ids=[0])
    return r.results[0]["out"]
```

```python
from contextlib import ExitStack

import numpy as np
import concourse.bass as bass
from concourse import mybir

F32 = mybir.dt.float32
F32R = mybir.dt.float32r
U32 = mybir.dt.uint32
U8 = mybir.dt.uint8
ALU = mybir.AluOpType
ACT = mybir.ActivationFunctionType
AX = mybir.AxisListType

P = 128
D = 1024
KT = D // P
SEQ = 256
CTX = 256
TOK = SEQ + CTX
NB = TOK // P
DEPTH = 2
ALPHA = (2 * DEPTH) ** 0.25
LN_EPS = 1e-5
RMS_EPS = 1e-6
HEADS = 8
LEVELS = 8
CHUNKS = 6
WCOLS = 512
MOD_TILES = DEPTH * CHUNKS * D // WCOLS
HCOLS = 5 * P
WSLOT = KT * HCOLS
SWA_Q, SWA_KV, SWA_D = 16, 4, 64
SWA_SCALE = SWA_D ** -0.5
PH = 8
TOPK = 16
ACT_T = 5
NK = 128
PT_ = 256
PASSES = 3
LOWEST = -3.4e38
SCORE_MASK = -1e30

C_ID, C_IOTA, C_ONE, C_ROT, C_COS, C_SIN, C_MASK = 0, 128, 256, 384, 512, 768, 1024
C_KEEP, C_ALL = 384, 1024 + 256


class Steps:

    def __init__(self, eng, sem):
        self.eng, self.sem, self.base, self.k = eng, sem, 0, 0

    def did(self, ins):
        ins.then_inc(self.sem, 1)
        self.k += 1

    def wait(self):
        self.eng.wait_ge(self.sem, self.base + self.k)

    def link(self, ins):
        self.did(ins)
        self.wait()

    def enter(self, i, per):
        self.start = self.base + self.k
        self.base, self.k, self.per = self.start + i * per, 0, per

    def leave(self, n):
        assert self.k == self.per, (self.k, self.per)
        self.base, self.k = self.start + n * self.per, 0


def build(nc, a):
    ctx = ExitStack()
    with ctx:
        def sem(name):
            return ctx.enter_context(nc.semaphore(name))

        def sb(name, shape, dt=F32):
            return ctx.enter_context(nc.sbuf_tensor(name, shape, dt))

        modd = nc.dram_tensor("mod_scratch", [2, DEPTH * CHUNKS * D], F32, kind="Internal").ap()
        xs = nc.dram_tensor("x_scratch", [NB, P, D], F32, kind="Internal").ap()

        arena = sb("arena", [P, 128 * PT_])
        const = sb("const", [P, 384])
        modcol = sb("modcol", [P, DEPTH, 96])
        small = sb("small", [P, 160])
        u_raw = sb("u_raw", [P, 2, D])
        v_raw = sb("v_raw", [P, 2, D])
        u_hi = sb("u_hi", [P, 2, D], F32R)
        u_lo = sb("u_lo", [P, 2, D], F32R)
        v_parts = sb("v_parts", [P, 4, D], F32R)
        v_hi, v_lo = v_parts[:, 0:2, :], v_parts[:, 2:4, :]
        h_parts = sb("h_parts", [P, 2, KT, PT_], F32R)
        h_hi, h_lo = h_parts[:, 0, :, :], h_parts[:, 1, :, :]
        act_s = sb("act_s", [P, 2, PT_])
        prod = sb("prod", [P, 2, PT_])
        p_hi = sb("p_hi", [P, 2, PT_], F32R)
        p_lo = sb("p_lo", [P, 2, PT_], F32R)
        ijw = sb("ijw", [P, 4, PT_])
        banks = [ctx.enter_context(nc.psum_tensor(f"bank{i}", [P, 512], F32)) for i in range(8)]

        def ar(off, size, **dims):
            v = arena[:, off:off + size]
            if dims:
                names = " ".join(dims)
                v = v.rearrange(f"p ({names}) -> p {names}", **dims)
            return v

        ident = const[:, C_ID:C_ID + P]
        iota = const[:, C_IOTA:C_IOTA + P]
        mean_w = const[:, C_ONE:C_ONE + P]
        lvlmask = prod[:, 0, :].bitcast(U8).rearrange("p (l t) -> p l t", l=LEVELS)
        sqbuf = act_s[:, :, :].rearrange("p a t -> p (a t)")

        W = [0, WSLOT]
        A_HT = 2 * WSLOT
        A_OT = A_HT + 4096
        A_HD = A_OT + 4096
        HD = 6144
        A_KT = A_HD + 2 * HD
        A_ST = A_KT + 768
        assert A_ST + 768 <= 128 * PT_
        hT = ar(A_HT, 4096, k=KT, t=TOK)
        hT_hi = h_parts
        hT_lo = v_parts.rearrange("p (s x) (k t) -> p s (x k) t", s=2, t=PT_)
        oT = ar(A_OT, 4096, k=KT, t=TOK)
        xtok = ar(A_HD, 4096, b=NB, d=D)
        A_LN = A_HD + 1024
        ln_x = ar(A_LN, 4096, b=NB, d=D)
        ln_t = ar(A_LN + 4096, 4096, s=4, d=D)
        ln_m = ar(A_LN + 8192, 2048, s=2, d=D)
        ln_g = ar(A_LN + 10240, 1024)
        ln_b = ar(A_LN + 11264, 1024)

        cond = small[:, 0:16].rearrange("p (s k) -> p s k", s=2)
        lb = small[:, 16:24]
        omlb = small[:, 24:32]
        ng = small[:, 32:33]
        lgt = small[:, 33:57].rearrange("p (r h) -> p r h", r=3)
        sink = small[:, 57:73]
        stat = small[:, 73:153]
        neg_half = small[:, 153:154]

        const_in = sem("const_in")
        cond_in = sem("cond_in")
        lvlmask_in = sem("lvlmask_in")
        bias_in = sem("bias_in")
        w_loaded = [sem(f"w_loaded{i}") for i in range(2)]
        setup_t = sem("setup_transposed")
        setup_a = sem("setup_act")
        setup_v = sem("setup_vector")
        cond_done = sem("cond_done")
        mod_pe = [sem(f"mod_product{i}") for i in range(2)]
        mod_v = [sem(f"mod_biased{i}") for i in range(2)]
        mod_out = sem("mod_stored")
        mod_back = sem("mod_reloaded")
        mod_t = sem("mod_transposed")
        mod_c = sem("mod_columns")
        x_in = sem("x_loaded")
        xT_pe = sem("x_transposed")
        hT_done = sem("hT_ready")
        hT_h = sem("hT_high")
        hT_l = sem("hT_low")
        hw_h = sem("head_weights_high")
        hw_l = sem("head_weights_low")
        proj = sem("head_projected")
        vproj = sem("head_values_projected")
        sig = sem("head_sigmoids")
        vsb = sem("head_values_copied")
        init = sem("head_scaled")
        lvl = sem("level_products")
        lvlcp = sem("level_copied_out")
        upd = sem("level_decays_applied")
        kc_sb = sem("level_keys_ready")
        kt_pe = sem("keys_transposed")
        kt_sb = sem("keys_copied")
        ds = sem("state_products")
        st_done = sem("states_ready")
        o_pe = sem("head_output")
        sq_done = sem("head_squares")
        ss_pe = sem("head_square_sums")
        ms_a = sem("head_mean_squares")
        rms_p = sem("head_scales")
        y_done = sem("head_finished")
        rdiag = sem("head_scale_diagonals")
        rbc = sem("head_scales_spread")
        onorm = sem("head_normalised")
        ln_in = sem("ln_rows_loaded")
        ln_res = sem("ln_residual_loaded")
        y_pe = sem("mixer_output")
        y_used = sem("mixer_output_used")
        ln_v = sem("ln_variances")
        ln_p = sem("ln_scales")
        ln_r = sem("ln_statistics")
        ln_n = sem("ln_normalised")
        ln_o = sem("ln_finished")
        x_out = sem("x_stored")
        x1T = sem("tokens_transposed")
        h1 = sem("tokens_modulated")
        hh = sem("tokens_high_part")
        hl = sem("tokens_low_part")
        keys_in = sem("keys_loaded")
        qw_h = [sem(f"query_weights_high{i}") for i in range(4)]
        qw_l = [sem(f"query_weights_low{i}") for i in range(4)]
        qw_pe = [sem(f"query_products{i}") for i in range(4)]
        pq_sb = sem("queries_copied")
        ps_pe = sem("score_products")
        ps_sb = sem("scores_copied")
        jch = sem("choices_made")
        jon = sem("column_numbers_ready")
        ex_v = sem("gate_shifted")
        ex_a = sem("gate_exponentials")
        ch_t = sem("choices_transposed")
        ch_sb = sem("choices_copied")
        onehot = [sem(f"onehots{i}") for i in range(2)]
        coleq = [sem(f"column_onehots{i}") for i in range(2)]
        colw = [sem(f"columns_weighed{i}") for i in range(2)]
        g_pe = [sem(f"gate_products{i}") for i in range(2)]
        g_sb = [sem(f"gates_stored{i}") for i in range(2)]
        u_in = [sem(f"u_loaded{i}") for i in range(2)]
        v_in = [sem(f"v_loaded{i}") for i in range(2)]
        u_h = [sem(f"u_high{i}") for i in range(2)]
        u_l = [sem(f"u_low{i}") for i in range(2)]
        v_h = [sem(f"v_high{i}") for i in range(2)]
        v_l = [sem(f"v_low{i}") for i in range(2)]
        s_pe = [sem(f"expert_scores{i}") for i in range(2)]
        s_act = [sem(f"expert_gelus{i}") for i in range(2)]
        p_do = [sem(f"expert_weights{i}") for i in range(2)]
        p_h = [sem(f"weights_high{i}") for i in range(2)]
        p_l = [sem(f"weights_low{i}") for i in range(2)]
        y_ac = [sem(f"expert_outputs{i}") for i in range(2)]
        qk_pe = sem("swa_projected")
        qk_sb = sem("swa_copied")
        rot_pe = sem("swa_rotated")
        rope = sem("swa_roped")
        sv_pe = sem("swa_values_projected")
        sv_sb = sem("swa_values_copied")
        at_s = sem("swa_scores")
        at_m = sem("swa_maxima")
        at_e = sem("swa_exponentials")
        at_d = sem("swa_diagonals")
        at_t = sem("swa_probs_transposed")
        at_tc = sem("swa_probs_copied")
        at_o = sem("swa_outputs")
        at_oc = sem("swa_outputs_copied")
        swa_c = sem("swa_constants_loaded")
        lnv = sem("ln_scaled")
        jon2 = sem("column_numbers_masked")
        dstep = sem("vector_steps")

        B_HF = 2 * WSLOT
        B_K = B_HF + 2048
        B_Q = B_K + 2048
        B_S = B_Q + 1024
        B_C = B_S + 4096
        B_E = B_C + 2048
        B_F = B_E + 2048
        B_R = B_F + 2048
        assert B_R + 3328 <= 128 * PT_
        hf = ar(B_HF, 2048, k=KT, t=PT_)
        qp = ar(B_Q, 1024, c=4, t=PT_)
        sc = ar(B_S, 4096, b=2, m=16, n=NK)
        kp = ar(B_K, 2048, m=16, n=NK)
        cand = ar(B_C, 1024, c=2, h=2, a=TOPK, b=TOPK)
        eqa = ar(B_E, 2048, h=PH, k=TOPK, a=TOPK)
        eqb = ar(B_F, 2048, h=PH, k=TOPK, a=TOPK)
        sv = ar(B_R + 2048, 512, b=2, m=16, k=TOPK)
        si = ar(B_R + 2560, 512, b=2, m=16, k=TOPK)
        sif = ar(B_R + 512, 256, m=16, k=TOPK)
        bs = ar(B_R + 768, 256, b=2, h=PH, k=TOPK)
        bi = ar(B_R + 3072, 256, b=2, h=PH, k=TOPK)
        ba = ar(B_R + 1024, 128, h=PH, k=TOPK)
        bb = ar(B_R + 1152, 128, h=PH, k=TOPK)
        af = ar(B_R + 1280, 128, h=PH, k=TOPK)
        bf = ar(B_R + 1408, 128, h=PH, k=TOPK)
        ijt = ar(B_R + 1536, 384, c=3, m=128)
        gsums = ar(B_R + 1920, 16, b=2, h=PH)
        gate = arena[:, :].rearrange("p (t j) -> p t j", j=NK)

        def weight_parts(m):
            return [(u, v)[m // 2][:, m % 2, :].rearrange("p (k n) -> p k n", k=KT) for u, v in ((u_hi, v_hi), (u_lo, v_lo))]


        T_WOUT0, T_WQ0, T_QKV, T_WOUT1, T_WQ1 = MOD_TILES, MOD_TILES + 2, MOD_TILES + 6, MOD_TILES + 9, MOD_TILES + 11

        def wt(slot):
            return ar(W[slot], KT * WCOLS, k=KT, n=WCOLS)

        def wh(slot):
            return ar(W[slot], WSLOT, k=KT, n=HCOLS)

        ORDER = ([("loop", i) for i in range(MOD_TILES)] + [("head", i) for i in range(HEADS)]
                 + [("wout0", i) for i in range(2)] + [("wqa", i) for i in range(4)] + [("wqb", i) for i in range(4)]
                 + [("qkv", i) for i in range(3)] + [("wout1", i) for i in range(2)] + [("wqc", i) for i in range(4)])
        RING = {n: k for k, n in enumerate(ORDER)}
        SRC = {"wout0": T_WOUT0, "wqa": T_WQ0, "wqb": T_WQ0, "qkv": T_QKV, "wout1": T_WOUT1, "wqc": T_WQ1}


        def onehots(buf, slot):
            return buf[:, slot, :].rearrange("p (t j) -> p t j", t=8)

        A_MOD = 2 * WSLOT
        MODN = DEPTH * CHUNKS * D
        modsb = arena[0:2, A_MOD:A_MOD + MODN]
        A_RAW = A_MOD + MODN
        modraw = arena[0:96, A_RAW:A_RAW + 256].rearrange("p (l d) -> p l d", l=DEPTH)
        condraw = arena[0:16, A_RAW + 256:A_RAW + 384]
        lbraw = arena[0:24, A_RAW + 384:A_RAW + 512]

        lvlraw = ar(A_RAW + 512, LEVELS * P)

        def mcol(layer, s, chunk, k):
            n = s * 48 + chunk * KT + k
            return modcol[:, layer, n:n + 1]

        def hd(slot, off, n):
            return arena[:, A_HD + slot * HD + off:A_HD + slot * HD + off + n]

        O_Q, O_QD, O_KD, O_C, O_G, O_V, O_AT = 0, 512, 1536, 2560, 4608, 5120, 5632

        def coff(k):
            return O_C + 2048 - (2048 >> k)

        def hap(slot, off, *dims):
            return bass.AP(tensor=arena[:, 0:1].tensor, offset=A_HD + slot * HD + off,
                           ap=[[128 * PT_, P]] + [list(d) for d in dims])

        def level_operand(slot, off, m, blk):
            return hap(slot, off + blk * P, (2 * m, P // (2 * m)), (TOK + m, 2), (1, m))

        def rmsdiag(h):
            return u_raw[:, h % 2, 0:TOK]

        kc = ijw[:, :, :].rearrange("p (s a) t -> p s (a t)", s=2)
        KTr = ar(A_KT, 768, c=6, k=P)
        STr = ar(A_ST, 768, c=6, k=P)
        FW, BW = [0, 1, 2], [1, 0, 3]
        CHAIN = FW + BW

        A_Q1 = A_OT + 2048
        A_K1 = A_HD + 4096
        q1 = ar(A_Q1, 2048, j=8, t=SEQ)
        k1 = ar(A_K1, 1024, j=2, t=TOK)
        v1 = ar(A_K1 + 1024, 1024, b=NB, c=256)
        c1 = ar(A_K1 + 2048, C_ALL - C_KEEP)
        o1 = ar(A_OT, 2048, j=8, t=SEQ)
        rawq = ar(A_K1 + 2048 + 1024, 1024, s=2, t=512)
        rtmp = ar(A_K1 + 2048 + 2048, 1024, s=2, t=512)
        prb = ar(A_K1 + 2048 + 1024, 1024, s=2, t=512)
        prT = ar(A_K1 + 2048 + 2048, 1024, s=2, t=512)
        diag = ar(A_K1 + 2048 + 3072, 256, s=2, t=P)
        assert A_K1 + 2048 + 3072 + 256 <= 128 * PT_
        rot = c1[:, C_ROT - C_KEEP:C_ROT - C_KEEP + P]
        cos = c1[:, C_COS - C_KEEP:C_COS - C_KEEP + SEQ]
        sin = c1[:, C_SIN - C_KEEP:C_SIN - C_KEEP + SEQ]
        wmask = c1[:, C_MASK - C_KEEP:C_MASK - C_KEEP + 256].rearrange("p (b k) -> p b k", b=2)

        assert B_C == A_LN
        PASS_LAYER = [0, 0, 1]
        PASS_S = [0, 1, 1]
        LN_BASE = [4, 6, 10]
        LN1_BASE = [0, 8]
        PAIRS = NK // 2

        ON_PE = [*mod_pe, lvl, ds, ss_pe, o_pe, *g_pe, *y_ac]
        ON_ACT = [*g_sb, ms_a]
        ON_DVE = [*mod_v, *u_l, *v_l, *p_l, *p_do]

        def in_hand(eng, sems):
            for x in sems:
                eng.sem_inc(x, 1)

        block = ctx.enter_context(nc.Block())

        @block.sync
        def _(sp):
            def tile(name, i):
                k = RING[(name, i)]
                s = k % 2
                was, at = ORDER[k - 2]
                if was == "head":
                    sp.wait_ge(vproj, at + 1)
                elif was in ("wout0", "wout1"):
                    sp.wait_ge(y_pe, 4 * (at + 1) if was == "wout0" else 8 + 2 * (at + 1))
                elif was == "qkv":
                    sp.wait_ge(qk_pe if at < 2 else sv_pe, 4 * (at + 1) if at < 2 else 4)
                else:
                    sp.wait_ge(qw_l[3], 4 * ["wqa", "wqb", "wqc"].index(was) + at + 1)
                sp.dma_start(ar(W[s], KT * WCOLS), a["wst"][SRC[name] + i]).then_inc(w_loaded[s], 16)

            sp.dma_start(const[:, :], a["const"][:, 0:C_KEEP]).then_inc(const_in, 16)
            sp.dma_start(condraw[0:8, :], a["c_ctx"].rearrange("(k d) -> k d", d=P)).then_inc(cond_in, 16)
            sp.dma_start(condraw[8:16, :], a["c"].rearrange("o (k d) -> (o k) d", d=P)).then_inc(cond_in, 16)
            sp.dma_start(lbraw[:, :], a["lb"].rearrange("r (h d) -> (r h) d", d=P)).then_inc(cond_in, 16)
            sp.dma_start(ng, a["ng"].rearrange("o d -> d o")).then_inc(cond_in, 16)
            sp.dma_start(sink, a["sink"].partition_broadcast(P)).then_inc(cond_in, 16)
            sp.dma_start(lvlraw, a["lvlmask"]).then_inc(lvlmask_in, 16)
            for s in range(2):
                sp.dma_start(modsb[s:s + 1, :], a["mod_b"].rearrange("(o l) n -> o (l n)", o=1)).then_inc(bias_in, 16)
            with sp.Fori(0, MOD_TILES // 2) as n:
                for s in range(2):
                    sp.wait_ge(mod_pe[s], 1 + n)
                    sp.dma_start(ar(W[s], KT * WCOLS), a["wst"][2 * n + s]).then_inc(w_loaded[s], 16)
            MT = MOD_TILES // 2
            for s in range(2):
                sp.wait_ge(mod_pe[s], 1 + MT)
                sp.dma_start(ar(W[s], WSLOT), a["whd"][s]).then_inc(w_loaded[s], 16)
            for s in range(2):
                sp.wait_ge(mod_v[s], 1 + MT)
            sp.dma_start(modd[:, :], modsb[:, :]).then_inc(mod_out, 16)
            sp.wait_ge(mod_out, 16)
            rows = modd.rearrange("s (l r d) -> s l r d", l=DEPTH, d=P)
            for l in range(DEPTH):
                for s in range(2):
                    sp.dma_start(modraw[s * 48:s * 48 + 48, l, :], rows[s, l]).then_inc(mod_back, 16)
            for b in range(2):
                sp.dma_start(xtok[:, b, :], a["ctx"][0, b * P:b * P + P, :]).then_inc(x_in, 16)
                sp.dma_start(xtok[:, 2 + b, :], a["x"][0, b * P:b * P + P, :]).then_inc(x_in, 16)
            with sp.Fori(1, HEADS // 2) as n:
                for s in range(2):
                    sp.wait_ge(vproj, 2 * n + (s - 1))
                    sp.dma_start(ar(W[s], WSLOT), a["whd"][2 * n + s]).then_inc(w_loaded[s], 16)

            def ln_rows(layer, which, streams, base, blocks, src):
                sp.dma_start(ln_g, a["ln_g"][layer, which].partition_broadcast(P)).then_inc(ln_in, 16)
                sp.dma_start(ln_b, a["ln_b"][layer, which].partition_broadcast(P)).then_inc(ln_in, 16)
                chunk = 2 if which == 0 else 5
                at = (layer * CHUNKS + chunk) * D
                for s in streams:
                    sp.dma_start(ln_m[:, s, :], modd[s, at:at + D].partition_broadcast(P)).then_inc(ln_in, 16)
                for b in blocks:
                    sp.dma_start(ln_x[:, b, :], src(b)).then_inc(ln_res, 16)

            def peer_first(p):
                if p == 1:
                    for b in range(2, 4):
                        sp.dma_start(ln_x[:, b, :], xs[b]).then_inc(x_in, 16)
                for i in range(2):
                    tile(["wqa", "wqb", "wqc"][p], i)
                sp.dma_start(kp.rearrange("p m n -> p (m n)"), a["keys"][PASS_LAYER[p]]).then_inc(keys_in, 16)

            def ln_store(base, blocks, dst):
                for k, b in enumerate(blocks):
                    sp.wait_ge(ln_o, base + k + 1)
                    sp.dma_start(dst(b), ln_x[:, b, :]).then_inc(x_out, 16)

            def x_of(b):
                return a["ctx"][0, b * P:b * P + P, :] if b < 2 else a["x"][0, (b - 2) * P:(b - 1) * P, :]

            def peer(p):
                layer, s = PASS_LAYER[p], PASS_S[p]
                blocks = [2 * s, 2 * s + 1]
                names = ["wqa", "wqb", "wqc"][p]
                for i in range(2, 4):
                    tile(names, i)
                for q in range(2):
                    sp.wait_ge(g_pe[q], 1 + 2 * (PT_ // 16) * (p + 1))
                with sp.Fori(0, PAIRS) as n:
                    for q in range(2):
                        j = 2 * n + q
                        sp.wait_ge(u_l[q], 1 + n + p * PAIRS)
                        sp.dma_start(u_raw[:, q, :], a["u"][layer, j]).then_inc(u_in[q], 16)
                        sp.wait_ge(v_l[q], 1 + n + p * PAIRS)
                        sp.dma_start(v_raw[:, q, :], a["v"][layer, j]).then_inc(v_in[q], 16)
                sp.wait_ge(y_ac[1], 1 + PAIRS * (p + 1))
                sp.wait_ge(x_out, 16 * LN_BASE[p])
                ln_rows(layer, 1, [s], LN_BASE[p], blocks, lambda b: xs[b])
                if p == 0:
                    peer_first(1)
                if p == 1:
                    for b in range(2):
                        sp.dma_start(ln_x[:, b, :], xs[b]).then_inc(x_in, 16)
                    for i in range(2):
                        tile("qkv", i)
                if p < 2:
                    ln_store(LN_BASE[p], blocks, lambda b: xs[b])
                else:
                    ln_store(LN_BASE[p], blocks, lambda b: a["out"][0, (b - 2) * P:(b - 1) * P, :])

            for i in range(2):
                tile("wout0", i)
            sp.wait_ge(y_done, 1 + HEADS)
            ln_rows(0, 0, [0, 1], 0, range(4), x_of)
            peer_first(0)
            ln_store(0, range(4), lambda b: xs[b])
            peer(0)
            peer(1)
            sp.dma_start(c1, a["const"][:, C_KEEP:C_ALL]).then_inc(swa_c, 16)
            tile("qkv", 2)
            for i in range(2):
                tile("wout1", i)
            sp.wait_ge(at_oc, 32)
            ln_rows(1, 0, [1], 8, [2, 3], lambda b: xs[b])
            peer_first(2)
            ln_store(8, [2, 3], lambda b: xs[b])
            peer(2)
            sp.wait_ge(x_out, 16 * 12)

        @block.tensor
        def _(pe):
            mm = nc.tensor.matmul
            in_hand(pe, ON_PE)

            def arrived(name, i):
                k = RING[(name, i)]
                pe.wait_ge(w_loaded[k % 2], 16 * (k // 2 + 1))
                return k % 2

            pe.wait_ge(const_in, 16)
            pe.wait_ge(cond_in, 80)
            nc.tensor.transpose(banks[2][:, 0:16], condraw, ident[0:16, 0:16])
            nc.tensor.transpose(banks[3][:, 0:24], lbraw, ident[0:24, 0:24]).then_inc(setup_t, 1)
            pe.wait_ge(cond_done, 1)
            with pe.Fori(0, MOD_TILES // 2) as n:
                for s in range(2):
                    pe.wait_ge(w_loaded[s], 16 * n + 16)
                    pe.wait_ge(mod_v[s], 1 + n)
                    for k in range(KT):
                        last = mm(banks[s][0:2, :], cond[:, :, k], wt(s)[:, k, :], start=(k == 0), stop=(k == KT - 1))
                    last.then_inc(mod_pe[s], 1)
            pe.wait_ge(mod_back, 64)
            for l in range(DEPTH):
                last = nc.tensor.transpose(banks[2 + l][:, 0:96], modraw[:, l, :], ident[0:96, 0:96])
            last.then_inc(mod_t, 1)

            def transpose_x(layer, need, src):
                pe.wait_ge(x_in, need)
                for k in range(KT):
                    if k >= 2:
                        pe.wait_ge(hT_done, 2 * (8 * layer + k - 1))
                    for b in range(NB):
                        last = nc.tensor.transpose(banks[k % 2][:, b * P:(b + 1) * P], src[:, b, k * P:(k + 1) * P], ident)
                    last.then_inc(xT_pe, 1)
                pe.wait_ge(hT_done, 16 * (layer + 1))

            transpose_x(0, 64, xtok)

            MT = MOD_TILES // 2

            def proj_piece(g, c, half):
                w_hi, w_lo = weight_parts(c % 2)
                if half == 0:
                    pe.wait_ge(hw_l, 4 * g + (c + 1))
                out = banks[c][:, :].rearrange("p (s t) -> p s t", s=2)
                for k in range(4 * half, 4 * half + 4):
                    for i, (w, x) in enumerate(((w_hi, hT_hi[:, :, k, :]), (w_hi, hT_lo[:, :, k, :]), (w_lo, hT_hi[:, :, k, :]))):
                        last = mm(out, w[:, k, :], x, start=(k == 0 and i == 0), stop=(k == KT - 1 and i == 2))
                if half:
                    last.then_inc(proj, 1)

            def value_piece(slot, b, final):
                for k in range(KT):
                    last = mm(banks[7][:, b * P:(b + 1) * P], hT[:, k, b * P:(b + 1) * P], wh(slot)[:, k, 4 * P:5 * P],
                              start=(k == 0), stop=(k == KT - 1))
                if final:
                    last.then_inc(vproj, 1)

            pe.wait_ge(hT_l, KT)
            for c in range(4):
                for half in range(2):
                    proj_piece(0, c, half)
            for b in range(NB):
                value_piece(0, b, b == NB - 1)

            def head(h, slot, more):
                for l in range(LEVELS):
                    if l == 0:
                        pe.wait_ge(init, h + 1)
                    if more:
                        proj_piece(h + 1, l // 2, l % 2)
                    if l == 0:
                        pe.wait_ge(y_done, h + 1)
                    if l == 1:
                        pe.wait_ge(ms_a, 1 + h)
                    if l >= 2:
                        pe.wait_ge(lvlcp, 8 * h + l - 1)
                    bank = banks[4 + l % 2]
                    for b in range(NB):
                        out = bank[:, b * P:(b + 1) * P]
                        if l == 0:
                            qb = hd(slot, O_Q + b * P, P)
                            mm(out, hd(slot, O_KD + b * P, P), qb, start=True, stop=False)
                            last = mm(out, hd(slot, O_KD + TOK + b * P, P), qb, start=False, stop=True)
                        else:
                            m = 1 << (l - 1)
                            if b == 0:
                                pe.wait_ge(kc_sb, 7 * h + l)
                            last = mm(out, kc[:, l % 2, b * P:(b + 1) * P], level_operand(slot, O_QD, m, b), start=True, stop=True)
                    last.then_inc(lvl, 1)
                pe.wait_ge(upd, 7 * h + 7)
                for d in range(2):
                    if d:
                        pe.wait_ge(lvlcp, 8 * h + 7)
                    for i in range(3):
                        b = CHAIN[3 * d + i]
                        last = nc.tensor.transpose(banks[6 - 2 * d][:, i * P:(i + 1) * P], hd(slot, O_KD + d * TOK + b * P, P), ident)
                    last.then_inc(kt_pe, 1)
                if more:
                    value_piece(1 - slot, 0, False)
                for d in range(2):
                    pe.wait_ge(kt_sb, 2 * h + d + 1)
                    if d == 0:
                        pe.wait_ge(lvlcp, 8 * h + 8)
                        pe.wait_ge(vsb, h + 1)
                    for i in range(3):
                        b = CHAIN[3 * d + i]
                        last = mm(banks[5 + d][:, i * P:(i + 1) * P], KTr[:, 3 * d + i, :], hd(slot, O_V + b * P, P), start=True, stop=True)
                    last.then_inc(ds, 1)
                    if more:
                        value_piece(1 - slot, 1 + d, False)
                for b in range(NB):
                    out = banks[4][:, b * P:(b + 1) * P]
                    terms = [(hd(slot, O_V + b * P, P), hd(slot, O_AT + b * P, P))]
                    if b:
                        terms.append((STr[:, b - 1, :], hd(slot, O_QD + TOK + b * P, P)))
                    if b != 1:
                        terms.append((STr[:, {0: 3, 3: 4, 2: 5}[b], :], hd(slot, O_QD + b * P, P)))
                    if b == 0:
                        pe.wait_ge(st_done, h + 1)
                    for i, (x, y) in enumerate(terms):
                        last = mm(out, x, y, start=(i == 0), stop=(i == len(terms) - 1))
                last.then_inc(o_pe, 1)
                if more:
                    value_piece(1 - slot, 3, True)
                pe.wait_ge(sq_done, h + 1)
                for b in range(NB):
                    last = mm(banks[5][:, b:b + 1], sqbuf[:, b * P:(b + 1) * P], mean_w[:, 0:1], start=True, stop=True)
                last.then_inc(ss_pe, 1)

            with pe.Fori(0, HEADS // 2 - 1) as n:
                head(2 * n, 0, True)
                head(2 * n + 1, 1, True)
            head(HEADS - 2, 0, True)
            head(HEADS - 1, 1, False)

            def mixer_out(name, oview, blocks, bank0):
                for half in range(2):
                    s = arrived(name, half)
                    for i, b in enumerate(blocks):
                        for k in range(KT):
                            last = mm(banks[bank0 + 2 * i + half][:, :], oview[:, k, b * P:(b + 1) * P], wt(s)[:, k, :],
                                      start=(k == 0), stop=(k == KT - 1))
                        last.then_inc(y_pe, 1)

            for h in range(HEADS):
                pe.wait_ge(rdiag, h + 1)
                mm(banks[h % 4][:, :], mean_w, rmsdiag(h), start=True, stop=True).then_inc(rbc, 1)
            pe.wait_ge(onorm, HEADS)
            mixer_out("wout0", oT, range(4), 0)

            def peer(p):
                layer, s = PASS_LAYER[p], PASS_S[p]
                if p == 1:
                    pe.wait_ge(x_in, 64 + 32)
                else:
                    pe.wait_ge(ln_o, LN_BASE[p])
                for k in range(KT):
                    if k >= 2:
                        pe.wait_ge(h1, 8 * p + k - 1)
                    for b in range(2):
                        last = nc.tensor.transpose(banks[k % 2][:, b * P:(b + 1) * P], ln_x[:, 2 * s + b, k * P:(k + 1) * P], ident)
                    last.then_inc(x1T, 1)
                pe.wait_ge(h1, 8 * p + 8)
                pe.wait_ge(hl, 8 * (p + 1))

                def query_unit(g):
                    i, m = g // 4, g % 4
                    if m == 0 and i == 1:
                        pe.wait_ge(ln_v, LN_BASE[p])
                    if m == 0 and i >= 2:
                        pe.wait_ge(pq_sb, 4 * p + i - 1)
                    pe.wait_ge(qw_l[m], 4 * p + i + 1)
                    w_hi, w_lo = weight_parts(m)
                    out = banks[(6 if i % 2 == 0 else 2) + m // 2][:, (m % 2) * PT_:(m % 2 + 1) * PT_]
                    n3 = 0
                    for k in range(KT):
                        for w, h in ((w_hi, h_hi), (w_hi, h_lo), (w_lo, h_hi)):
                            last = mm(out, w[:, k, :], h[:, k, :], start=(n3 == 0), stop=(n3 == 3 * KT - 1))
                            n3 += 1
                    last.then_inc(qw_pe[m], 1)

                def key_scores(i):
                    if i == 0:
                        pe.wait_ge(keys_in, 16 * (p + 1))
                    pe.wait_ge(pq_sb, 4 * p + i + 1)
                    for b in range(2):
                        if i:
                            pe.wait_ge(ps_sb, 2 * (4 * p + i - 1) + b + 1)
                        for m in range(4):
                            last = mm(banks[4 + b][:, m * NK:(m + 1) * NK], qp[:, m, b * P:(b + 1) * P], kp[:, 4 * i + m, :],
                                      start=True, stop=True)
                        last.then_inc(ps_pe, 1)

                for g in range(16):
                    query_unit(g)
                    if g % 4 == 0 and g:
                        key_scores(g // 4 - 1)
                key_scores(3)
                for b in range(2):
                    pe.wait_ge(jch, 2 * p + b + 1)
                    for c in range(3):
                        last = nc.tensor.transpose(banks[6 + b][:, c * P:(c + 1) * P], ijt[:, c, :], ident)
                    last.then_inc(ch_t, 1)
                with pe.Fori(0, PT_ // 16) as n:
                    for q in range(2):
                        N = n + p * (PT_ // 16)
                        pe.wait_ge(onehot[q], N + 1)
                        pe.wait_ge(colw[q], N + 1)
                        pe.wait_ge(g_sb[q], 1 + 2 * N)
                        for half in range(2):
                            for t in range(4 * half, 4 * half + 4):
                                out = banks[2 * q + half][:, (t % 4) * NK:(t % 4 + 1) * NK]
                                last = mm(out, onehots(u_raw, q)[:, t, :], onehots(v_raw, q)[:, t, :], start=True, stop=True)
                            last.then_inc(g_pe[q], 1)

                def scores(q, N):
                    pe.wait_ge(u_l[q], 1 + N + 1)
                    pe.wait_ge(s_act[q], N)
                    n3 = 0
                    for k in range(KT):
                        col = slice(k * P, (k + 1) * P)
                        for w, h in ((u_hi, h_hi), (u_hi, h_lo), (u_lo, h_hi)):
                            last = mm(banks[q][:, 0:PT_], w[:, q, col], h[:, k, :], start=(n3 == 0), stop=(n3 == 3 * KT - 1))
                            n3 += 1
                    last.then_inc(s_pe[q], 1)

                def outputs(q, N, first, final):
                    pe.wait_ge(p_l[q], 1 + N + 1)
                    pe.wait_ge(v_l[q], 1 + N + 1)
                    for b in range(2):
                        for half in range(2):
                            col = slice(half * 512, half * 512 + 512)
                            for i, (x, y) in enumerate(((p_hi, v_hi), (p_hi, v_lo), (p_lo, v_hi))):
                                last = mm(banks[2 + 2 * b + half][:, :], x[:, q, b * P:(b + 1) * P], y[:, q, col],
                                          start=(first and i == 0), stop=(final and i == 2))
                    last.then_inc(y_ac[q], 1)

                N0 = p * PAIRS
                scores(0, N0)
                pe.wait_ge(g_sb[1], 1 + 2 * (PT_ // 16) * (p + 1))
                scores(1, N0)
                outputs(0, N0, True, False)
                with pe.Fori(0, PAIRS - 1) as n:
                    scores(0, n + N0 + 1)
                    outputs(1, n + N0, False, False)
                    scores(1, n + N0 + 1)
                    outputs(0, n + N0 + 1, False, False)
                outputs(1, N0 + PAIRS - 1, False, True)

            peer(0)
            peer(1)
            pe.wait_ge(ln_o, 8)
            transpose_x(1, 64 + 32 + 32, ln_x)

            n_qk = 0
            for i in range(2):
                w = arrived("qkv", i)
                for m in range(4):
                    if n_qk >= 2:
                        pe.wait_ge(rope, n_qk - 1)
                    for k in range(KT):
                        last = mm(banks[n_qk % 2][:, 0:SEQ], wt(w)[:, k, m * P:(m + 1) * P], hT[:, k, CTX:TOK],
                                  start=(k == 0), stop=(k == KT - 1))
                    last.then_inc(qk_pe, 1)
                    pe.wait_ge(qk_sb, n_qk + 1)
                    if n_qk == 0:
                        pe.wait_ge(swa_c, 16)
                    mm(banks[2 + n_qk % 2][:, 0:SEQ], rot, rawq[:, n_qk % 2, 0:SEQ], start=True, stop=True).then_inc(rot_pe, 1)
                    n_qk += 1
            w = arrived("qkv", 2)
            for m in range(2):
                pe.wait_ge(rope, n_qk - 1)
                for k in range(KT):
                    last = mm(banks[n_qk % 2][:, :], wt(w)[:, k, m * P:(m + 1) * P], hT[:, k, :], start=(k == 0), stop=(k == KT - 1))
                last.then_inc(qk_pe, 1)
                pe.wait_ge(qk_sb, n_qk + 1)
                mm(banks[2 + n_qk % 2][:, 0:SEQ], rot, rawq[:, n_qk % 2, CTX:TOK], start=True, stop=True).then_inc(rot_pe, 1)
                n_qk += 1
            for b in range(NB):
                for k in range(KT):
                    last = mm(banks[4 + b // 2][:, (b % 2) * 256:(b % 2 + 1) * 256], hT[:, k, b * P:(b + 1) * P], wt(w)[:, k, 256:512],
                              start=(k == 0), stop=(k == KT - 1))
                last.then_inc(sv_pe, 1)
            pe.wait_ge(rope, 10)
            pe.wait_ge(sv_sb, 1)

            def att_scores(i):
                j, half, b = i // 4, i % 2, (i // 2) % 2
                bank = banks[i % 2]
                rows = slice(half * SWA_D, (half + 1) * SWA_D)
                if i >= 2:
                    pe.wait_ge(at_e, i - 1)
                mm(bank[:, :], q1[rows, j, b * P:(b + 1) * P], k1[rows, j // 4, :], start=True, stop=False)
                far = slice(CTX + P, TOK) if b == 0 else slice(CTX, CTX + P)
                mm(bank[:, far], ident, wmask[:, b, :], start=False, stop=True).then_inc(at_s, 1)

            att_scores(0)
            att_scores(1)
            for i in range(32):
                j, half, b = i // 4, i % 2, (i // 2) % 2
                pe.wait_ge(at_d, i + 1)
                pe.wait_ge(at_e, i + 1)
                if i >= 2:
                    pe.wait_ge(at_tc, i - 1)
                for c in range(4):
                    last = mm(banks[2 + i % 2][:, c * P:(c + 1) * P], prb[:, i % 2, c * P:(c + 1) * P], diag[:, i % 2, :],
                              start=True, stop=True)
                last.then_inc(at_t, 1)
                if i < 30:
                    att_scores(i + 2)
                pe.wait_ge(at_tc, i + 1)
                if i >= 2:
                    pe.wait_ge(at_oc, i - 1)
                kv = 2 * (j // 4) + half
                for c in range(4):
                    last = mm(banks[4 + i % 2][half * SWA_D:(half + 1) * SWA_D, 0:P], v1[:, c, kv * SWA_D:(kv + 1) * SWA_D],
                              prT[:, i % 2, c * P:(c + 1) * P], start=(c == 0), stop=(c == 3))
                last.then_inc(at_o, 1)
            pe.wait_ge(at_oc, 32)
            mixer_out("wout1", o1, range(2), 0)
            peer(2)

        @block.scalar
        def _(act):
            af_ = nc.scalar.activation
            in_hand(act, ON_ACT)
            act.wait_ge(setup_t, 1)
            af_(cond.rearrange("p s k -> p (s k)"), banks[2][:, 0:16], ACT.Sigmoid).then_inc(setup_a, 1)
            act.wait_ge(setup_v, 1)
            af_(lgt, lgt, ACT.Exp).then_inc(setup_a, 1)

            def modulate_x(layer):
                for k in range(KT):
                    act.wait_ge(xT_pe, 8 * layer + k + 1)
                    for s in range(2):
                        cols = slice(s * CTX, (s + 1) * CTX)
                        af_(hT[:, k, cols], banks[k % 2][:, cols], ACT.Identity,
                            scale=mcol(layer, s, 1, k), bias=mcol(layer, s, 0, k)).then_inc(hT_done, 1)
                    if layer == 0:
                        act.wait_ge(hT_done, 2 * (k + 1))
                        af_(hT_hi[:, :, k, :], hT[:, k, :].rearrange("p (s t) -> p s t", s=2), ACT.Copy).then_inc(hT_h, 1)

            MT = MOD_TILES // 2

            def high_w(slot, c):
                af_(weight_parts(c % 2)[0], wh(slot)[:, :, c * P:(c + 1) * P], ACT.Copy).then_inc(hw_h, 1)

            act.wait_ge(w_loaded[0], 16 * (MT + 1))
            for c in range(2):
                high_w(0, c)
            act.wait_ge(mod_c, 2)
            modulate_x(0)

            def sigmoid(g, slot, c):
                off = (O_Q, coff(0) + TOK, coff(0), O_G)[c]
                act.wait_ge(proj, 4 * g + c + 1)
                af_(hd(slot, off, TOK), banks[c][:, :], ACT.Sigmoid).then_inc(sig, 1)

            def values(g, slot):
                act.wait_ge(vproj, g + 1)
                af_(hd(slot, O_V, TOK), banks[7][:, :], ACT.Copy).then_inc(vsb, 1)

            def head(h, slot, more, fill=None):
                if more:
                    high_w(1 - slot, 1)
                for l in range(1, LEVELS):
                    if l == 1:
                        act.wait_ge(init, h + 1)
                    else:
                        act.wait_ge(upd, 7 * h + l - 1)
                    act.wait_ge(lvl, 1 + 8 * h + (l - 1 if l > 2 else 0))
                    m = 1 << (l - 1)
                    af_(kc[:, l % 2, :].rearrange("p (n w r) -> p n w r", w=2, r=m),
                        hap(slot, O_KD, (2 * m, TOK // (2 * m)), (TOK + m, 2), (1, m)), ACT.Copy).then_inc(kc_sb, 1)
                    if more and l in (2, 4):
                        high_w(1 - slot, l // 2 + 1)
                    if more and l % 2:
                        if l == 1:
                            act.wait_ge(y_done, h + 1)
                        sigmoid(h + 1, 1 - slot, l // 2)
                if fill is not None:
                    act.wait_ge(w_loaded[slot], fill)
                    high_w(slot, 0)
                for d in range(2):
                    act.wait_ge(kt_pe, 2 * h + d + 1)
                    act.wait_ge(ds, 1 + 2 * h)
                    af_(KTr[:, 3 * d:3 * d + 3, :].rearrange("p c k -> p (c k)"), banks[6 - 2 * d][:, 0:3 * P], ACT.Copy).then_inc(kt_sb, 1)
                act.wait_ge(o_pe, 1 + h + 1)
                act.wait_ge(ss_pe, 1 + h)
                af_(sqbuf, banks[4][:, :], ACT.Square).then_inc(sq_done, 1)
                if more:
                    values(h + 1, 1 - slot)
                act.wait_ge(ss_pe, 1 + h + 1)
                dst = stat[:, h * NB:(h + 1) * NB] if isinstance(h, int) else stat[:, bass.ds(h * NB, NB)]
                af_(dst, banks[5][:, 0:NB], ACT.Copy, bias=RMS_EPS).then_inc(ms_a, 1)

            for c in range(4):
                sigmoid(0, 0, c)
                if c < 2:
                    high_w(0, c + 2)
            act.wait_ge(w_loaded[1], 16 * (MT + 1))
            high_w(1, 0)
            values(0, 0)
            with act.Fori(0, HEADS // 2 - 1) as n:
                head(2 * n, 0, True, 16 * n + 16 * (MT + 2))
                head(2 * n + 1, 1, True, 16 * n + 16 * (MT + 2))
            head(HEADS - 2, 0, True)
            head(HEADS - 1, 1, False)

            def norms(base, blocks):
                for i, b in enumerate(blocks):
                    act.wait_ge(ln_r, base + i + 1)
                    st = stat[:, (i % 4) * 20:(i % 4) * 20 + 20]
                    af_(ln_t[:, i % 4, :], ln_x[:, b, :], ACT.Identity, scale=st[:, 14:15], bias=st[:, 15:16]).then_inc(ln_n, 1)

            norms(0, range(4))

            def peer(p):
                layer, s = PASS_LAYER[p], PASS_S[p]

                def high_w(g):
                    if g >= 16:
                        return
                    i, m = g // 4, g % 4
                    k = RING[(["wqa", "wqb", "wqc"][p], i)]
                    if m == 0:
                        act.wait_ge(w_loaded[k % 2], 16 * (k // 2 + 1))
                    if i:
                        act.wait_ge(qw_pe[m], 4 * p + i)
                    af_(weight_parts(m)[0], wt(k % 2)[:, :, m * P:(m + 1) * P], ACT.Copy).then_inc(qw_h[m], 1)

                for g in range(4):
                    high_w(g)
                for k in range(KT):
                    act.wait_ge(x1T, 8 * p + k + 1)
                    af_(hf[:, k, :], banks[k % 2][:, 0:PT_], ACT.Identity,
                        scale=mcol(layer, s, 4, k), bias=mcol(layer, s, 3, k)).then_inc(h1, 1)
                for k in range(KT):
                    if k == 0:
                        act.wait_ge(h1, 8 * p + 8)
                    af_(h_hi[:, k, :], hf[:, k, :], ACT.Copy).then_inc(hh, 1)

                for i in range(4):
                    for g in range(4 * i + 4, 4 * i + 7):
                        high_w(g)
                    act.wait_ge(qw_pe[3], 4 * p + i + 1)
                    act.wait_ge(ps_pe, 2 * (4 * p + i))
                    for half in range(2):
                        ins = af_(qp[:, 2 * half:2 * half + 2, :].rearrange("p c t -> p (c t)"),
                                  banks[(6 if i % 2 == 0 else 2) + half][:, :], ACT.Copy)
                    ins.then_inc(pq_sb, 1)
                    high_w(4 * i + 7)
                    for b in range(2):
                        act.wait_ge(ps_pe, 2 * (4 * p + i) + b + 1)
                        af_(sc[:, b, 4 * i:4 * i + 4, :].rearrange("p m n -> p (m n)"), banks[4 + b][:, :], ACT.Copy).then_inc(ps_sb, 1)
                for b in range(2):
                    act.wait_ge(ex_v, 2 * p + b + 1)
                    af_(bs[:, b], bs[:, b], ACT.Exp).then_inc(ex_a, 1)
                for b in range(2):
                    act.wait_ge(ch_t, 2 * p + b + 1)
                    ins = af_(ijw[:, 0:3, b * P:(b + 1) * P], banks[6 + b][:, 0:3 * P].rearrange("p (c t) -> p c t", c=3), ACT.Copy)
                    ins.then_inc(ch_sb, 1)

                def weigh(q, n):
                    act.wait_ge(coleq[q], n + p * (PT_ // 16) + 1)
                    for t in range(ACT_T):
                        at = 16 * n + (8 * q + t)
                        w_t = ijw[:, 2, at:at + 1] if isinstance(n, int) else ijw[:, 2, bass.ds(at, 1)]
                        ins = af_(onehots(v_raw, q)[:, t, :], onehots(v_raw, q)[:, t, :], ACT.Copy, scale=w_t)
                    ins.then_inc(colw[q], 1)

                def store(q, n):
                    for half in range(2):
                        act.wait_ge(g_pe[q], 1 + 2 * (n + p * (PT_ // 16)) + half + 1)
                        t0 = 16 * n + 8 * q + 4 * half
                        dst = gate[:, t0:t0 + 4, :] if isinstance(n, int) else gate[:, bass.ds(t0, 4), :]
                        af_(dst, banks[2 * q + half][:, :].rearrange("p (t j) -> p t j", t=4), ACT.Copy).then_inc(g_sb[q], 1)

                weigh(0, 0)
                with act.Fori(0, PT_ // 16 - 1) as n:
                    weigh(1, n)
                    store(0, n)
                    weigh(0, n + 1)
                    store(1, n)
                weigh(1, PT_ // 16 - 1)
                store(0, PT_ // 16 - 1)
                store(1, PT_ // 16 - 1)

                def high_u(q, N):
                    act.wait_ge(u_in[q], 16 * N + 16)
                    act.wait_ge(s_pe[q], N)
                    af_(u_hi[:, q, :], u_raw[:, q, :], ACT.Copy).then_inc(u_h[q], 1)

                def step(q, N, nq, nN, more=True):
                    if more:
                        high_u(nq, nN)
                    act.wait_ge(s_pe[q], N + 1)
                    act.wait_ge(p_do[q], 1 + N)
                    af_(act_s[:, q, :], banks[q][:, 0:PT_], ACT.Gelu_apprx_tanh).then_inc(s_act[q], 1)
                    act.wait_ge(v_in[q], 16 * N + 16)
                    act.wait_ge(y_ac[q], 1 + N)
                    af_(v_hi[:, q, :], v_raw[:, q, :], ACT.Copy).then_inc(v_h[q], 1)
                    act.wait_ge(p_do[q], 1 + N + 1)
                    af_(p_hi[:, q, :], prod[:, q, :], ACT.Copy).then_inc(p_h[q], 1)

                N0 = p * PAIRS
                G16 = PT_ // 16
                for q in range(2):
                    act.wait_ge(g_pe[q], 1 + 2 * G16 * (p + 1))
                high_u(0, N0)
                step(0, N0, 1, N0)
                with act.Fori(0, PAIRS - 1) as n:
                    step(1, n + N0, 0, n + N0 + 1)
                    step(0, n + N0 + 1, 1, n + N0 + 1)
                step(1, N0 + PAIRS - 1, 0, 0, more=False)
                norms(LN_BASE[p], [2 * s, 2 * s + 1])

            peer(0)
            peer(1)
            modulate_x(1)
            for i in range(10):
                act.wait_ge(qk_pe, i + 1)
                if i >= 2:
                    act.wait_ge(rope, i - 1)
                n = SEQ if i < 8 else TOK
                af_(rawq[:, i % 2, 0:n], banks[i % 2][:, 0:n], ACT.Copy).then_inc(qk_sb, 1)
            act.wait_ge(sv_pe, 4)
            for i in range(2):
                ins = af_(v1[:, 2 * i:2 * i + 2, :].rearrange("p b c -> p (b c)"), banks[4 + i][:, :], ACT.Copy)
            ins.then_inc(sv_sb, 1)

            def exponentials(i):
                st = stat[:, (i % 4) * 20:(i % 4) * 20 + 20]
                act.wait_ge(at_m, i + 1)
                if i == 0:
                    act.wait_ge(rope, 10)
                if i >= 2:
                    act.wait_ge(at_t, i - 1)
                af_(prb[:, i % 2, :], banks[i % 2][:, :], ACT.Exp, scale=SWA_SCALE, bias=st[:, 2:3], accum_out=st[:, 3:4])
                af_(st[:, 4:5], st[:, 5:6], ACT.Exp, bias=st[:, 2:3]).then_inc(at_e, 1)

            exponentials(0)
            for i in range(32):
                if i < 31:
                    exponentials(i + 1)
                act.wait_ge(at_t, i + 1)
                if i >= 2:
                    act.wait_ge(at_o, i - 1)
                af_(prT[:, i % 2, :], banks[2 + i % 2][:, :], ACT.Copy).then_inc(at_tc, 1)
            norms(8, [2, 3])
            peer(2)

        @block.vector
        def _(dve):
            V = nc.vector
            st_ = Steps(dve, dstep)
            link, did = st_.link, st_.did
            in_hand(dve, ON_DVE)
            V.memset(neg_half, -0.5)
            dve.wait_ge(setup_a, 1)
            V.tensor_tensor(cond.rearrange("p s k -> p (s k)"), banks[2][:, 0:16], cond.rearrange("p s k -> p (s k)"), ALU.mult).then_inc(cond_done, 1)
            lgf = banks[3][:, 0:24].rearrange("p (r h) -> p r h", r=3)
            link(V.tensor_copy(lgt, lgf))
            link(V.tensor_tensor(lb, lgt[:, 0, :], lgt[:, 1, :], ALU.max))
            link(V.tensor_tensor(lb, lb, lgt[:, 2, :], ALU.max))
            V.tensor_tensor(lgt, lgt, lb.unsqueeze(1).broadcast_to([P, 3, HEADS]), ALU.subtract).then_inc(setup_v, 1)
            dve.wait_ge(setup_a, 2)
            link(V.tensor_tensor(lb, lgt[:, 0, :], lgt[:, 1, :], ALU.add))
            link(V.tensor_tensor(lb, lb, lgt[:, 2, :], ALU.add))
            link(V.reciprocal(lb, lb))
            link(V.tensor_tensor(lb, lb, lgt[:, 0, :], ALU.mult))
            link(V.tensor_scalar(omlb, lb, -1.0, 1.0, ALU.mult, ALU.add))
            dve.wait_ge(lvlmask_in, 16)
            V.tensor_copy(lvlmask.rearrange("p l t -> p (l t)"), lvlraw)
            dve.wait_ge(bias_in, 32)
            with dve.Fori(0, MOD_TILES // 2) as n:
                for s in range(2):
                    dve.wait_ge(mod_pe[s], 1 + n + 1)
                    row = modsb[:, bass.ds((2 * n + s) * WCOLS, WCOLS)]
                    V.tensor_tensor(row, banks[s][0:2, :], row, ALU.add).then_inc(mod_v[s], 1)

            def low_w(g, slot, c):
                hi, lo = weight_parts(c % 2)
                dve.wait_ge(hw_h, 4 * g + (c + 1))
                V.tensor_tensor(lo, wh(slot)[:, :, c * P:(c + 1) * P], hi, ALU.subtract).then_inc(hw_l, 1)

            for c in range(2):
                low_w(0, 0, c)
            dve.wait_ge(mod_t, 1)
            for l in range(DEPTH):
                did(V.tensor_copy(modcol[:, l, :], banks[2 + l][:, 0:96]))
            st_.wait()
            for chunk in (1, 4):
                c = modcol[:, :, :].rearrange("p l (s c k) -> p l s c k", s=2, c=CHUNKS)[:, :, :, chunk, :]
                V.tensor_scalar(c, c, 1.0, None, ALU.add).then_inc(mod_c, 1)

            link(V.tensor_scalar(ng, ng, float(P), None, ALU.mult))
            V.memset(stat, 0.0).then_inc(y_done, 1)

            def scale_head(g, slot):
                dve.wait_ge(sig, 4 * g + 4)
                dve.wait_ge(proj, 4 * g + 4)
                q = hd(slot, O_Q, TOK)
                f2 = hd(slot, coff(0), 2 * TOK)
                did(V.tensor_tensor(q, banks[0][:, :], q, ALU.mult))
                gg = hd(slot, O_G, TOK)
                did(V.tensor_tensor(gg, banks[3][:, :], gg, ALU.mult))
                h1_, l1_ = (omlb[:, bass.ds(g, 1)], lb[:, bass.ds(g, 1)])
                did(V.tensor_scalar(f2, f2, h1_, l1_, ALU.mult, ALU.add))
                st_.wait()
                for d in range(2):
                    did(V.tensor_scalar(hd(slot, O_KD + d * TOK, TOK), hd(slot, coff(0) + (1 - d) * TOK, TOK), -1.0, 1.0, ALU.mult, ALU.add))
                V.tensor_tensor(hap(slot, O_QD, (TOK, 2), (1, TOK)), hap(slot, coff(0), (TOK, 2), (1, TOK)),
                                hap(slot, O_Q, (0, 2), (1, TOK)), ALU.mult).then_inc(init, 1)

            def levels(h, slot, more, more2):
                if more:
                    low_w(h + 1, 1 - slot, 1)
                at = hd(slot, O_AT, TOK).rearrange("p (b t) -> p b t", b=NB)
                for l in range(LEVELS):
                    dve.wait_ge(lvl, 1 + 8 * h + l + 1)
                    src = banks[4 + l % 2][:, :].rearrange("p (b t) -> p b t", b=NB)
                    if l == 0:
                        V.tensor_copy(at, src).then_inc(lvlcp, 1)
                        continue
                    dve.wait_ge(lvlcp, 8 * h + l)
                    k, m = l - 1, 1 << (l - 1)
                    ns, blocks = TOK // m, TOK // (2 * m)
                    qv = hap(slot, O_QD, (2 * m, blocks), (TOK + m, 2), (1, m))
                    kv = hap(slot, O_KD, (2 * m, blocks), (TOK + m, 2), (1, m))
                    cq = hap(slot, coff(k) + 1, (2, blocks), (ns - 1, 2), (0, m))
                    ck = hap(slot, coff(k) + ns + 1, (2, blocks), (-(ns + 1), 2), (0, m))
                    if l == 1:
                        dve.wait_ge(init, h + 1)
                    else:
                        dve.wait_ge(upd, 7 * h + l - 1)
                    V.tensor_tensor(hap(slot, coff(k + 1), (1, 2 * blocks)), hap(slot, coff(k), (2, 2 * blocks)), hap(slot, coff(k) + 1, (2, 2 * blocks)), ALU.mult)
                    V.tensor_tensor(qv, qv, cq, ALU.mult)
                    V.tensor_tensor(kv, kv, ck, ALU.mult).then_inc(upd, 1)
                    V.copy_predicated(at, lvlmask[:, l, :].unsqueeze(1).broadcast_to([P, NB, P]), src).then_inc(lvlcp, 1)
                    if more and l in (2, 4):
                        low_w(h + 1, 1 - slot, l // 2 + 1)
                if more2:
                    low_w(h + 2, slot, 0)

            def states(h, slot):
                decay = lambda d, b: hd(slot, coff(7) + 4 * (1 - d) + b, 1)
                dve.wait_ge(o_pe, 1 + h)
                dve.wait_ge(upd, 7 * h + 7)
                for d in range(2):
                    dve.wait_ge(ds, 1 + 2 * h + d + 1)
                    for i in range(3):
                        src = banks[5 + d][:, i * P:(i + 1) * P]
                        if i == 0:
                            ins = V.tensor_copy(STr[:, 3 * d, :], src)
                        else:
                            ins = V.scalar_tensor_tensor(STr[:, 3 * d + i, :], STr[:, 3 * d + i - 1, :], decay(d, CHAIN[3 * d + i]), src, ALU.mult, ALU.add)
                        if d == 1 and i == 2:
                            ins.then_inc(st_done, 1)
                        else:
                            link(ins)

            def finish(h, slot):
                dve.wait_ge(sq_done, h + 1)
                V.scalar_tensor_tensor(arena[:, bass.ds(A_OT + h * TOK, TOK)] if not isinstance(h, int) else oT[:, h, :],
                                       banks[4][:, :], ng, hd(slot, O_G, TOK), ALU.mult, ALU.mult).then_inc(y_done, 1)

            def head(h, slot, more, more2=True):
                levels(h, slot, more, more2)
                states(h, slot)
                if more:
                    scale_head(h + 1, 1 - slot)
                finish(h, slot)

            for k in range(KT):
                dve.wait_ge(hT_h, k + 1)
                V.tensor_tensor(hT_lo[:, :, k, :], hT[:, k, :].rearrange("p (s t) -> p s t", s=2),
                                hT_hi[:, :, k, :], ALU.subtract).then_inc(hT_l, 1)
            for c in range(2, 4):
                low_w(0, 0, c)
            low_w(1, 1, 0)
            scale_head(0, 0)
            PER = 2 * (5 + 5)
            with dve.Fori(0, HEADS // 2 - 1) as n:
                st_.enter(n, PER)
                head(2 * n, 0, True)
                head(2 * n + 1, 1, True)
            st_.leave(HEADS // 2 - 1)
            head(HEADS - 2, 0, True, False)
            head(HEADS - 1, 1, False, False)
            dve.wait_ge(rms_p, 1)
            for h in range(HEADS):
                if h >= 2:
                    dve.wait_ge(rbc, h - 1)
                V.tensor_tensor(rmsdiag(h).rearrange("p (b t) -> p b t", b=NB), ident.unsqueeze(1).broadcast_to([P, NB, P]),
                                stat[:, h * NB:(h + 1) * NB].unsqueeze(2).broadcast_to([P, NB, P]), ALU.mult).then_inc(rdiag, 1)
                if h:
                    dve.wait_ge(rbc, h)
                    V.tensor_tensor(oT[:, h - 1, :], banks[(h - 1) % 4][:, :], oT[:, h - 1, :], ALU.mult).then_inc(onorm, 1)
            dve.wait_ge(rbc, HEADS)
            V.tensor_tensor(oT[:, HEADS - 1, :], banks[(HEADS - 1) % 4][:, :], oT[:, HEADS - 1, :], ALU.mult).then_inc(onorm, 1)

            def norms(base, blocks, bank0, rows_in, res_in, stream):
                dve.wait_ge(ln_in, rows_in)
                dve.wait_ge(ln_res, res_in)
                done = []

                def front(i, b):
                    st = stat[:, (i % 4) * 20:(i % 4) * 20 + 20]
                    for half in range(2):
                        cols = slice(512 * half, 512 * half + 512)
                        ins = V.tensor_tensor(ln_t[:, i % 4, cols], banks[bank0 + 2 * i + half][:, :], ln_m[:, stream(b), cols], ALU.mult)
                        did(ins)
                    st_.wait()
                    link(V.scalar_tensor_tensor(ln_x[:, b, :], ln_x[:, b, :], ALPHA, ln_t[:, i % 4, :], ALU.mult, ALU.add))
                    for half in range(2):
                        did(V.bn_stats(st[:, 6 * half:6 * half + 6], ln_x[:, b, 512 * half:512 * half + 512]))
                    st_.wait()
                    link(V.bn_aggr(st[:, 12:14], st[:, 0:12]))
                    V.tensor_scalar(st[:, 13:14], st[:, 13:14], LN_EPS, None, ALU.add).then_inc(ln_v, 1)
                    dve.wait_ge(ln_p, base + i + 1)
                    V.scalar_tensor_tensor(st[:, 15:16], st[:, 12:13], -1.0, st[:, 14:15], ALU.mult, ALU.mult).then_inc(ln_r, 1)

                def back(i, b):
                    dve.wait_ge(ln_n, base + i + 1)
                    V.tensor_tensor(ln_t[:, i % 4, :], ln_t[:, i % 4, :], ln_g, ALU.mult).then_inc(lnv, 1)

                for i, b in enumerate(blocks):
                    front(i, b)
                    if i:
                        back(i - 1, blocks[i - 1])
                back(len(blocks) - 1, blocks[len(blocks) - 1])

            dve.wait_ge(y_pe, 8)
            norms(0, list(range(4)), 0, 64, 64, lambda b: b // 2)

            def top16(rows):
                stages = (lambda v, i, x: V.max(v[:, 0:8], x),
                          lambda v, i, x: V.max_index(i[:, 0:8], v[:, 0:8], x),
                          lambda v, i, x: V.match_replace(x, v[:, 0:8], x, LOWEST),
                          lambda v, i, x: V.max(v[:, 8:16], x),
                          lambda v, i, x: V.max_index(i[:, 8:16], v[:, 8:16], x))
                for stage in stages:
                    for v, i, x in rows:
                        did(stage(v, i, x))
                    st_.wait()

            def peer(p):
                layer, s = PASS_LAYER[p], PASS_S[p]
                for k in range(KT):
                    dve.wait_ge(hh, 8 * p + k + 1)
                    V.tensor_tensor(h_lo[:, k, :], hf[:, k, :], h_hi[:, k, :], ALU.subtract).then_inc(hl, 1)
                dve.wait_ge(x_out, 16 * LN_BASE[p])
                siu = si.bitcast(U32)
                biu = bi.bitcast(U32)
                for i in range(4):
                    for b in range(2):
                        dve.wait_ge(ps_sb, 2 * (4 * p + i) + b + 1)
                        top16([(sv[:, b, m, :], siu[:, b, m, :], sc[:, b, m, :]) for m in range(4 * i, 4 * i + 4)])
                        svh = sv[:, b, 4 * i:4 * i + 4, :].rearrange("p (h c) k -> p h c k", c=2)
                        did(V.tensor_tensor(cand[:, b], svh[:, :, 0, :].unsqueeze(3).broadcast_to([P, 2, TOPK, TOPK]),
                                            svh[:, :, 1, :].unsqueeze(2).broadcast_to([P, 2, TOPK, TOPK]), ALU.add))
                    st_.wait()
                    top16([(bs[:, b, 2 * i + h, :], biu[:, b, 2 * i + h, :], cand[:, b, h, :, :].rearrange("p a b -> p (a b)"))
                           for b in range(2) for h in range(2)])
                for b in range(2):
                    if b:
                        dve.wait_ge(jon2, 2 * p + b)
                    did(V.tensor_copy(sif.rearrange("p m k -> p (m k)"), siu[:, b, :, :].rearrange("p m k -> p (m k)")))
                    gsum = gsums[:, b, :]
                    link(V.tensor_copy(gsum, bs[:, b, :, 0]))
                    V.tensor_tensor(bs[:, b], bs[:, b], gsum.unsqueeze(2).broadcast_to([P, PH, TOPK]), ALU.subtract).then_inc(ex_v, 1)
                    did(V.tensor_scalar(ba.bitcast(U32), biu[:, b], 4, None, ALU.logical_shift_right))
                    link(V.tensor_scalar(bb.bitcast(U32), biu[:, b], TOPK - 1, None, ALU.bitwise_and))
                    did(V.tensor_copy(bf, bb.bitcast(U32)))
                    link(V.tensor_copy(af, ba.bitcast(U32)))
                    i16 = iota[:, 0:TOPK].unsqueeze(1).unsqueeze(1).broadcast_to([P, PH, TOPK, TOPK])
                    V.tensor_tensor(eqb, bf.unsqueeze(3).broadcast_to([P, PH, TOPK, TOPK]), i16, ALU.is_equal).then_inc(jon, 1)
                    link(V.tensor_tensor(eqa, af.unsqueeze(3).broadcast_to([P, PH, TOPK, TOPK]), i16, ALU.is_equal))
                    sih = sif.rearrange("p (h c) k -> p h c k", c=2)
                    link(V.tensor_tensor(eqa, eqa, sih[:, :, 0, :].unsqueeze(2).broadcast_to([P, PH, TOPK, TOPK]), ALU.mult))
                    if b:
                        dve.wait_ge(ch_t, 2 * p + b)
                    did(V.tensor_reduce(ijt[:, 0, :].rearrange("p (h k) -> p h k", h=PH), eqa, AX.X, ALU.add))
                    dve.wait_ge(ex_a, 2 * p + b + 1)
                    link(V.tensor_reduce(gsum, bs[:, b], AX.X, ALU.add))
                    link(V.reciprocal(gsum, gsum))
                    did(V.tensor_tensor(ijt[:, 2, :].rearrange("p (h k) -> p h k", h=PH), bs[:, b], gsum.unsqueeze(2).broadcast_to([P, PH, TOPK]), ALU.mult))
                    dve.wait_ge(jon2, 2 * p + b + 1)
                    V.tensor_reduce(ijt[:, 1, :].rearrange("p (h k) -> p h k", h=PH), eqb, AX.X, ALU.add).then_inc(jch, 1)
                dve.wait_ge(ch_sb, 2 * p + 2)
                with dve.Fori(0, PT_ // 16) as n:
                    for q in range(2):
                        N = n + p * (PT_ // 16)
                        dve.wait_ge(g_pe[q], 1 + 2 * N)
                        number = lambda c, m: ijw[:, c, bass.ds(16 * n + 8 * q, m)].unsqueeze(2).broadcast_to([P, m, NK])
                        key = lambda m: iota.unsqueeze(1).broadcast_to([P, m, NK])
                        V.tensor_tensor(onehots(v_raw, q)[:, 0:ACT_T, :], number(1, ACT_T), key(ACT_T), ALU.is_equal).then_inc(coleq[q], 1)
                        for t in range(ACT_T, 8):
                            j_t, w_t = (ijw[:, c, bass.ds(16 * n + (8 * q + t), 1)] for c in (1, 2))
                            V.tensor_scalar(onehots(v_raw, q)[:, t, :], iota, j_t, w_t, ALU.is_equal, ALU.mult)
                        V.tensor_tensor(onehots(u_raw, q), number(0, 8), key(8), ALU.is_equal).then_inc(onehot[q], 1)

                def low_u(q, N):
                    dve.wait_ge(u_h[q], N + 1)
                    V.tensor_tensor(u_lo[:, q, :], u_raw[:, q, :], u_hi[:, q, :], ALU.subtract).then_inc(u_l[q], 1)

                def step(j, q, N, nq, nN, more=True):
                    if more:
                        low_u(nq, nN)
                    dve.wait_ge(s_act[q], N + 1)
                    dve.wait_ge(p_l[q], 1 + N)
                    V.tensor_tensor(prod[:, q, :], act_s[:, q, :], gate[:, :, j] if isinstance(j, int) else gate[:, :, bass.ds(j, 1)].rearrange("p t o -> p (t o)"), ALU.mult).then_inc(p_do[q], 1)
                    dve.wait_ge(v_h[q], N + 1)
                    V.tensor_tensor(v_lo[:, q, :], v_raw[:, q, :], v_hi[:, q, :], ALU.subtract).then_inc(v_l[q], 1)
                    dve.wait_ge(p_h[q], N + 1)
                    V.tensor_tensor(p_lo[:, q, :], prod[:, q, :], p_hi[:, q, :], ALU.subtract).then_inc(p_l[q], 1)

                N0 = p * PAIRS
                for q in range(2):
                    dve.wait_ge(g_sb[q], 1 + 2 * (PT_ // 16) * (p + 1))
                low_u(0, N0)
                step(0, 0, N0, 1, N0)
                with dve.Fori(0, PAIRS - 1) as n:
                    step(2 * n + 1, 1, n + N0, 0, n + N0 + 1)
                    step(2 * n + 2, 0, n + N0 + 1, 1, n + N0 + 1)
                step(NK - 1, 1, N0 + PAIRS - 1, 0, 0, more=False)
                dve.wait_ge(y_ac[1], 1 + PAIRS * (p + 1))
                norms(LN_BASE[p], [2 * s, 2 * s + 1], 2, 16 * [7, 10, 16][p], 16 * [6, 8, 12][p], lambda b: s)

            peer(0)
            peer(1)
            dve.wait_ge(x_out, 16 * 8)
            dve.wait_ge(swa_c, 16)
            for i in range(10):
                if i < 8:
                    dst, lo = q1[:, i, :], 0
                else:
                    dst, lo = k1[:, i - 8, CTX:TOK], CTX
                raw = rawq[:, i % 2, lo:lo + SEQ]
                dve.wait_ge(qk_sb, i + 1)
                did(V.tensor_tensor(dst, raw, cos, ALU.mult))
                if i >= 8:
                    did(V.tensor_copy(k1[:, i - 8, 0:CTX], rawq[:, i % 2, 0:CTX]))
                dve.wait_ge(rot_pe, i + 1)
                link(V.tensor_tensor(rtmp[:, i % 2, 0:SEQ], banks[2 + i % 2][:, 0:SEQ], sin, ALU.mult))
                V.tensor_tensor(dst, dst, rtmp[:, i % 2, 0:SEQ], ALU.add).then_inc(rope, 1)

            def out_copy(i):
                j, half, b = i // 4, i % 2, (i // 2) % 2
                rows = slice(half * SWA_D, (half + 1) * SWA_D)
                dve.wait_ge(at_o, i + 1)
                V.tensor_copy(o1[rows, j, b * P:(b + 1) * P], banks[4 + i % 2][rows, 0:P]).then_inc(at_oc, 1)

            def maxima(i):
                j, half = i // 4, i % 2
                hq = (2 * (j // 4) + half) * 4 + j % 4
                st = stat[:, (i % 4) * 20:(i % 4) * 20 + 20]
                dve.wait_ge(at_s, i + 1)
                did(V.tensor_copy(st[:, 5:6], sink[:, hq:hq + 1]))
                link(V.reduce_max(st[:, 0:1], banks[i % 2][:, :], AX.X))
                link(V.tensor_scalar(st[:, 1:2], st[:, 0:1], SWA_SCALE, sink[:, hq:hq + 1], ALU.mult, ALU.max))
                V.tensor_scalar(st[:, 2:3], st[:, 1:2], -1.0, None, ALU.mult).then_inc(at_m, 1)

            maxima(0)
            for i in range(32):
                st = stat[:, (i % 4) * 20:(i % 4) * 20 + 20]
                if i < 31:
                    maxima(i + 1)
                dve.wait_ge(at_e, i + 1)
                link(V.tensor_tensor(st[:, 6:7], st[:, 3:4], st[:, 4:5], ALU.add))
                link(V.reciprocal(st[:, 7:8], st[:, 6:7]))
                if i >= 2:
                    dve.wait_ge(at_t, i - 1)
                V.tensor_scalar(diag[:, i % 2, :], ident, st[:, 7:8], None, ALU.mult).then_inc(at_d, 1)
                if i:
                    out_copy(i - 1)
            out_copy(31)
            dve.wait_ge(y_pe, 12)
            norms(8, [2, 3], 0, 16 * 13, 16 * 10, lambda b: 1)
            peer(2)

        @block.gpsimd
        def _(pool):
            G = nc.gpsimd

            def norms(base, blocks):
                def shift(i):
                    pool.wait_ge(lnv, base + i + 1)
                    G.tensor_tensor(ln_x[:, blocks[i], :], ln_t[:, i % 4, :], ln_b, ALU.add).then_inc(ln_o, 1)

                for i in range(len(blocks)):
                    st = stat[:, (i % 4) * 20:(i % 4) * 20 + 20]
                    pool.wait_ge(ln_v, base + i + 1)
                    G.tensor_tensor(st[:, 14:15], st[:, 13:14], neg_half, ALU.pow).then_inc(ln_p, 1)
                    if i:
                        shift(i - 1)
                shift(len(blocks) - 1)

            pool.wait_ge(setup_v, 1)
            pool.wait_ge(ms_a, 1 + HEADS)
            ms = stat[:, 0:HEADS * NB]
            G.tensor_tensor(ms, ms, neg_half.broadcast_to([P, HEADS * NB]), ALU.pow).then_inc(rms_p, 1)
            norms(0, range(4))

            def peer(p):
                s = PASS_S[p]
                for i in range(4):
                    w = wt(RING[(["wqa", "wqb", "wqc"][p], i)] % 2)
                    for m in range(4):
                        pool.wait_ge(qw_h[m], 4 * p + i + 1)
                        hi, lo = weight_parts(m)
                        G.tensor_tensor(lo, w[:, :, m * P:(m + 1) * P], hi, ALU.subtract).then_inc(qw_l[m], 1)
                for b in range(2):
                    pool.wait_ge(jon, 2 * p + b + 1)
                    sih = sif.rearrange("p (h c) k -> p h c k", c=2)
                    G.tensor_tensor(eqb, eqb, sih[:, :, 1, :].unsqueeze(2).broadcast_to([P, PH, TOPK, TOPK]), ALU.mult).then_inc(jon2, 1)
                norms(LN_BASE[p], [2 * s, 2 * s + 1])

            peer(0)
            peer(1)
            norms(8, [2, 3])
            peer(2)


def constants():
    c = np.zeros((P, C_ALL), np.float32)
    c[:, C_ID:C_ID + P] = np.eye(P)
    c[:, C_IOTA:C_IOTA + P] = np.arange(P)
    c[:, C_ONE:C_ONE + P] = 1.0 / P
    rot = np.zeros((P, P), np.float32)
    for h in range(2):
        for ax in range(2):
            for f in range(16):
                x1 = h * 64 + ax * 32 + f
                rot[x1, x1 + 16] = -1.0
                rot[x1 + 16, x1] = 1.0
    c[:, C_ROT:C_ROT + P] = rot.T
    t = np.arange(SEQ)
    pos = np.stack([t // 64, t % 64]).astype(np.float32)
    inv = (np.float32(10000.0) ** (-np.arange(0, 32, 2, dtype=np.float32) / np.float32(32))).astype(np.float32)
    ang = pos[:, :, None] * inv
    for p in range(P):
        ax, f = (p % 64) // 32, p % 16
        c[p, C_COS:C_COS + SEQ] = np.cos(ang[ax, :, f])
        c[p, C_SIN:C_SIN + SEQ] = np.sin(ang[ax, :, f])
    q, k = np.arange(P)[:, None], np.arange(P)[None, :]
    c[:, C_MASK:C_MASK + P] = np.where(k <= q, 0.0, SCORE_MASK)
    c[:, C_MASK + P:C_MASK + 2 * P] = np.where(q <= k, 0.0, SCORE_MASK)
    m = np.zeros((P, LEVELS, P), np.float32)
    for l in range(1, LEVELS):
        h = 1 << (l - 1)
        m[:, l, :] = (q // (2 * h) == k // (2 * h)) & (q // h != k // h)
    return c, m.reshape(P, LEVELS * P)


def kernel(**inputs):
    import concourse.bacc as bacc
    from concourse.bass_utils import run_bass_kernel_spmd as run

    x = {k: np.ascontiguousarray(np.asarray(v)) for k, v in inputs.items()}

    def tiles(w, cols):
        n = w.shape[1] // cols
        return w.reshape(KT, P, n, cols).transpose(2, 1, 0, 3).reshape(n, P, KT * cols)

    qh = [(2 * (j // 4) + half) * 4 + j % 4 for j in range(8) for half in range(2)]
    qcols = np.concatenate([np.arange(64) + 64 * h for h in qh])
    swa = x["swa_w_in"][0]
    qkv = np.concatenate([swa[:, qcols], swa[:, 1024:]], axis=1)
    wst = np.concatenate(
        [tiles(x["mod_w"][l], WCOLS) for l in range(DEPTH)]
        + [tiles(x["hgrn_w_out"][0], WCOLS), tiles(x["peer_wq"][0], WCOLS), tiles(qkv, WCOLS),
           tiles(x["swa_w_out"][0][qcols], WCOLS), tiles(x["peer_wq"][1], WCOLS)])
    w5 = x["hgrn_w_in"][0].reshape(D, 5, HEADS, P)
    whd = tiles(w5[:, [0, 2, 3, 4, 1]].transpose(0, 2, 1, 3).reshape(D, HEADS * HCOLS), HCOLS)
    u = x["peer_u"].reshape(DEPTH, P, NK, KT, P).transpose(0, 2, 4, 3, 1).reshape(DEPTH, NK, P, D)
    v = x["peer_v"].reshape(DEPTH, P, NK, D).transpose(0, 2, 1, 3)
    keys = x["peer_keys"].transpose(0, 4, 1, 2, 3).reshape(DEPTH, P, 16 * NK)
    const, lvlmask = constants()
    arrays = {"x": x["x"], "ctx": x["ctx"], "c": x["c"], "c_ctx": x["c_ctx"], "mod_b": x["mod_b"], "ln_g": x["ln_g"],
              "ln_b": x["ln_b"], "lb": x["hgrn_lb_logits"], "ng": x["hgrn_norm_g"], "sink": x["swa_sink"][0],
              "wst": wst, "whd": whd, "u": u, "v": v, "keys": keys, "const": const, "lvlmask": lvlmask}
    arrays = {"in_" + k: np.ascontiguousarray(v) for k, v in arrays.items()}
    nc = bacc.Bacc("TRN2", target_bir_lowering=False, num_devices=1)
    args = {k[3:]: nc.dram_tensor(k, v.shape, mybir.dt.from_np(v.dtype), kind="ExternalInput").ap() for k, v in arrays.items()}
    args["out"] = nc.dram_tensor("out", (1, SEQ, D), F32, kind="ExternalOutput").ap()
    build(nc, args)
    r = run(nc, [arrays], core_ids=[0])
    return r.results[0]["out"]
```

```python
from contextlib import ExitStack

import numpy as np
import concourse.bass as bass
from concourse import mybir

F32 = mybir.dt.float32
F32R = mybir.dt.float32r
U32 = mybir.dt.uint32
U8 = mybir.dt.uint8
ALU = mybir.AluOpType
ACT = mybir.ActivationFunctionType
AX = mybir.AxisListType

P = 128
D = 1024
KT = D // P
SEQ = 256
CTX = 256
TOK = SEQ + CTX
NB = TOK // P
DEPTH = 2
ALPHA = (2 * DEPTH) ** 0.25
LN_EPS = 1e-5
RMS_EPS = 1e-6
HEADS = 8
LEVELS = 8
CHUNKS = 6
WCOLS = 512
MOD_TILES = CHUNKS * D // WCOLS
MOD_PART = MOD_TILES // 2
HCOLS = 5 * P
WSLOT = KT * HCOLS
SWA_D = 64
SWA_SCALE = SWA_D ** -0.5
PH = 8
TOPK = 16
PAIR_SETS = ((0, 0, 1, 16), (16, 1, 3, 8), (40, 4, 4, 4), (56, 8, 8, 1))
NCAND = 64
ACT_T = 5
NK = 128
PT_ = 256
LOWEST = -3.4e38
SCORE_MASK = -1e30

C_ID, C_IOTA, C_ONE, C_ROT, C_COS, C_SIN, C_MASK = 0, 128, 256, 384, 512, 768, 1024
C_KEEP, C_ALL = 384, 1024 + 256


class Steps:

    def __init__(self, eng, sem):
        self.eng, self.sem, self.base, self.k = eng, sem, 0, 0

    def did(self, ins):
        ins.then_inc(self.sem, 1)
        self.k += 1

    def wait(self):
        self.eng.wait_ge(self.sem, self.base + self.k)

    def link(self, ins):
        self.did(ins)
        self.wait()

    def enter(self, i, per):
        self.start = self.base + self.k
        self.base, self.k, self.per = self.start + i * per, 0, per

    def leave(self, n):
        assert self.k == self.per, (self.k, self.per)
        self.base, self.k = self.start + n * self.per, 0


def build(nc, a):
    ctx = ExitStack()
    with ctx:
        def sem(name):
            return ctx.enter_context(nc.semaphore(name))

        def sb(name, shape, dt=F32):
            return ctx.enter_context(nc.sbuf_tensor(name, shape, dt))

        modd = nc.dram_tensor("mod_scratch", [2, DEPTH * CHUNKS * D], F32, kind="Internal").ap()
        xs = nc.dram_tensor("x_scratch", [NB, P, D], F32, kind="Internal").ap()

        arena = sb("arena", [P, 128 * PT_])
        const = sb("const", [P, 384])
        modcol = sb("modcol", [P, DEPTH, 96])
        small = sb("small", [P, 160])
        u_raw = sb("u_raw", [P, 2, D])
        v_raw = sb("v_raw", [P, 2, D])
        u_hi = sb("u_hi", [P, 2, D], F32R)
        u_lo = sb("u_lo", [P, 2, D], F32R)
        v_parts = sb("v_parts", [P, 4, D], F32R)
        v_hi, v_lo = v_parts[:, 0:2, :], v_parts[:, 2:4, :]
        h_parts = sb("h_parts", [P, 2, KT, PT_], F32R)
        h_hi, h_lo = h_parts[:, 0, :, :], h_parts[:, 1, :, :]
        act_s = sb("act_s", [P, 2, PT_])
        prod = sb("prod", [P, 2, PT_])
        p_hi = sb("p_hi", [P, 2, PT_], F32R)
        p_lo = sb("p_lo", [P, 2, PT_], F32R)
        ijw = sb("ijw", [P, 4, PT_])
        banks = [ctx.enter_context(nc.psum_tensor(f"bank{i}", [P, 512], F32)) for i in range(8)]

        def ar(off, size, **dims):
            v = arena[:, off:off + size]
            if dims:
                names = " ".join(dims)
                v = v.rearrange(f"p ({names}) -> p {names}", **dims)
            return v

        ident = const[:, C_ID:C_ID + P]
        iota = const[:, C_IOTA:C_IOTA + P]
        mean_w = const[:, C_ONE:C_ONE + P]
        lvlmask = prod[:, 0, :].bitcast(U8).rearrange("p (l t) -> p l t", l=LEVELS)
        sqbuf = act_s[:, :, :].rearrange("p a t -> p (a t)")

        W = [0, WSLOT]
        A_HT = 2 * WSLOT
        A_OT = A_HT + 4096
        A_HD = A_OT + 4096
        HD = 6144
        A_KT = A_HD + 2 * HD
        A_ST = A_KT + 768
        assert A_ST + 768 <= 128 * PT_
        hT = ar(A_HT, 4096, k=KT, t=TOK)
        hT_hi = h_parts
        hT_lo = v_parts.rearrange("p (s x) (k t) -> p s (x k) t", s=2, t=PT_)
        oT = ar(A_OT, 4096, k=KT, t=TOK)
        xtok = ar(A_HD, 4096, b=NB, d=D)
        A_LN = A_HD + 1024
        ln_x = ar(A_LN, 4096, b=NB, d=D)
        ln_t = ar(A_LN + 4096, 4096, s=4, d=D)
        ln_m = ar(A_LN + 8192, 2048, s=2, d=D)
        ln_g = ar(A_LN + 10240, 1024)
        ln_b = ar(A_LN + 11264, 1024)

        cond = small[:, 0:16].rearrange("p (s k) -> p s k", s=2)
        lb = small[:, 16:24]
        omlb = small[:, 24:32]
        ng = small[:, 32:33]
        lgt = small[:, 33:57].rearrange("p (r h) -> p r h", r=3)
        sink = small[:, 57:73]
        stat = small[:, 73:153]
        neg_half = small[:, 153:154]

        const_in = sem("const_in")
        cond_in = sem("cond_in")
        lvlmask_in = sem("lvlmask_in")
        bias_in = sem("bias_in")
        w_loaded = [sem(f"w_loaded{i}") for i in range(2)]
        setup_t = sem("setup_transposed")
        setup_a = sem("setup_act")
        setup_v = sem("setup_vector")
        cond_done = sem("cond_done")
        mod_pe = [sem(f"mod_product{i}") for i in range(2)]
        mod_v = [sem(f"mod_biased{i}") for i in range(2)]
        mod_out = sem("mod_stored")
        mod1_b = sem("mod1_bias_loaded")
        mod1_pe = sem("mod1_products")
        mod1_a = sem("mod1_copied")
        mod1_v = sem("mod1_biased")
        mod1_out = sem("mod1_stored")
        mod_t = sem("mod_transposed")
        mod_c = sem("mod_columns")
        x_in = sem("x_loaded")
        xT_pe = sem("x_transposed")
        hT_done = sem("hT_ready")
        hT_h = sem("hT_high")
        hT_l = sem("hT_low")
        hw_h = sem("head_weights_high")
        hw_l = sem("head_weights_low")
        proj = sem("head_projected")
        vproj = sem("head_values_projected")
        sig = sem("head_sigmoids")
        vsb = sem("head_values_copied")
        init = sem("head_scaled")
        lvl = sem("level_products")
        lvlcp = sem("level_copied_out")
        upd = sem("level_decays_applied")
        kc_sb = sem("level_keys_ready")
        kt_pe = sem("keys_transposed")
        kt_sb = sem("keys_copied")
        ds = sem("state_products")
        st_done = sem("states_ready")
        o_pe = sem("head_output")
        sq_done = sem("head_squares")
        ss_pe = sem("head_square_sums")
        ms_a = sem("head_mean_squares")
        rms_p = sem("head_scales")
        y_done = sem("head_finished")
        rdiag = sem("head_scale_diagonals")
        rbc = sem("head_scales_spread")
        onorm = sem("head_normalised")
        ln_in = sem("ln_rows_loaded")
        ln_min = sem("ln_modulation_loaded")
        ln_res = [sem(f"ln_residual_loaded{i}") for i in range(NB)]
        y_pe = sem("mixer_output")
        ln_v = sem("ln_variances")
        ln_p = sem("ln_scales")
        ln_o = sem("ln_finished")
        x_out = sem("x_stored")
        x1T = sem("tokens_transposed")
        h1 = sem("tokens_modulated")
        hh = sem("tokens_high_part")
        hl = sem("tokens_low_part")
        keys_in = sem("keys_loaded")
        qw_h = [sem(f"query_weights_high{i}") for i in range(4)]
        qw_l = [sem(f"query_weights_low{i}") for i in range(4)]
        qw_pe = [sem(f"query_products{i}") for i in range(4)]
        pq_sb = sem("queries_copied")
        ps_pe = sem("score_products")
        ps_sb = sem("scores_copied")
        jch = sem("choices_made")
        jon = sem("column_numbers_ready")
        ex_v = sem("gate_shifted")
        ex_a = sem("gate_exponentials")
        ch_t = sem("choices_transposed")
        ch_sb = sem("choices_copied")
        onehot = [sem(f"onehots{i}") for i in range(2)]
        coleq = [sem(f"column_onehots{i}") for i in range(2)]
        colw = [sem(f"columns_weighed{i}") for i in range(2)]
        g_pe = [sem(f"gate_products{i}") for i in range(2)]
        g_sb = [sem(f"gates_stored{i}") for i in range(2)]
        u_in = [sem(f"u_loaded{i}") for i in range(2)]
        v_in = [sem(f"v_loaded{i}") for i in range(2)]
        u_h = [sem(f"u_high{i}") for i in range(2)]
        u_l = [sem(f"u_low{i}") for i in range(2)]
        v_h = [sem(f"v_high{i}") for i in range(2)]
        v_l = [sem(f"v_low{i}") for i in range(2)]
        s_pe = [sem(f"expert_scores{i}") for i in range(2)]
        s_act = [sem(f"expert_gelus{i}") for i in range(2)]
        p_do = [sem(f"expert_weights{i}") for i in range(2)]
        p_h = [sem(f"weights_high{i}") for i in range(2)]
        p_l = [sem(f"weights_low{i}") for i in range(2)]
        y_ac = [sem(f"expert_outputs{i}") for i in range(2)]
        qk_pe = sem("swa_projected")
        qk_sb = sem("swa_copied")
        rot_pe = sem("swa_rotated")
        rope = sem("swa_roped")
        sv_pe = sem("swa_values_projected")
        sv_sb = sem("swa_values_copied")
        at_s = sem("swa_scores")
        at_m = sem("swa_maxima")
        at_e = sem("swa_exponentials")
        at_d = sem("swa_diagonals")
        at_t = sem("swa_probs_transposed")
        at_tc = sem("swa_probs_copied")
        at_o = sem("swa_outputs")
        at_oc = sem("swa_outputs_copied")
        swa_c = sem("swa_constants_loaded")
        jon2 = sem("column_numbers_masked")
        dstep = sem("vector_steps")

        B_HF = 2 * WSLOT
        B_K = B_HF + 2048
        B_Q = B_K + 2048
        B_S = B_Q + 1024
        B_C = B_S + 4096
        B_E = B_C + 2048
        B_F = B_E + 2048
        B_R = B_F + 2048
        hf = ar(B_HF, 2048, k=KT, t=PT_)
        qp = ar(B_Q, 1024, c=4, t=PT_)
        sc = ar(B_S, 4096, b=2, m=16, n=NK)
        kp = ar(B_K, 2048, m=16, n=NK)
        cand = ar(B_C, 4 * NCAND, c=2, h=2, n=NCAND)
        eqa = ar(B_E, 2048, h=PH, k=TOPK, a=TOPK)
        eqb = ar(B_F, 2048, h=PH, k=TOPK, a=TOPK)
        sv = ar(B_R + 2048, 512, b=2, m=16, k=TOPK)
        si = ar(B_R + 2560, 512, b=2, m=16, k=TOPK)
        sif = ar(B_R + 512, 256, m=16, k=TOPK)
        bs = ar(B_R + 768, 256, b=2, h=PH, k=TOPK)
        bi = ar(B_R + 3072, 256, b=2, h=PH, k=TOPK)
        ba = ar(B_R, 256)
        bb = ar(B_R + 256, 256)
        af = ar(B_R + 1024, 256)
        bf = ar(B_R + 1280, 256)
        B_M = B_R + 3328
        assert B_M + MOD_PART * WCOLS <= 128 * PT_
        mod1 = arena[0:2, B_M:B_M + MOD_PART * WCOLS]
        mod1_t = [x[0:2, :, :].rearrange("p a t -> p (a t)") for x in (act_s, prod)]
        ijt = ar(B_R + 1536, 384, c=3, m=128)
        gsums = ar(B_R + 1920, 16, b=2, h=PH)
        gate = arena[:, :].rearrange("p (t j) -> p t j", j=NK)

        WOUT_ORDER = [[(0, 1), (1, 1), (0, 0), (1, 0), (2, 0), (3, 0), (2, 1), (3, 1)], [(0, 1), (0, 0), (1, 0), (1, 1)]]
        Y_BLOCK = [[max(k for k, x in enumerate(o) if x[0] == b) + 1 for b in range(len(o) // 2)] for o in WOUT_ORDER]
        Y_TILE = [[max(k for k, x in enumerate(o) if x[1] == half) + 1 for half in range(2)] for o in WOUT_ORDER]

        def weight_parts(m):
            return [(u, v)[m // 2][:, m % 2, :].rearrange("p (k n) -> p k n", k=KT) for u, v in ((u_hi, v_hi), (u_lo, v_lo))]


        T_WOUT0 = DEPTH * MOD_TILES
        T_WQ0, T_QKV, T_WOUT1, T_WQ1 = T_WOUT0 + 2, T_WOUT0 + 6, T_WOUT0 + 9, T_WOUT0 + 11

        def wt(slot):
            return ar(W[slot], KT * WCOLS, k=KT, n=WCOLS)

        def wh(slot):
            return ar(W[slot], WSLOT, k=KT, n=HCOLS)

        ORDER = ([("loop", i) for i in range(MOD_TILES)] + [("head", i) for i in range(HEADS)]
                 + [("wout0", i) for i in range(2)] + [("wqa", i) for i in range(4)] + [("mod1a", i) for i in range(MOD_PART)]
                 + [("wqb", i) for i in range(4)] + [("mod1b", i) for i in range(MOD_PART)]
                 + [("qkv", i) for i in range(3)] + [("wout1", i) for i in range(2)] + [("wqc", i) for i in range(4)])
        RING = {n: k for k, n in enumerate(ORDER)}
        SRC = {"mod1a": MOD_TILES, "mod1b": MOD_TILES + MOD_PART, "wout0": T_WOUT0, "wqa": T_WQ0, "wqb": T_WQ0, "qkv": T_QKV, "wout1": T_WOUT1, "wqc": T_WQ1}


        def onehots(buf, slot):
            return buf[:, slot, :].rearrange("p (t j) -> p t j", t=8)

        A_MOD = A_HD + HD
        MODN = CHUNKS * D
        modsb = arena[0:2, A_MOD:A_MOD + MODN]
        A_RAW = A_MOD + MODN
        condraw = arena[0:16, A_RAW:A_RAW + P]
        lbraw = arena[0:24, A_RAW + P:A_RAW + 2 * P]

        lvlraw = ar(A_RAW + 2 * P, LEVELS * P)

        def mcol(layer, s, chunk, k):
            n = 2 * (chunk * KT + k) + s
            return modcol[:, layer, n:n + 1]

        def hd(slot, off, n):
            return arena[:, A_HD + slot * HD + off:A_HD + slot * HD + off + n]

        O_Q, O_QD, O_KD, O_C, O_G, O_V, O_AT = 0, 512, 1536, 2560, 4608, 5120, 5632

        def coff(k):
            return O_C + 2048 - (2048 >> k)

        def hap(slot, off, *dims):
            return bass.AP(tensor=arena[:, 0:1].tensor, offset=A_HD + slot * HD + off,
                           ap=[[128 * PT_, P]] + [list(d) for d in dims])

        def level_operand(slot, off, m, blk):
            return hap(slot, off + blk * P, (2 * m, P // (2 * m)), (TOK + m, 2), (1, m))

        def rmsdiag(h):
            return u_raw[:, h % 2, 0:TOK]

        kc = ijw[:, :, :].rearrange("p (s a) t -> p s (a t)", s=2)
        KTr = ar(A_KT, 768, c=6, k=P)
        STr = ar(A_ST, 768, c=6, k=P)
        FW, BW = [0, 1, 2], [1, 0, 3]
        CHAIN = FW + BW

        A_Q1 = A_OT + 2048
        A_K1 = A_HD + 4096
        q1 = ar(A_Q1, 2048, j=8, t=SEQ)
        k1 = ar(A_K1, 1024, j=2, t=TOK)
        v1 = ar(A_K1 + 1024, 1024, b=NB, c=256)
        c1 = ar(A_K1 + 2048, C_ALL - C_KEEP)
        o1 = ar(A_OT, 2048, j=8, t=SEQ)
        rawq = ar(A_K1 + 2048 + 1024, 1024, s=2, t=512)
        rtmp = ar(A_K1 + 2048 + 2048, 1024, s=2, t=512)
        prb = ar(A_K1 + 2048 + 1024, 1024, s=2, t=512)
        prT = ar(A_K1 + 2048 + 2048, 1024, s=2, t=512)
        diag = ar(A_K1 + 2048 + 3072, 256, s=2, t=P)
        assert A_K1 + 2048 + 3072 + 256 <= 128 * PT_
        rot = c1[:, C_ROT - C_KEEP:C_ROT - C_KEEP + P]
        cos = c1[:, C_COS - C_KEEP:C_COS - C_KEEP + SEQ]
        sin = c1[:, C_SIN - C_KEEP:C_SIN - C_KEEP + SEQ]
        wmask = c1[:, C_MASK - C_KEEP:C_MASK - C_KEEP + 256].rearrange("p (b k) -> p b k", b=2)

        assert B_C == A_LN
        PASS_LAYER = [0, 0, 1]
        PASS_S = [0, 1, 1]
        LN_BASE = [4, 6, 10]
        PAIRS = NK // 2

        ON_PE = [*mod_pe, lvl, ds, ss_pe, o_pe, *g_pe, *y_ac]
        ON_ACT = [*g_sb, ms_a]
        ON_DVE = [*mod_v, *u_l, *v_l, *p_l, *p_do]

        def in_hand(eng, sems):
            for x in sems:
                eng.sem_inc(x, 1)

        block = ctx.enter_context(nc.Block())

        @block.sync
        def _(sp):
            def tile(name, i):
                k = RING[(name, i)]
                s = k % 2
                was, at = ORDER[k - 2]
                if was == "head":
                    sp.wait_ge(vproj, at + 1)
                elif was in ("wout0", "wout1"):
                    sp.wait_ge(y_pe, Y_TILE[0][at] if was == "wout0" else 8 + Y_TILE[1][at])
                elif was in ("mod1a", "mod1b"):
                    sp.wait_ge(mod1_pe, (0 if was == "mod1a" else MOD_PART) + at + 1)
                elif was == "qkv":
                    sp.wait_ge(qk_pe if at < 2 else sv_pe, 4 * (at + 1) if at < 2 else 4)
                else:
                    sp.wait_ge(qw_l[3], 4 * ["wqa", "wqb", "wqc"].index(was) + at + 1)
                sp.dma_start(ar(W[s], KT * WCOLS), a["wst"][SRC[name] + i]).then_inc(w_loaded[s], 16)

            sp.dma_start(const[:, :], a["const"][:, 0:C_KEEP]).then_inc(const_in, 16)
            sp.dma_start(condraw[0:8, :], a["c_ctx"].rearrange("(k d) -> k d", d=P)).then_inc(cond_in, 16)
            sp.dma_start(condraw[8:16, :], a["c"].rearrange("o (k d) -> (o k) d", d=P)).then_inc(cond_in, 16)
            sp.dma_start(lbraw[:, :], a["lb"].rearrange("r (h d) -> (r h) d", d=P)).then_inc(cond_in, 16)
            sp.dma_start(ng, a["ng"].rearrange("o d -> d o")).then_inc(cond_in, 16)
            sp.dma_start(sink, a["sink"].partition_broadcast(P)).then_inc(cond_in, 16)
            sp.dma_start(lvlraw, a["lvlmask"]).then_inc(lvlmask_in, 16)
            for s in range(2):
                sp.dma_start(modsb[s:s + 1, :], a["mod_b"][0:1, :]).then_inc(bias_in, 16)
            with sp.Fori(0, MOD_TILES // 2) as n:
                for s in range(2):
                    sp.wait_ge(mod_pe[s], 1 + n)
                    sp.dma_start(ar(W[s], KT * WCOLS), a["wst"][2 * n + s]).then_inc(w_loaded[s], 16)
            MT = MOD_TILES // 2
            for s in range(2):
                sp.wait_ge(mod_pe[s], 1 + MT)
                sp.dma_start(ar(W[s], WSLOT), a["whd"][s]).then_inc(w_loaded[s], 16)
            for s in range(2):
                sp.wait_ge(mod_v[s], 1 + MT)
            sp.dma_start(modd[:, 0:MODN], modsb[:, :]).then_inc(mod_out, 16)
            for b in range(2):
                sp.dma_start(xtok[:, b, :], a["ctx"][0, b * P:b * P + P, :]).then_inc(x_in, 16)
                sp.dma_start(xtok[:, 2 + b, :], a["x"][0, b * P:b * P + P, :]).then_inc(x_in, 16)
            with sp.Fori(1, HEADS // 2) as n:
                for s in range(2):
                    sp.wait_ge(vproj, 2 * n + (s - 1))
                    sp.dma_start(ar(W[s], WSLOT), a["whd"][2 * n + s]).then_inc(w_loaded[s], 16)

            def ln_rows(layer, which, streams, base, blocks, src):
                chunk = 2 if which == 0 else 5
                at = (layer * CHUNKS + chunk) * D
                for s in streams:
                    sp.dma_start(ln_m[:, s, :], modd[s, at:at + D].partition_broadcast(P)).then_inc(ln_min, 16)
                for b in blocks:
                    sp.dma_start(ln_x[:, b, :], src(b)).then_inc(ln_res[b], 16)
                sp.dma_start(ln_g, a["ln_g"][layer, which].partition_broadcast(P)).then_inc(ln_in, 16)
                sp.dma_start(ln_b, a["ln_b"][layer, which].partition_broadcast(P)).then_inc(ln_in, 16)

            def peer_first(p):
                if p == 1:
                    for b in range(2, 4):
                        sp.dma_start(ln_x[:, b, :], xs[b]).then_inc(x_in, 16)
                for i in range(2):
                    tile(["wqa", "wqb", "wqc"][p], i)
                sp.dma_start(kp.rearrange("p m n -> p (m n)"), a["keys"][PASS_LAYER[p]]).then_inc(keys_in, 16)

            def ln_store(base, blocks, dst):
                for k, b in enumerate(blocks):
                    sp.wait_ge(ln_o, base + k + 1)
                    sp.dma_start(dst(b), ln_x[:, b, :]).then_inc(x_out, 16)

            def x_of(b):
                return a["ctx"][0, b * P:b * P + P, :] if b < 2 else a["x"][0, (b - 2) * P:(b - 1) * P, :]

            def peer(p):
                layer, s = PASS_LAYER[p], PASS_S[p]
                blocks = [2 * s, 2 * s + 1]
                names = ["wqa", "wqb", "wqc"][p]
                for i in range(2, 4):
                    tile(names, i)
                if p < 2:
                    cols = slice(p * MOD_PART * WCOLS, (p + 1) * MOD_PART * WCOLS)
                    for x in range(2):
                        sp.dma_start(mod1[x:x + 1, :], a["mod_b"][1:2, cols]).then_inc(mod1_b, 16)
                    for i in range(MOD_PART):
                        tile("mod1" + "ab"[p], i)
                    sp.wait_ge(mod1_v, MOD_PART * (p + 1))
                    sp.dma_start(modd[:, MODN + cols.start:MODN + cols.stop], mod1).then_inc(mod1_out, 16)
                for q in range(2):
                    sp.wait_ge(g_pe[q], 1 + 2 * (PT_ // 16) * (p + 1))
                    sp.wait_ge(u_l[q], 1 + p * PAIRS)
                    sp.dma_start(u_raw[:, q, :], a["u"][layer, q]).then_inc(u_in[q], 16)
                    sp.wait_ge(v_l[q], 1 + p * PAIRS)
                    sp.dma_start(v_raw[:, q, :], a["v"][layer, q]).then_inc(v_in[q], 16)
                with sp.Fori(1, PAIRS) as n:
                    for q in range(2):
                        j = 2 * n + q
                        sp.wait_ge(u_l[q], 1 + n + p * PAIRS)
                        sp.dma_start(u_raw[:, q, :], a["u"][layer, j]).then_inc(u_in[q], 16)
                        sp.wait_ge(v_l[q], 1 + n + p * PAIRS)
                        sp.dma_start(v_raw[:, q, :], a["v"][layer, j]).then_inc(v_in[q], 16)
                sp.wait_ge(y_ac[1], 1 + PAIRS * (p + 1))
                sp.wait_ge(x_out, 16 * LN_BASE[p])
                ln_rows(layer, 1, [s], LN_BASE[p], blocks, lambda b: xs[b])
                if p == 0:
                    peer_first(1)
                if p == 1:
                    sp.wait_ge(mod1_out, 32)
                    for b in range(2):
                        sp.dma_start(ln_x[:, b, :], xs[b]).then_inc(x_in, 16)
                    for i in range(2):
                        tile("qkv", i)
                if p < 2:
                    ln_store(LN_BASE[p], blocks, lambda b: xs[b])
                else:
                    ln_store(LN_BASE[p], blocks, lambda b: a["out"][0, (b - 2) * P:(b - 1) * P, :])

            for i in range(2):
                tile("wout0", i)
            sp.wait_ge(y_done, 1 + HEADS)
            sp.wait_ge(mod_out, 16)
            ln_rows(0, 0, [0, 1], 0, range(4), x_of)
            peer_first(0)
            ln_store(0, range(4), lambda b: xs[b])
            peer(0)
            peer(1)
            sp.dma_start(c1, a["const"][:, C_KEEP:C_ALL]).then_inc(swa_c, 16)
            tile("qkv", 2)
            for i in range(2):
                tile("wout1", i)
            sp.wait_ge(at_oc, 32)
            ln_rows(1, 0, [1], 8, [2, 3], lambda b: xs[b])
            peer_first(2)
            ln_store(8, [2, 3], lambda b: xs[b])
            peer(2)
            sp.wait_ge(x_out, 16 * 12)

        @block.tensor
        def _(pe):
            mm = nc.tensor.matmul
            in_hand(pe, ON_PE)

            def arrived(name, i):
                k = RING[(name, i)]
                pe.wait_ge(w_loaded[k % 2], 16 * (k // 2 + 1))
                return k % 2

            pe.wait_ge(const_in, 16)
            pe.wait_ge(cond_in, 80)
            nc.tensor.transpose(banks[2][:, 0:16], condraw, ident[0:16, 0:16])
            nc.tensor.transpose(banks[3][:, 0:24], lbraw, ident[0:24, 0:24]).then_inc(setup_t, 1)
            pe.wait_ge(cond_done, 1)
            with pe.Fori(0, MOD_TILES // 2) as n:
                for s in range(2):
                    pe.wait_ge(w_loaded[s], 16 * n + 16)
                    pe.wait_ge(mod_v[s], 1 + n)
                    for k in range(KT):
                        last = mm(banks[s][0:2, :], cond[:, :, k], wt(s)[:, k, :], start=(k == 0), stop=(k == KT - 1))
                    last.then_inc(mod_pe[s], 1)
            def mod_columns(rows, n, bank):
                for i in range(n):
                    last = nc.tensor.transpose(bank[:, 2 * i:2 * i + 2], rows[:, i * P:(i + 1) * P], ident[0:2, 0:2])
                last.then_inc(mod_t, 1)

            for s in range(2):
                pe.wait_ge(mod_v[s], 1 + MOD_TILES // 2)
            mod_columns(modsb, CHUNKS * KT, banks[6])

            def transpose_x(layer, need, src):
                pe.wait_ge(x_in, need)
                for k in range(KT):
                    if k >= 2:
                        pe.wait_ge(hT_done, 2 * (8 * layer + k - 1))
                    for b in range(NB):
                        last = nc.tensor.transpose(banks[k % 2][:, b * P:(b + 1) * P], src[:, b, k * P:(k + 1) * P], ident)
                    last.then_inc(xT_pe, 1)
                pe.wait_ge(hT_done, 16 * (layer + 1))

            transpose_x(0, 64, xtok)

            MT = MOD_TILES // 2

            def proj_piece(g, c, half):
                w_hi, w_lo = weight_parts(c % 2)
                if half == 0:
                    pe.wait_ge(hw_l, 4 * g + (c + 1))
                out = banks[c][:, :].rearrange("p (s t) -> p s t", s=2)
                for k in range(4 * half, 4 * half + 4):
                    for i, (w, x) in enumerate(((w_hi, hT_hi[:, :, k, :]), (w_hi, hT_lo[:, :, k, :]), (w_lo, hT_hi[:, :, k, :]))):
                        last = mm(out, w[:, k, :], x, start=(k == 0 and i == 0), stop=(k == KT - 1 and i == 2))
                if half:
                    last.then_inc(proj, 1)

            def value_piece(slot, b, final):
                for k in range(KT):
                    last = mm(banks[7][:, b * P:(b + 1) * P], hT[:, k, b * P:(b + 1) * P], wh(slot)[:, k, 4 * P:5 * P],
                              start=(k == 0), stop=(k == KT - 1))
                if final:
                    last.then_inc(vproj, 1)

            pe.wait_ge(hT_l, KT)
            for c in range(4):
                for half in range(2):
                    proj_piece(0, c, half)
            for b in range(NB):
                value_piece(0, b, b == NB - 1)

            def head(h, slot, more):
                for l in range(LEVELS):
                    if l == 0:
                        pe.wait_ge(init, h + 1)
                    if more:
                        proj_piece(h + 1, l // 2, l % 2)
                    if l == 0:
                        pe.wait_ge(y_done, h + 1)
                    if l == 1:
                        pe.wait_ge(ms_a, 1 + h)
                    if l >= 2:
                        pe.wait_ge(lvlcp, 8 * h + l - 1)
                    bank = banks[4 + l % 2]
                    for b in range(NB):
                        out = bank[:, b * P:(b + 1) * P]
                        if l == 0:
                            qb = hd(slot, O_Q + b * P, P)
                            mm(out, hd(slot, O_KD + b * P, P), qb, start=True, stop=False)
                            last = mm(out, hd(slot, O_KD + TOK + b * P, P), qb, start=False, stop=True)
                        else:
                            m = 1 << (l - 1)
                            if b == 0:
                                pe.wait_ge(kc_sb, 7 * h + l)
                            last = mm(out, kc[:, l % 2, b * P:(b + 1) * P], level_operand(slot, O_QD, m, b), start=True, stop=True)
                    last.then_inc(lvl, 1)
                pe.wait_ge(upd, 7 * h + 7)
                for d in range(2):
                    if d:
                        pe.wait_ge(lvlcp, 8 * h + 7)
                    for i in range(3):
                        b = CHAIN[3 * d + i]
                        last = nc.tensor.transpose(banks[6 - 2 * d][:, i * P:(i + 1) * P], hd(slot, O_KD + d * TOK + b * P, P), ident)
                    last.then_inc(kt_pe, 1)
                if more:
                    value_piece(1 - slot, 0, False)
                for d in range(2):
                    pe.wait_ge(kt_sb, 2 * h + d + 1)
                    if d == 0:
                        pe.wait_ge(lvlcp, 8 * h + 8)
                        pe.wait_ge(vsb, h + 1)
                    for i in range(3):
                        b = CHAIN[3 * d + i]
                        last = mm(banks[5 + d][:, i * P:(i + 1) * P], KTr[:, 3 * d + i, :], hd(slot, O_V + b * P, P), start=True, stop=True)
                    last.then_inc(ds, 1)
                    if more:
                        value_piece(1 - slot, 1 + d, False)
                for b in range(NB):
                    out = banks[4][:, b * P:(b + 1) * P]
                    terms = [(hd(slot, O_V + b * P, P), hd(slot, O_AT + b * P, P))]
                    if b:
                        terms.append((STr[:, b - 1, :], hd(slot, O_QD + TOK + b * P, P)))
                    if b != 1:
                        terms.append((STr[:, {0: 3, 3: 4, 2: 5}[b], :], hd(slot, O_QD + b * P, P)))
                    if b == 0:
                        pe.wait_ge(st_done, h + 1)
                    for i, (x, y) in enumerate(terms):
                        last = mm(out, x, y, start=(i == 0), stop=(i == len(terms) - 1))
                last.then_inc(o_pe, 1)
                if more:
                    value_piece(1 - slot, 3, True)
                pe.wait_ge(sq_done, h + 1)
                for b in range(NB):
                    last = mm(banks[5][:, b:b + 1], sqbuf[:, b * P:(b + 1) * P], mean_w[:, 0:1], start=True, stop=True)
                last.then_inc(ss_pe, 1)

            with pe.Fori(0, HEADS // 2 - 1) as n:
                head(2 * n, 0, True)
                head(2 * n + 1, 1, True)
            head(HEADS - 2, 0, True)
            head(HEADS - 1, 1, False)

            def mixer_out(name, oview, order):
                slots = [arrived(name, half) for half in range(2)]
                for b, half in order:
                    for k in range(KT):
                        last = mm(banks[2 * b + half][:, :], oview[:, k, b * P:(b + 1) * P], wt(slots[half])[:, k, :],
                                  start=(k == 0), stop=(k == KT - 1))
                    last.then_inc(y_pe, 1)

            for h in range(HEADS):
                pe.wait_ge(rdiag, h + 1)
                mm(banks[h % 4][:, :], mean_w, rmsdiag(h), start=True, stop=True).then_inc(rbc, 1)
            pe.wait_ge(onorm, HEADS)
            mixer_out("wout0", oT, WOUT_ORDER[0])

            def peer(p):
                layer, s = PASS_LAYER[p], PASS_S[p]
                if p == 1:
                    pe.wait_ge(x_in, 64 + 32)
                else:
                    pe.wait_ge(ln_o, [2, 0, 10][p])
                for k in range(KT):
                    if k >= 2:
                        pe.wait_ge(h1, 8 * p + k - 1)
                    for b in range(2):
                        last = nc.tensor.transpose(banks[k % 2][:, b * P:(b + 1) * P], ln_x[:, 2 * s + b, k * P:(k + 1) * P], ident)
                    last.then_inc(x1T, 1)
                pe.wait_ge(h1, 8 * p + 8)
                pe.wait_ge(hl, 8 * (p + 1))

                def query_unit(g):
                    i, m = g // 4, g % 4
                    if g == (0 if p == 0 else 4):
                        pe.wait_ge(ln_v, LN_BASE[p])
                    if m == 0 and i >= 2:
                        pe.wait_ge(pq_sb, 4 * p + i - 1)
                    pe.wait_ge(qw_l[m], 4 * p + i + 1)
                    w_hi, w_lo = weight_parts(m)
                    out = banks[(6 if i % 2 == 0 else 2) + m // 2][:, (m % 2) * PT_:(m % 2 + 1) * PT_]
                    n3 = 0
                    for k in range(KT):
                        for w, h in ((w_hi, h_hi), (w_hi, h_lo), (w_lo, h_hi)):
                            last = mm(out, w[:, k, :], h[:, k, :], start=(n3 == 0), stop=(n3 == 3 * KT - 1))
                            n3 += 1
                    last.then_inc(qw_pe[m], 1)

                def key_scores(i):
                    if i == 0:
                        pe.wait_ge(keys_in, 16 * (p + 1))
                    pe.wait_ge(pq_sb, 4 * p + i + 1)
                    for b in range(2):
                        if i:
                            pe.wait_ge(ps_sb, 2 * (4 * p + i - 1) + b + 1)
                        for m in range(4):
                            last = mm(banks[4 + b][:, m * NK:(m + 1) * NK], qp[:, m, b * P:(b + 1) * P], kp[:, 4 * i + m, :],
                                      start=True, stop=True)
                        last.then_inc(ps_pe, 1)

                for g in range(16):
                    query_unit(g)
                    if g % 4 == 0 and g:
                        key_scores(g // 4 - 1)
                key_scores(3)
                if p < 2:
                    for i in range(MOD_PART):
                        w = arrived("mod1" + "ab"[p], i)
                        if i >= 2:
                            pe.wait_ge(mod1_a, MOD_PART * p + i - 1)
                        for k in range(KT):
                            last = mm(banks[i % 2][0:2, :], cond[:, :, k], wt(w)[:, k, :], start=(k == 0), stop=(k == KT - 1))
                        last.then_inc(mod1_pe, 1)
                    pe.wait_ge(mod1_a, MOD_PART * (p + 1))
                    pe.wait_ge(mod1_v, MOD_PART * (p + 1))
                    mod_columns(mod1, CHUNKS * KT // 2, banks[0])
                for b in range(2):
                    pe.wait_ge(jch, 2 * p + b + 1)
                    for c in range(3):
                        last = nc.tensor.transpose(banks[6 + b][:, c * P:(c + 1) * P], ijt[:, c, :], ident)
                    last.then_inc(ch_t, 1)
                if p < 2:
                    pe.wait_ge(mod_c, p + 2)
                with pe.Fori(0, PT_ // 16) as n:
                    for q in range(2):
                        N = n + p * (PT_ // 16)
                        pe.wait_ge(onehot[q], N + 1)
                        pe.wait_ge(colw[q], N + 1)
                        pe.wait_ge(g_sb[q], 1 + 2 * N)
                        for half in range(2):
                            for t in range(4 * half, 4 * half + 4):
                                out = banks[2 * q + half][:, (t % 4) * NK:(t % 4 + 1) * NK]
                                last = mm(out, onehots(u_raw, q)[:, t, :], onehots(v_raw, q)[:, t, :], start=True, stop=True)
                            last.then_inc(g_pe[q], 1)

                def scores(q, N):
                    pe.wait_ge(u_l[q], 1 + N + 1)
                    pe.wait_ge(s_act[q], N)
                    n3 = 0
                    for k in range(KT):
                        col = slice(k * P, (k + 1) * P)
                        for w, h in ((u_hi, h_hi), (u_hi, h_lo), (u_lo, h_hi)):
                            last = mm(banks[q][:, 0:PT_], w[:, q, col], h[:, k, :], start=(n3 == 0), stop=(n3 == 3 * KT - 1))
                            n3 += 1
                    last.then_inc(s_pe[q], 1)

                def outputs(q, N, first, final):
                    pe.wait_ge(p_l[q], 1 + N + 1)
                    pe.wait_ge(v_l[q], 1 + N + 1)
                    for b in range(2):
                        for half in range(2):
                            col = slice(half * 512, half * 512 + 512)
                            for i, (x, y) in enumerate(((p_hi, v_hi), (p_hi, v_lo), (p_lo, v_hi))):
                                last = mm(banks[2 + 2 * b + half][:, :], x[:, q, b * P:(b + 1) * P], y[:, q, col],
                                          start=(first and i == 0), stop=(final and i == 2))
                    last.then_inc(y_ac[q], 1)

                N0 = p * PAIRS
                scores(0, N0)
                pe.wait_ge(g_sb[1], 1 + 2 * (PT_ // 16) * (p + 1))
                scores(1, N0)
                outputs(0, N0, True, False)
                with pe.Fori(0, PAIRS - 1) as n:
                    scores(0, n + N0 + 1)
                    outputs(1, n + N0, False, False)
                    scores(1, n + N0 + 1)
                    outputs(0, n + N0 + 1, False, False)
                outputs(1, N0 + PAIRS - 1, False, True)

            peer(0)
            peer(1)
            pe.wait_ge(ln_o, 8)
            transpose_x(1, 64 + 32 + 32, ln_x)

            n_qk = 0
            for i in range(2):
                w = arrived("qkv", i)
                for m in range(4):
                    if n_qk >= 2:
                        pe.wait_ge(rope, n_qk - 1)
                    for k in range(KT):
                        last = mm(banks[n_qk % 2][:, 0:SEQ], wt(w)[:, k, m * P:(m + 1) * P], hT[:, k, CTX:TOK],
                                  start=(k == 0), stop=(k == KT - 1))
                    last.then_inc(qk_pe, 1)
                    pe.wait_ge(qk_sb, n_qk + 1)
                    if n_qk == 0:
                        pe.wait_ge(swa_c, 16)
                    mm(banks[2 + n_qk % 2][:, 0:SEQ], rot, rawq[:, n_qk % 2, 0:SEQ], start=True, stop=True).then_inc(rot_pe, 1)
                    n_qk += 1
            w = arrived("qkv", 2)
            for m in range(2):
                pe.wait_ge(rope, n_qk - 1)
                for k in range(KT):
                    last = mm(banks[n_qk % 2][:, :], wt(w)[:, k, m * P:(m + 1) * P], hT[:, k, :], start=(k == 0), stop=(k == KT - 1))
                last.then_inc(qk_pe, 1)
                pe.wait_ge(qk_sb, n_qk + 1)
                mm(banks[2 + n_qk % 2][:, 0:SEQ], rot, rawq[:, n_qk % 2, CTX:TOK], start=True, stop=True).then_inc(rot_pe, 1)
                n_qk += 1
            for b in range(NB):
                for k in range(KT):
                    last = mm(banks[4 + b // 2][:, (b % 2) * 256:(b % 2 + 1) * 256], hT[:, k, b * P:(b + 1) * P], wt(w)[:, k, 256:512],
                              start=(k == 0), stop=(k == KT - 1))
                last.then_inc(sv_pe, 1)
            pe.wait_ge(rope, 10)
            pe.wait_ge(sv_sb, 1)

            def att_scores(i):
                j, half, b = i // 4, i % 2, (i // 2) % 2
                bank = banks[i % 2]
                rows = slice(half * SWA_D, (half + 1) * SWA_D)
                if i >= 2:
                    pe.wait_ge(at_e, i - 1)
                mm(bank[:, :], q1[rows, j, b * P:(b + 1) * P], k1[rows, j // 4, :], start=True, stop=False)
                far = slice(CTX + P, TOK) if b == 0 else slice(CTX, CTX + P)
                mm(bank[:, far], ident, wmask[:, b, :], start=False, stop=True).then_inc(at_s, 1)

            att_scores(0)
            att_scores(1)
            for i in range(32):
                j, half, b = i // 4, i % 2, (i // 2) % 2
                pe.wait_ge(at_d, i + 1)
                pe.wait_ge(at_e, i + 1)
                if i >= 2:
                    pe.wait_ge(at_tc, i - 1)
                for c in range(4):
                    last = mm(banks[2 + i % 2][:, c * P:(c + 1) * P], prb[:, i % 2, c * P:(c + 1) * P], diag[:, i % 2, :],
                              start=True, stop=True)
                last.then_inc(at_t, 1)
                if i < 30:
                    att_scores(i + 2)
                pe.wait_ge(at_tc, i + 1)
                if i >= 2:
                    pe.wait_ge(at_oc, i - 1)
                kv = 2 * (j // 4) + half
                for c in range(4):
                    last = mm(banks[4 + i % 2][half * SWA_D:(half + 1) * SWA_D, 0:P], v1[:, c, kv * SWA_D:(kv + 1) * SWA_D],
                              prT[:, i % 2, c * P:(c + 1) * P], start=(c == 0), stop=(c == 3))
                last.then_inc(at_o, 1)
            pe.wait_ge(at_oc, 32)
            mixer_out("wout1", o1, WOUT_ORDER[1])
            peer(2)

        @block.scalar
        def _(act):
            af_ = nc.scalar.activation
            in_hand(act, ON_ACT)
            act.wait_ge(setup_t, 1)
            af_(cond.rearrange("p s k -> p (s k)"), banks[2][:, 0:16], ACT.Sigmoid).then_inc(setup_a, 1)
            act.wait_ge(setup_v, 1)
            af_(lgt, lgt, ACT.Exp).then_inc(setup_a, 1)

            def modulate_x(layer):
                act.wait_ge(mod_c, 1 + 2 * layer)
                for k in range(KT):
                    act.wait_ge(xT_pe, 8 * layer + k + 1)
                    for s in range(2):
                        cols = slice(s * CTX, (s + 1) * CTX)
                        af_(hT[:, k, cols], banks[k % 2][:, cols], ACT.Identity,
                            scale=mcol(layer, s, 1, k), bias=mcol(layer, s, 0, k)).then_inc(hT_done, 1)
                    if layer == 0:
                        act.wait_ge(hT_done, 2 * (k + 1))
                        af_(hT_hi[:, :, k, :], hT[:, k, :].rearrange("p (s t) -> p s t", s=2), ACT.Copy).then_inc(hT_h, 1)

            MT = MOD_TILES // 2

            def high_w(slot, c):
                af_(weight_parts(c % 2)[0], wh(slot)[:, :, c * P:(c + 1) * P], ACT.Copy).then_inc(hw_h, 1)

            act.wait_ge(w_loaded[0], 16 * (MT + 1))
            for c in range(2):
                high_w(0, c)
            modulate_x(0)

            def sigmoid(g, slot, c):
                off = (O_Q, coff(0) + TOK, coff(0), O_G)[c]
                act.wait_ge(proj, 4 * g + c + 1)
                af_(hd(slot, off, TOK), banks[c][:, :], ACT.Sigmoid).then_inc(sig, 1)

            def values(g, slot):
                act.wait_ge(vproj, g + 1)
                af_(hd(slot, O_V, TOK), banks[7][:, :], ACT.Copy).then_inc(vsb, 1)

            def head(h, slot, more, fill=None):
                if more:
                    high_w(1 - slot, 1)
                for l in range(1, LEVELS):
                    if l == 1:
                        act.wait_ge(init, h + 1)
                    else:
                        act.wait_ge(upd, 7 * h + l - 1)
                    act.wait_ge(lvl, 1 + 8 * h + (l - 1 if l > 2 else 0))
                    m = 1 << (l - 1)
                    af_(kc[:, l % 2, :].rearrange("p (n w r) -> p n w r", w=2, r=m),
                        hap(slot, O_KD, (2 * m, TOK // (2 * m)), (TOK + m, 2), (1, m)), ACT.Copy).then_inc(kc_sb, 1)
                    if more and l in (2, 4):
                        high_w(1 - slot, l // 2 + 1)
                    if more and l % 2:
                        if l == 1:
                            act.wait_ge(y_done, h + 1)
                        sigmoid(h + 1, 1 - slot, l // 2)
                if fill is not None:
                    act.wait_ge(w_loaded[slot], fill)
                    high_w(slot, 0)
                for d in range(2):
                    act.wait_ge(kt_pe, 2 * h + d + 1)
                    act.wait_ge(ds, 1 + 2 * h)
                    af_(KTr[:, 3 * d:3 * d + 3, :].rearrange("p c k -> p (c k)"), banks[6 - 2 * d][:, 0:3 * P], ACT.Copy).then_inc(kt_sb, 1)
                act.wait_ge(o_pe, 1 + h + 1)
                act.wait_ge(ss_pe, 1 + h)
                af_(sqbuf, banks[4][:, :], ACT.Square).then_inc(sq_done, 1)
                if more:
                    values(h + 1, 1 - slot)
                act.wait_ge(ss_pe, 1 + h + 1)
                dst = stat[:, h * NB:(h + 1) * NB] if isinstance(h, int) else stat[:, bass.ds(h * NB, NB)]
                af_(dst, banks[5][:, 0:NB], ACT.Copy, bias=RMS_EPS).then_inc(ms_a, 1)

            act.wait_ge(mod_out, 16)
            for c in range(4):
                sigmoid(0, 0, c)
                if c < 2:
                    high_w(0, c + 2)
            act.wait_ge(w_loaded[1], 16 * (MT + 1))
            high_w(1, 0)
            values(0, 0)
            with act.Fori(0, HEADS // 2 - 1) as n:
                head(2 * n, 0, True, 16 * n + 16 * (MT + 2))
                head(2 * n + 1, 1, True, 16 * n + 16 * (MT + 2))
            head(HEADS - 2, 0, True)
            head(HEADS - 1, 1, False)

            def peer(p):
                layer, s = PASS_LAYER[p], PASS_S[p]

                def high_w(g):
                    if g >= 16:
                        return
                    i, m = g // 4, g % 4
                    k = RING[(["wqa", "wqb", "wqc"][p], i)]
                    if m == 0:
                        act.wait_ge(w_loaded[k % 2], 16 * (k // 2 + 1))
                    if i:
                        act.wait_ge(qw_pe[m], 4 * p + i)
                    af_(weight_parts(m)[0], wt(k % 2)[:, :, m * P:(m + 1) * P], ACT.Copy).then_inc(qw_h[m], 1)

                for g in range(4):
                    high_w(g)
                for k in range(KT):
                    act.wait_ge(x1T, 8 * p + k + 1)
                    af_(hf[:, k, :], banks[k % 2][:, 0:PT_], ACT.Identity,
                        scale=mcol(layer, s, 4, k), bias=mcol(layer, s, 3, k)).then_inc(h1, 1)
                for k in range(KT):
                    if k == 0:
                        act.wait_ge(h1, 8 * p + 8)
                    af_(h_hi[:, k, :], hf[:, k, :], ACT.Copy).then_inc(hh, 1)

                for i in range(4):
                    for g in range(4 * i + 4, 4 * i + 7):
                        high_w(g)
                    act.wait_ge(qw_pe[3], 4 * p + i + 1)
                    act.wait_ge(ps_pe, 2 * (4 * p + i))
                    for half in range(2):
                        ins = af_(qp[:, 2 * half:2 * half + 2, :].rearrange("p c t -> p (c t)"),
                                  banks[(6 if i % 2 == 0 else 2) + half][:, :], ACT.Copy)
                    ins.then_inc(pq_sb, 1)
                    high_w(4 * i + 7)
                    for b in range(2):
                        act.wait_ge(ps_pe, 2 * (4 * p + i) + b + 1)
                        af_(sc[:, b, 4 * i:4 * i + 4, :].rearrange("p m n -> p (m n)"), banks[4 + b][:, :], ACT.Copy).then_inc(ps_sb, 1)

                def mod1_copy(i):
                    act.wait_ge(mod1_pe, MOD_PART * p + i + 1)
                    if i >= 2:
                        act.wait_ge(mod1_v, MOD_PART * p + i - 1)
                    af_(mod1_t[i % 2], banks[i % 2][0:2, :], ACT.Copy).then_inc(mod1_a, 1)

                if p < 2:
                    mod1_copy(0)
                    mod1_copy(1)
                act.wait_ge(ex_v, p + 1)
                bsf = bs.rearrange("p b h k -> p (b h k)")
                af_(bsf, bsf, ACT.Exp).then_inc(ex_a, 1)
                if p < 2:
                    for i in range(2, MOD_PART):
                        mod1_copy(i)
                for b in range(2):
                    act.wait_ge(ch_t, 2 * p + b + 1)
                    ins = af_(ijw[:, 0:3, b * P:(b + 1) * P], banks[6 + b][:, 0:3 * P].rearrange("p (c t) -> p c t", c=3), ACT.Copy)
                    ins.then_inc(ch_sb, 1)

                def weigh(q, n):
                    act.wait_ge(coleq[q], n + p * (PT_ // 16) + 1)
                    for t in range(ACT_T):
                        at = 16 * n + (8 * q + t)
                        w_t = ijw[:, 2, at:at + 1] if isinstance(n, int) else ijw[:, 2, bass.ds(at, 1)]
                        ins = af_(onehots(v_raw, q)[:, t, :], onehots(v_raw, q)[:, t, :], ACT.Copy, scale=w_t)
                    ins.then_inc(colw[q], 1)

                def store(q, n):
                    for half in range(2):
                        act.wait_ge(g_pe[q], 1 + 2 * (n + p * (PT_ // 16)) + half + 1)
                        t0 = 16 * n + 8 * q + 4 * half
                        dst = gate[:, t0:t0 + 4, :] if isinstance(n, int) else gate[:, bass.ds(t0, 4), :]
                        af_(dst, banks[2 * q + half][:, :].rearrange("p (t j) -> p t j", t=4), ACT.Copy).then_inc(g_sb[q], 1)

                if p < 2:
                    act.wait_ge(mod1_out, 16 * (p + 1))
                weigh(0, 0)
                with act.Fori(0, PT_ // 16 - 1) as n:
                    weigh(1, n)
                    store(0, n)
                    weigh(0, n + 1)
                    store(1, n)
                weigh(1, PT_ // 16 - 1)
                store(0, PT_ // 16 - 1)
                store(1, PT_ // 16 - 1)

                def high_u(q, N):
                    act.wait_ge(u_in[q], 16 * N + 16)
                    act.wait_ge(s_pe[q], N)
                    af_(u_hi[:, q, :], u_raw[:, q, :], ACT.Copy).then_inc(u_h[q], 1)

                def step(q, N, nq, nN, more=True):
                    if more:
                        high_u(nq, nN)
                    act.wait_ge(s_pe[q], N + 1)
                    act.wait_ge(p_do[q], 1 + N)
                    af_(act_s[:, q, :], banks[q][:, 0:PT_], ACT.Gelu_apprx_tanh).then_inc(s_act[q], 1)
                    act.wait_ge(v_in[q], 16 * N + 16)
                    act.wait_ge(y_ac[q], 1 + N)
                    af_(v_hi[:, q, :], v_raw[:, q, :], ACT.Copy).then_inc(v_h[q], 1)
                    act.wait_ge(p_do[q], 1 + N + 1)
                    af_(p_hi[:, q, :], prod[:, q, :], ACT.Copy).then_inc(p_h[q], 1)

                N0 = p * PAIRS
                G16 = PT_ // 16
                for q in range(2):
                    act.wait_ge(g_pe[q], 1 + 2 * G16 * (p + 1))
                high_u(0, N0)
                step(0, N0, 1, N0)
                with act.Fori(0, PAIRS - 1) as n:
                    step(1, n + N0, 0, n + N0 + 1)
                    step(0, n + N0 + 1, 1, n + N0 + 1)
                step(1, N0 + PAIRS - 1, 0, 0, more=False)

            peer(0)
            peer(1)
            modulate_x(1)
            for i in range(10):
                act.wait_ge(qk_pe, i + 1)
                if i >= 2:
                    act.wait_ge(rope, i - 1)
                n = SEQ if i < 8 else TOK
                af_(rawq[:, i % 2, 0:n], banks[i % 2][:, 0:n], ACT.Copy).then_inc(qk_sb, 1)
            act.wait_ge(sv_pe, 4)
            for i in range(2):
                ins = af_(v1[:, 2 * i:2 * i + 2, :].rearrange("p b c -> p (b c)"), banks[4 + i][:, :], ACT.Copy)
            ins.then_inc(sv_sb, 1)

            def exponentials(i):
                st = stat[:, (i % 4) * 20:(i % 4) * 20 + 20]
                act.wait_ge(at_m, i + 1)
                if i == 0:
                    act.wait_ge(rope, 10)
                if i >= 2:
                    act.wait_ge(at_t, i - 1)
                af_(prb[:, i % 2, :], banks[i % 2][:, :], ACT.Exp, scale=SWA_SCALE, bias=st[:, 2:3], accum_out=st[:, 3:4])
                af_(st[:, 4:5], st[:, 5:6], ACT.Exp, bias=st[:, 2:3]).then_inc(at_e, 1)

            exponentials(0)
            exponentials(1)
            for i in range(32):
                act.wait_ge(at_t, i + 1)
                if i >= 2:
                    act.wait_ge(at_o, i - 1)
                af_(prT[:, i % 2, :], banks[2 + i % 2][:, :], ACT.Copy).then_inc(at_tc, 1)
                if i < 30:
                    exponentials(i + 2)
            peer(2)

        @block.vector
        def _(dve):
            V = nc.vector
            st_ = Steps(dve, dstep)
            link, did = st_.link, st_.did
            in_hand(dve, ON_DVE)
            V.memset(neg_half, -0.5)
            dve.wait_ge(setup_a, 1)
            V.tensor_tensor(cond.rearrange("p s k -> p (s k)"), banks[2][:, 0:16], cond.rearrange("p s k -> p (s k)"), ALU.mult).then_inc(cond_done, 1)
            lgf = banks[3][:, 0:24].rearrange("p (r h) -> p r h", r=3)
            link(V.tensor_copy(lgt, lgf))
            link(V.tensor_tensor(lb, lgt[:, 0, :], lgt[:, 1, :], ALU.max))
            link(V.tensor_tensor(lb, lb, lgt[:, 2, :], ALU.max))
            V.tensor_tensor(lgt, lgt, lb.unsqueeze(1).broadcast_to([P, 3, HEADS]), ALU.subtract).then_inc(setup_v, 1)
            dve.wait_ge(setup_a, 2)
            link(V.tensor_tensor(lb, lgt[:, 0, :], lgt[:, 1, :], ALU.add))
            link(V.tensor_tensor(lb, lb, lgt[:, 2, :], ALU.add))
            link(V.reciprocal(lb, lb))
            link(V.tensor_tensor(lb, lb, lgt[:, 0, :], ALU.mult))
            link(V.tensor_scalar(omlb, lb, -1.0, 1.0, ALU.mult, ALU.add))
            dve.wait_ge(lvlmask_in, 16)
            V.tensor_copy(lvlmask.rearrange("p l t -> p (l t)"), lvlraw)
            dve.wait_ge(bias_in, 32)
            with dve.Fori(0, MOD_TILES // 2) as n:
                for s in range(2):
                    dve.wait_ge(mod_pe[s], 1 + n + 1)
                    row = modsb[:, bass.ds((2 * n + s) * WCOLS, WCOLS)]
                    V.tensor_tensor(row, banks[s][0:2, :], row, ALU.add).then_inc(mod_v[s], 1)

            def low_w(g, slot, c):
                hi, lo = weight_parts(c % 2)
                dve.wait_ge(hw_h, 4 * g + (c + 1))
                V.tensor_tensor(lo, wh(slot)[:, :, c * P:(c + 1) * P], hi, ALU.subtract).then_inc(hw_l, 1)

            for c in range(2):
                low_w(0, 0, c)

            def mod_columns(l, c0, nc_, bank, nth):
                dve.wait_ge(mod_t, nth)
                m = modcol[:, l, c0 * 2 * KT:(c0 + nc_) * 2 * KT]
                link(V.tensor_copy(m, bank[:, 0:nc_ * 2 * KT]))
                c = m.rearrange("p (c n) -> p c n", c=nc_)[:, 1::3, :]
                V.tensor_scalar(c, c, 1.0, None, ALU.add).then_inc(mod_c, 1)

            mod_columns(0, 0, CHUNKS, banks[6], 1)
            link(V.tensor_scalar(ng, ng, float(P), None, ALU.mult))
            V.memset(stat, 0.0).then_inc(y_done, 1)

            def scale_head(g, slot):
                dve.wait_ge(sig, 4 * g + 4)
                dve.wait_ge(proj, 4 * g + 4)
                q = hd(slot, O_Q, TOK)
                f2 = hd(slot, coff(0), 2 * TOK)
                did(V.tensor_tensor(q, banks[0][:, :], q, ALU.mult))
                gg = hd(slot, O_G, TOK)
                did(V.tensor_tensor(gg, banks[3][:, :], gg, ALU.mult))
                h1_, l1_ = (omlb[:, bass.ds(g, 1)], lb[:, bass.ds(g, 1)])
                did(V.tensor_scalar(f2, f2, h1_, l1_, ALU.mult, ALU.add))
                st_.wait()
                for d in range(2):
                    did(V.tensor_scalar(hd(slot, O_KD + d * TOK, TOK), hd(slot, coff(0) + (1 - d) * TOK, TOK), -1.0, 1.0, ALU.mult, ALU.add))
                V.tensor_tensor(hap(slot, O_QD, (TOK, 2), (1, TOK)), hap(slot, coff(0), (TOK, 2), (1, TOK)),
                                hap(slot, O_Q, (0, 2), (1, TOK)), ALU.mult).then_inc(init, 1)

            def levels(h, slot, more, more2):
                if more:
                    low_w(h + 1, 1 - slot, 1)
                at = hd(slot, O_AT, TOK).rearrange("p (b t) -> p b t", b=NB)
                for l in range(LEVELS):
                    dve.wait_ge(lvl, 1 + 8 * h + l + 1)
                    src = banks[4 + l % 2][:, :].rearrange("p (b t) -> p b t", b=NB)
                    if l == 0:
                        V.tensor_copy(at, src).then_inc(lvlcp, 1)
                        continue
                    dve.wait_ge(lvlcp, 8 * h + l)
                    k, m = l - 1, 1 << (l - 1)
                    ns, blocks = TOK // m, TOK // (2 * m)
                    qv = hap(slot, O_QD, (2 * m, blocks), (TOK + m, 2), (1, m))
                    kv = hap(slot, O_KD, (2 * m, blocks), (TOK + m, 2), (1, m))
                    cq = hap(slot, coff(k) + 1, (2, blocks), (ns - 1, 2), (0, m))
                    ck = hap(slot, coff(k) + ns + 1, (2, blocks), (-(ns + 1), 2), (0, m))
                    if l == 1:
                        dve.wait_ge(init, h + 1)
                    else:
                        dve.wait_ge(upd, 7 * h + l - 1)
                    V.tensor_tensor(hap(slot, coff(k + 1), (1, 2 * blocks)), hap(slot, coff(k), (2, 2 * blocks)), hap(slot, coff(k) + 1, (2, 2 * blocks)), ALU.mult)
                    V.tensor_tensor(qv, qv, cq, ALU.mult)
                    V.tensor_tensor(kv, kv, ck, ALU.mult).then_inc(upd, 1)
                    V.copy_predicated(at, lvlmask[:, l, :].unsqueeze(1).broadcast_to([P, NB, P]), src).then_inc(lvlcp, 1)
                    if more and l in (2, 4):
                        low_w(h + 1, 1 - slot, l // 2 + 1)
                if more2:
                    low_w(h + 2, slot, 0)

            def states(h, slot):
                decay = lambda d, b: hd(slot, coff(7) + 4 * (1 - d) + b, 1)
                dve.wait_ge(o_pe, 1 + h)
                dve.wait_ge(upd, 7 * h + 7)
                for d in range(2):
                    dve.wait_ge(ds, 1 + 2 * h + d + 1)
                    for i in range(3):
                        src = banks[5 + d][:, i * P:(i + 1) * P]
                        if i == 0:
                            ins = V.tensor_copy(STr[:, 3 * d, :], src)
                        else:
                            ins = V.scalar_tensor_tensor(STr[:, 3 * d + i, :], STr[:, 3 * d + i - 1, :], decay(d, CHAIN[3 * d + i]), src, ALU.mult, ALU.add)
                        if d == 1 and i == 2:
                            ins.then_inc(st_done, 1)
                        else:
                            link(ins)

            def finish(h, slot):
                dve.wait_ge(sq_done, h + 1)
                V.scalar_tensor_tensor(arena[:, bass.ds(A_OT + h * TOK, TOK)] if not isinstance(h, int) else oT[:, h, :],
                                       banks[4][:, :], ng, hd(slot, O_G, TOK), ALU.mult, ALU.mult).then_inc(y_done, 1)

            def head(h, slot, more, more2=True):
                levels(h, slot, more, more2)
                states(h, slot)
                if more:
                    scale_head(h + 1, 1 - slot)
                finish(h, slot)

            for k in range(KT):
                dve.wait_ge(hT_h, k + 1)
                V.tensor_tensor(hT_lo[:, :, k, :], hT[:, k, :].rearrange("p (s t) -> p s t", s=2),
                                hT_hi[:, :, k, :], ALU.subtract).then_inc(hT_l, 1)
            for c in range(2, 4):
                low_w(0, 0, c)
            low_w(1, 1, 0)
            scale_head(0, 0)
            PER = 2 * (5 + 5)
            with dve.Fori(0, HEADS // 2 - 1) as n:
                st_.enter(n, PER)
                head(2 * n, 0, True)
                head(2 * n + 1, 1, True)
            st_.leave(HEADS // 2 - 1)
            head(HEADS - 2, 0, True, False)
            head(HEADS - 1, 1, False, False)
            dve.wait_ge(rms_p, 1)
            for h in range(HEADS):
                if h >= 2:
                    dve.wait_ge(rbc, h - 1)
                V.tensor_tensor(rmsdiag(h).rearrange("p (b t) -> p b t", b=NB), ident.unsqueeze(1).broadcast_to([P, NB, P]),
                                stat[:, h * NB:(h + 1) * NB].unsqueeze(2).broadcast_to([P, NB, P]), ALU.mult).then_inc(rdiag, 1)
                if h:
                    dve.wait_ge(rbc, h)
                    V.tensor_tensor(oT[:, h - 1, :], banks[(h - 1) % 4][:, :], oT[:, h - 1, :], ALU.mult).then_inc(onorm, 1)
            dve.wait_ge(rbc, HEADS)
            V.tensor_tensor(oT[:, HEADS - 1, :], banks[(HEADS - 1) % 4][:, :], oT[:, HEADS - 1, :], ALU.mult).then_inc(onorm, 1)

            def norms(call, base, blocks, bank0, stream, y_need=None):
                dve.wait_ge(ln_min, 16 * (call + 2))

                def front(i, b):
                    st = stat[:, (i % 4) * 20:(i % 4) * 20 + 20]
                    if y_need:
                        dve.wait_ge(y_pe, y_need[i])
                    for half in range(2):
                        cols = slice(512 * half, 512 * half + 512)
                        did(V.tensor_tensor(ln_t[:, i % 4, cols], banks[bank0 + 2 * i + half][:, :], ln_m[:, stream(b), cols], ALU.mult))
                    dve.wait_ge(ln_res[b], [16, 32, 32, 48, 64][call])
                    st_.wait()
                    link(V.scalar_tensor_tensor(ln_x[:, b, :], ln_x[:, b, :], ALPHA, ln_t[:, i % 4, :], ALU.mult, ALU.add))
                    for half in range(2):
                        did(V.bn_stats(st[:, 6 * half:6 * half + 6], ln_x[:, b, 512 * half:512 * half + 512]))
                    st_.wait()
                    link(V.bn_aggr(st[:, 12:14], st[:, 0:12]))
                    link(V.tensor_scalar(st[:, 15:16], st[:, 12:13], -1.0, None, ALU.mult))
                    V.tensor_scalar(st[:, 13:14], st[:, 13:14], LN_EPS, None, ALU.add).then_inc(ln_v, 1)

                def back(i, b):
                    st = stat[:, (i % 4) * 20:(i % 4) * 20 + 20]
                    if i == 0:
                        dve.wait_ge(ln_in, 32 * (call + 1))
                    link(V.scalar_tensor_tensor(ln_t[:, i % 4, :], ln_x[:, b, :], st[:, 15:16], ln_g, ALU.add, ALU.mult))
                    dve.wait_ge(ln_p, base + i + 1)
                    V.scalar_tensor_tensor(ln_x[:, b, :], ln_t[:, i % 4, :], st[:, 14:15], ln_b, ALU.mult, ALU.add).then_inc(ln_o, 1)

                for i in range(0, len(blocks), 2):
                    front(i, blocks[i])
                    front(i + 1, blocks[i + 1])
                    back(i, blocks[i])
                    back(i + 1, blocks[i + 1])

            norms(0, 0, list(range(4)), 0, lambda b: b // 2, Y_BLOCK[0])

            def top16(rows):
                stages = (lambda v, i, x: V.max(v[:, 0:8], x),
                          lambda v, i, x: V.max_index(i[:, 0:8], v[:, 0:8], x),
                          lambda v, i, x: V.match_replace(x, v[:, 0:8], x, LOWEST),
                          lambda v, i, x: V.max(v[:, 8:16], x),
                          lambda v, i, x: V.max_index(i[:, 8:16], v[:, 8:16], x))
                for stage in stages:
                    for v, i, x in rows:
                        did(stage(v, i, x))
                    st_.wait()

            def peer(p):
                layer, s = PASS_LAYER[p], PASS_S[p]
                for k in range(KT):
                    dve.wait_ge(hh, 8 * p + k + 1)
                    V.tensor_tensor(h_lo[:, k, :], hf[:, k, :], h_hi[:, k, :], ALU.subtract).then_inc(hl, 1)
                dve.wait_ge(x_out, 16 * LN_BASE[p])
                siu = si.bitcast(U32)
                biu = bi.bitcast(U32)
                for i in range(4):
                    for b in range(2):
                        dve.wait_ge(ps_sb, 2 * (4 * p + i) + b + 1)
                        top16([(sv[:, b, m, :], siu[:, b, m, :], sc[:, b, m, :]) for m in range(4 * i, 4 * i + 4)])
                        svh = sv[:, b, 4 * i:4 * i + 4, :].rearrange("p (h c) k -> p h c k", c=2)
                        for at, a0, na, w in PAIR_SETS:
                            did(V.tensor_tensor(cand[:, b, :, at:at + na * w].rearrange("p h (a w) -> p h a w", w=w),
                                                svh[:, :, 0, a0:a0 + na].unsqueeze(3).broadcast_to([P, 2, na, w]),
                                                svh[:, :, 1, 0:w].unsqueeze(2).broadcast_to([P, 2, na, w]), ALU.add))
                    st_.wait()
                    top16([(bs[:, b, 2 * i + h, :], biu[:, b, 2 * i + h, :], cand[:, b, h, :])
                           for b in range(2) for h in range(2)])
                bsf, gsf = bs.rearrange("p b h k -> p (b h) k"), gsums.rearrange("p b h -> p (b h)")
                spread = gsf.unsqueeze(2).broadcast_to([P, 2 * PH, TOPK])
                link(V.tensor_copy(gsf, bsf[:, :, 0]))
                V.tensor_tensor(bsf, bsf, spread, ALU.subtract).then_inc(ex_v, 1)
                places = biu.rearrange("p b h k -> p (b h k)")
                did(V.tensor_scalar(ba.bitcast(U32), places, 3, None, ALU.logical_shift_right))
                link(V.tensor_scalar(bb.bitcast(U32), places, 2, None, ALU.logical_shift_right))
                did(V.tensor_copy(bf, places))
                did(V.tensor_copy(ba, ba.bitcast(U32)))
                link(V.tensor_copy(bb, bb.bitcast(U32)))
                link(V.tensor_scalar(af, ba, 1.0, 0.0, ALU.subtract, ALU.max))
                link(V.scalar_tensor_tensor(af, bb, 6.0, af, ALU.subtract, ALU.max))
                link(V.scalar_tensor_tensor(af, bf, 48.0, af, ALU.subtract, ALU.max))
                did(V.tensor_scalar(ba, af, 8.0, 8.0, ALU.mult, ALU.add))
                link(V.tensor_scalar(bb, af, 4.0, 24.0, ALU.mult, ALU.add))
                link(V.scalar_tensor_tensor(ba, af, 16.0, ba, ALU.mult, ALU.min))
                link(V.tensor_tensor(ba, ba, bb, ALU.min))
                link(V.scalar_tensor_tensor(ba, af, 48.0, ba, ALU.add, ALU.min))
                link(V.tensor_tensor(bf, bf, ba, ALU.subtract))
                dve.wait_ge(ex_a, p + 1)
                link(V.tensor_reduce(gsf, bsf, AX.X, ALU.add))
                link(V.reciprocal(gsf, gsf))
                link(V.tensor_tensor(bsf, bsf, spread, ALU.mult))
                for b in range(2):
                    if b:
                        dve.wait_ge(jon2, 2 * p + b)
                    link(V.tensor_copy(sif.rearrange("p m k -> p (m k)"), siu[:, b, :, :].rearrange("p m k -> p (m k)")))
                    i16 = iota[:, 0:TOPK].unsqueeze(1).unsqueeze(1).broadcast_to([P, PH, TOPK, TOPK])
                    af_b, bf_b = (x.rearrange("p (b h k) -> p b h k", b=2, h=PH)[:, b] for x in (af, bf))
                    V.tensor_tensor(eqb, bf_b.unsqueeze(3).broadcast_to([P, PH, TOPK, TOPK]), i16, ALU.is_equal).then_inc(jon, 1)
                    link(V.tensor_tensor(eqa, af_b.unsqueeze(3).broadcast_to([P, PH, TOPK, TOPK]), i16, ALU.is_equal))
                    sih = sif.rearrange("p (h c) k -> p h c k", c=2)
                    link(V.tensor_tensor(eqa, eqa, sih[:, :, 0, :].unsqueeze(2).broadcast_to([P, PH, TOPK, TOPK]), ALU.mult))
                    if b:
                        dve.wait_ge(ch_t, 2 * p + b)
                    did(V.tensor_reduce(ijt[:, 0, :].rearrange("p (h k) -> p h k", h=PH), eqa, AX.X, ALU.add))
                    did(V.tensor_copy(ijt[:, 2, :].rearrange("p (h k) -> p h k", h=PH), bs[:, b]))
                    dve.wait_ge(jon2, 2 * p + b + 1)
                    V.tensor_reduce(ijt[:, 1, :].rearrange("p (h k) -> p h k", h=PH), eqb, AX.X, ALU.add).then_inc(jch, 1)
                if p < 2:
                    mod_columns(1, p * CHUNKS // 2, CHUNKS // 2, banks[0], p + 2)
                dve.wait_ge(ch_sb, 2 * p + 2)
                with dve.Fori(0, PT_ // 16) as n:
                    for q in range(2):
                        N = n + p * (PT_ // 16)
                        dve.wait_ge(g_pe[q], 1 + 2 * N)
                        number = lambda c, m: ijw[:, c, bass.ds(16 * n + 8 * q, m)].unsqueeze(2).broadcast_to([P, m, NK])
                        key = lambda m: iota.unsqueeze(1).broadcast_to([P, m, NK])
                        V.tensor_tensor(onehots(v_raw, q)[:, 0:ACT_T, :], number(1, ACT_T), key(ACT_T), ALU.is_equal).then_inc(coleq[q], 1)
                        for t in range(ACT_T, 8):
                            j_t, w_t = (ijw[:, c, bass.ds(16 * n + (8 * q + t), 1)] for c in (1, 2))
                            V.tensor_scalar(onehots(v_raw, q)[:, t, :], iota, j_t, w_t, ALU.is_equal, ALU.mult)
                        V.tensor_tensor(onehots(u_raw, q), number(0, 8), key(8), ALU.is_equal).then_inc(onehot[q], 1)

                def low_u(q, N):
                    dve.wait_ge(u_h[q], N + 1)
                    V.tensor_tensor(u_lo[:, q, :], u_raw[:, q, :], u_hi[:, q, :], ALU.subtract).then_inc(u_l[q], 1)

                def step(j, q, N, nq, nN, more=True):
                    if more:
                        low_u(nq, nN)
                    dve.wait_ge(s_act[q], N + 1)
                    dve.wait_ge(p_l[q], 1 + N)
                    V.tensor_tensor(prod[:, q, :], act_s[:, q, :], gate[:, :, j] if isinstance(j, int) else gate[:, :, bass.ds(j, 1)].rearrange("p t o -> p (t o)"), ALU.mult).then_inc(p_do[q], 1)
                    dve.wait_ge(v_h[q], N + 1)
                    V.tensor_tensor(v_lo[:, q, :], v_raw[:, q, :], v_hi[:, q, :], ALU.subtract).then_inc(v_l[q], 1)
                    dve.wait_ge(p_h[q], N + 1)
                    V.tensor_tensor(p_lo[:, q, :], prod[:, q, :], p_hi[:, q, :], ALU.subtract).then_inc(p_l[q], 1)

                N0 = p * PAIRS
                for q in range(2):
                    dve.wait_ge(g_sb[q], 1 + 2 * (PT_ // 16) * (p + 1))
                low_u(0, N0)
                step(0, 0, N0, 1, N0)
                with dve.Fori(0, PAIRS - 1) as n:
                    step(2 * n + 1, 1, n + N0, 0, n + N0 + 1)
                    step(2 * n + 2, 0, n + N0 + 1, 1, n + N0 + 1)
                step(NK - 1, 1, N0 + PAIRS - 1, 0, 0, more=False)
                dve.wait_ge(y_ac[1], 1 + PAIRS * (p + 1))
                norms([1, 2, 4][p], LN_BASE[p], [2 * s, 2 * s + 1], 2, lambda b: s)

            peer(0)
            peer(1)
            dve.wait_ge(x_out, 16 * 8)
            dve.wait_ge(swa_c, 16)
            for i in range(10):
                if i < 8:
                    dst, lo = q1[:, i, :], 0
                else:
                    dst, lo = k1[:, i - 8, CTX:TOK], CTX
                raw = rawq[:, i % 2, lo:lo + SEQ]
                dve.wait_ge(qk_sb, i + 1)
                did(V.tensor_tensor(dst, raw, cos, ALU.mult))
                if i >= 8:
                    did(V.tensor_copy(k1[:, i - 8, 0:CTX], rawq[:, i % 2, 0:CTX]))
                dve.wait_ge(rot_pe, i + 1)
                link(V.tensor_tensor(rtmp[:, i % 2, 0:SEQ], banks[2 + i % 2][:, 0:SEQ], sin, ALU.mult))
                V.tensor_tensor(dst, dst, rtmp[:, i % 2, 0:SEQ], ALU.add).then_inc(rope, 1)

            def out_copy(i):
                j, half, b = i // 4, i % 2, (i // 2) % 2
                rows = slice(half * SWA_D, (half + 1) * SWA_D)
                dve.wait_ge(at_o, i + 1)
                V.tensor_copy(o1[rows, j, b * P:(b + 1) * P], banks[4 + i % 2][rows, 0:P]).then_inc(at_oc, 1)

            def maxima(i):
                j, half = i // 4, i % 2
                hq = (2 * (j // 4) + half) * 4 + j % 4
                st = stat[:, (i % 4) * 20:(i % 4) * 20 + 20]
                dve.wait_ge(at_s, i + 1)
                did(V.tensor_copy(st[:, 5:6], sink[:, hq:hq + 1]))
                link(V.reduce_max(st[:, 0:1], banks[i % 2][:, :], AX.X))
                link(V.tensor_scalar(st[:, 1:2], st[:, 0:1], SWA_SCALE, sink[:, hq:hq + 1], ALU.mult, ALU.max))
                V.tensor_scalar(st[:, 2:3], st[:, 1:2], -1.0, None, ALU.mult).then_inc(at_m, 1)

            def diagonals(i):
                st = stat[:, (i % 4) * 20:(i % 4) * 20 + 20]
                dve.wait_ge(at_e, i + 1)
                link(V.tensor_tensor(st[:, 6:7], st[:, 3:4], st[:, 4:5], ALU.add))
                link(V.reciprocal(st[:, 7:8], st[:, 6:7]))
                if i >= 2:
                    dve.wait_ge(at_t, i - 1)
                V.tensor_scalar(diag[:, i % 2, :], ident, st[:, 7:8], None, ALU.mult).then_inc(at_d, 1)

            maxima(0)
            maxima(1)
            diagonals(0)
            for i in range(32):
                if i < 31:
                    diagonals(i + 1)
                if i < 30:
                    maxima(i + 2)
                if i:
                    out_copy(i - 1)
            out_copy(31)
            norms(3, 8, [2, 3], 0, lambda b: 1, [8 + y for y in Y_BLOCK[1]])
            peer(2)

        @block.gpsimd
        def _(pool):
            G = nc.gpsimd

            def norms(base, blocks):
                for i in range(len(blocks)):
                    st = stat[:, (i % 4) * 20:(i % 4) * 20 + 20]
                    pool.wait_ge(ln_v, base + i + 1)
                    G.tensor_tensor(st[:, 14:15], st[:, 13:14], neg_half, ALU.pow).then_inc(ln_p, 1)

            pool.wait_ge(setup_v, 1)
            pool.wait_ge(ms_a, 1 + HEADS)
            ms = stat[:, 0:HEADS * NB]
            G.tensor_tensor(ms, ms, neg_half.broadcast_to([P, HEADS * NB]), ALU.pow).then_inc(rms_p, 1)
            norms(0, range(4))

            def peer(p):
                s = PASS_S[p]
                for i in range(4):
                    w = wt(RING[(["wqa", "wqb", "wqc"][p], i)] % 2)
                    for m in range(4):
                        pool.wait_ge(qw_h[m], 4 * p + i + 1)
                        hi, lo = weight_parts(m)
                        G.tensor_tensor(lo, w[:, :, m * P:(m + 1) * P], hi, ALU.subtract).then_inc(qw_l[m], 1)
                if p < 2:
                    for i in range(MOD_PART):
                        row = mod1[:, i * WCOLS:(i + 1) * WCOLS]
                        if i == 0:
                            pool.wait_ge(mod1_b, 32 * (p + 1))
                        pool.wait_ge(mod1_a, MOD_PART * p + i + 1)
                        G.tensor_tensor(row, mod1_t[i % 2], row, ALU.add).then_inc(mod1_v, 1)
                for b in range(2):
                    pool.wait_ge(jon, 2 * p + b + 1)
                    sih = sif.rearrange("p (h c) k -> p h c k", c=2)
                    G.tensor_tensor(eqb, eqb, sih[:, :, 1, :].unsqueeze(2).broadcast_to([P, PH, TOPK, TOPK]), ALU.mult).then_inc(jon2, 1)
                norms(LN_BASE[p], [2 * s, 2 * s + 1])

            peer(0)
            peer(1)
            norms(8, [2, 3])
            peer(2)


def constants():
    c = np.zeros((P, C_ALL), np.float32)
    c[:, C_ID:C_ID + P] = np.eye(P)
    c[:, C_IOTA:C_IOTA + P] = np.arange(P)
    c[:, C_ONE:C_ONE + P] = 1.0 / P
    rot = np.zeros((P, P), np.float32)
    for h in range(2):
        for ax in range(2):
            for f in range(16):
                x1 = h * 64 + ax * 32 + f
                rot[x1, x1 + 16] = -1.0
                rot[x1 + 16, x1] = 1.0
    c[:, C_ROT:C_ROT + P] = rot.T
    t = np.arange(SEQ)
    pos = np.stack([t // 64, t % 64]).astype(np.float32)
    inv = (np.float32(10000.0) ** (-np.arange(0, 32, 2, dtype=np.float32) / np.float32(32))).astype(np.float32)
    ang = pos[:, :, None] * inv
    for p in range(P):
        ax, f = (p % 64) // 32, p % 16
        c[p, C_COS:C_COS + SEQ] = np.cos(ang[ax, :, f])
        c[p, C_SIN:C_SIN + SEQ] = np.sin(ang[ax, :, f])
    q, k = np.arange(P)[:, None], np.arange(P)[None, :]
    c[:, C_MASK:C_MASK + P] = np.where(k <= q, 0.0, SCORE_MASK)
    c[:, C_MASK + P:C_MASK + 2 * P] = np.where(q <= k, 0.0, SCORE_MASK)
    m = np.zeros((P, LEVELS, P), np.float32)
    for l in range(1, LEVELS):
        h = 1 << (l - 1)
        m[:, l, :] = (q // (2 * h) == k // (2 * h)) & (q // h != k // h)
    return c, m.reshape(P, LEVELS * P)


def kernel(**inputs):
    import concourse.bacc as bacc
    from concourse.bass_utils import run_bass_kernel_spmd as run

    x = {k: np.ascontiguousarray(np.asarray(v)) for k, v in inputs.items()}

    def tiles(w, cols):
        n = w.shape[1] // cols
        return w.reshape(KT, P, n, cols).transpose(2, 1, 0, 3).reshape(n, P, KT * cols)

    qh = [(2 * (j // 4) + half) * 4 + j % 4 for j in range(8) for half in range(2)]
    qcols = np.concatenate([np.arange(64) + 64 * h for h in qh])
    swa = x["swa_w_in"][0]
    qkv = np.concatenate([swa[:, qcols], swa[:, 1024:]], axis=1)
    wst = np.concatenate(
        [tiles(x["mod_w"][l], WCOLS) for l in range(DEPTH)]
        + [tiles(x["hgrn_w_out"][0], WCOLS), tiles(x["peer_wq"][0], WCOLS), tiles(qkv, WCOLS),
           tiles(x["swa_w_out"][0][qcols], WCOLS), tiles(x["peer_wq"][1], WCOLS)])
    w5 = x["hgrn_w_in"][0].reshape(D, 5, HEADS, P)
    whd = tiles(w5[:, [0, 2, 3, 4, 1]].transpose(0, 2, 1, 3).reshape(D, HEADS * HCOLS), HCOLS)
    u = x["peer_u"].reshape(DEPTH, P, NK, KT, P).transpose(0, 2, 4, 3, 1).reshape(DEPTH, NK, P, D)
    v = x["peer_v"].reshape(DEPTH, P, NK, D).transpose(0, 2, 1, 3)
    keys = x["peer_keys"].transpose(0, 4, 1, 2, 3).reshape(DEPTH, P, 16 * NK)
    const, lvlmask = constants()
    arrays = {"x": x["x"], "ctx": x["ctx"], "c": x["c"], "c_ctx": x["c_ctx"], "mod_b": x["mod_b"], "ln_g": x["ln_g"],
              "ln_b": x["ln_b"], "lb": x["hgrn_lb_logits"], "ng": x["hgrn_norm_g"], "sink": x["swa_sink"][0],
              "wst": wst, "whd": whd, "u": u, "v": v, "keys": keys, "const": const, "lvlmask": lvlmask}
    arrays = {"in_" + k: np.ascontiguousarray(v) for k, v in arrays.items()}
    nc = bacc.Bacc("TRN2", target_bir_lowering=False, num_devices=1)
    args = {k[3:]: nc.dram_tensor(k, v.shape, mybir.dt.from_np(v.dtype), kind="ExternalInput").ap() for k, v in arrays.items()}
    args["out"] = nc.dram_tensor("out", (1, SEQ, D), F32, kind="ExternalOutput").ap()
    build(nc, args)
    r = run(nc, [arrays], core_ids=[0])
    return r.results[0]["out"]
```
